# Optimizing a Trainium2 kernel written in Bass

```python
import math
import jax, jax.numpy as jnp
from jax import lax
import numpy as np
import jax
import jax.numpy as jnp

D_MODEL = 1024
BATCH = 1
SEQ = 256
DEPTH = 2

CHUNK = 64
Q_BLOCK = 128
HEAD_DIM = 64
FOX_HEADS = 8
FOX_DIM = FOX_HEADS * HEAD_DIM
GLA_HEADS = 4
GLA_DK = 64
GLA_DV = 128
GLA_QK = GLA_HEADS * GLA_DK
GLA_V = GLA_HEADS * GLA_DV
GLA_RANK = 16
GLA_TAU = 16.0
MIX_WIDTH = FOX_DIM + GLA_V
IN_COLS = 3 * FOX_DIM + FOX_HEADS + 2 * GLA_QK + 2 * GLA_V + GLA_RANK
S5_GROUP = 16
S5_GROUPS = D_MODEL // S5_GROUP
S5_STATE = 64
D_FF = 2816
N_EXPERTS = 8
TOP_K = 2
EXPERT_FF = 2816
N_EVEN = (DEPTH + 1) // 2
N_ODD = DEPTH // 2
EPS = 1e-6


def rmsnorm(x, w):
    xf = x.astype(jnp.float32)
    y = xf * lax.rsqrt(jnp.mean(xf * xf, axis=-1, keepdims=True) + EPS)
    return y * w.astype(jnp.float32)

def adaln(c, w, b):
    m = jax.nn.silu(c.astype(jnp.float32)) @ w + b
    shift, scale, gate = jnp.split(m, 3, axis=-1)
    return shift[:, None, :], scale[:, None, :], gate[:, None, :]

def fox_attention(q, k, v, logf):
    B, H, S, dh = q.shape
    cum = jnp.cumsum(logf, axis=-1)
    nb = S // Q_BLOCK
    qb = q.reshape(B, H, nb, Q_BLOCK, dh).transpose(2, 0, 1, 3, 4)
    cb = cum.reshape(B, H, nb, Q_BLOCK).transpose(2, 0, 1, 3)
    kpos = jnp.arange(S)
    scale = dh ** -0.5

    def block(args):
        i, qi, ci = args
        s = jnp.einsum('bhqd,bhkd->bhqk', qi, k) * scale + ci[..., None] - cum[:, :, None, :]
        qpos = i * Q_BLOCK + jnp.arange(Q_BLOCK)
        s = jnp.where(kpos[None, :] <= qpos[:, None], s, -jnp.inf)
        p = jax.nn.softmax(s, axis=-1)
        return jnp.einsum('bhqk,bhkd->bhqd', p, v)

    out = lax.map(block, (jnp.arange(nb), qb, cb))
    return out.transpose(1, 2, 0, 3, 4).reshape(B, H, S, dh)

def gla_attention(q, k, v, log_a):
    B, H, S, dk = q.shape
    dv = v.shape[-1]
    nc = S // CHUNK

    def to_chunks(t):
        return t.reshape(B, H, nc, CHUNK, t.shape[-1]).transpose(2, 0, 1, 3, 4)

    qc, kc, vc, ac = (to_chunks(q * dk ** -0.5), to_chunks(k), to_chunks(v), to_chunks(log_a))
    bc = jnp.cumsum(ac, axis=3)
    causal = jnp.tril(jnp.ones((CHUNK, CHUNK), dtype=bool))

    def step(state, inp):
        qi, ki, vi, bi = inp
        diff = bi[:, :, :, None, :] - bi[:, :, None, :, :]
        decay = jnp.exp(jnp.where(causal[None, None, :, :, None], diff, -jnp.inf))
        attn = jnp.einsum('bhtd,bhsd,bhtsd->bhts', qi, ki, decay)
        o = (jnp.einsum('bhts,bhsv->bhtv', attn, vi)
             + jnp.einsum('bhtd,bhdv->bhtv', qi * jnp.exp(bi), state))
        blast = bi[:, :, -1:, :]
        state = (jnp.exp(blast[:, :, 0, :])[..., None] * state
                 + jnp.einsum('bhsd,bhsv->bhdv', ki * jnp.exp(blast - bi), vi))
        return state, o

    s0 = jnp.zeros((B, H, dk, dv), jnp.float32)
    _, o = lax.scan(step, s0, (qc, kc, vc, bc))
    return o.transpose(1, 2, 0, 3, 4).reshape(B, H, S, dv)

def even_mixer(h, w_in, fox_fb, gla_w2, gla_b2, gla_norm, w_o):
    B, S, _ = h.shape
    sizes = (FOX_DIM, FOX_DIM, FOX_DIM, FOX_HEADS, GLA_QK, GLA_QK, GLA_V, GLA_V, GLA_RANK)
    cuts = [sum(sizes[:i + 1]) for i in range(len(sizes) - 1)]
    fq, fk, fv, ff, gq, gk, gv, gg, glr = jnp.split(h @ w_in, cuts, axis=-1)

    def heads(t, n):
        return t.reshape(B, S, n, -1).transpose(0, 2, 1, 3)

    logf = jax.nn.log_sigmoid(ff + fox_fb).transpose(0, 2, 1)
    fox = fox_attention(heads(fq, FOX_HEADS), heads(fk, FOX_HEADS), heads(fv, FOX_HEADS), logf)
    fox = fox.transpose(0, 2, 1, 3).reshape(B, S, FOX_DIM)
    log_a = jax.nn.log_sigmoid(glr @ gla_w2 + gla_b2) / GLA_TAU
    gla = gla_attention(heads(gq, GLA_HEADS), heads(gk, GLA_HEADS), heads(gv, GLA_HEADS),
                        heads(log_a, GLA_HEADS))
    gla = rmsnorm(gla.transpose(0, 2, 1, 3), gla_norm).reshape(B, S, GLA_V) * jax.nn.silu(gg)
    return jnp.concatenate([fox, gla], axis=-1) @ w_o

def s5_mixer(h, w_in, lam_re, lam_im, log_dt, b_re, b_im, c_re, c_im, d_skip, w_glu, w_o):
    B, S, _ = h.shape
    f32 = jnp.float32
    lam_re, lam_im, log_dt = lam_re.astype(f32), lam_im.astype(f32), log_dt.astype(f32)
    b_re, b_im, c_re, c_im = b_re.astype(f32), b_im.astype(f32), c_re.astype(f32), c_im.astype(f32)
    u = h @ w_in
    ug = u.reshape(B, S, S5_GROUPS, S5_GROUP)
    dt = jnp.exp(log_dt)[:, None]
    mag = jnp.exp(lam_re * dt)
    a_re = mag * jnp.cos(lam_im * dt)
    a_im = mag * jnp.sin(lam_im * dt)
    den = lam_re * lam_re + lam_im * lam_im
    nr, ni = a_re - 1.0, a_im
    f_re = (nr * lam_re + ni * lam_im) / den
    f_im = (ni * lam_re - nr * lam_im) / den
    bb_re = f_re[..., None] * b_re - f_im[..., None] * b_im
    bb_im = f_re[..., None] * b_im + f_im[..., None] * b_re
    ut = ug.transpose(1, 0, 2, 3)
    bu_re = jnp.einsum('sbgk,gpk->sbgp', ut, bb_re)
    bu_im = jnp.einsum('sbgk,gpk->sbgp', ut, bb_im)
    ar_t = jnp.broadcast_to(a_re[None, None], (S, 1, S5_GROUPS, S5_STATE))
    ai_t = jnp.broadcast_to(a_im[None, None], (S, 1, S5_GROUPS, S5_STATE))

    def combine(e1, e2):
        a1r, a1i, b1r, b1i = e1
        a2r, a2i, b2r, b2i = e2
        return (a1r * a2r - a1i * a2i,
                a1r * a2i + a1i * a2r,
                a2r * b1r - a2i * b1i + b2r,
                a2r * b1i + a2i * b1r + b2i)

    _, _, xr, xi = lax.associative_scan(combine, (ar_t, ai_t, bu_re, bu_im), axis=0)
    y = jnp.einsum('sbgp,gkp->bsgk', xr, c_re) - jnp.einsum('sbgp,gkp->bsgk', xi, c_im)
    y = y.reshape(B, S, D_MODEL) + d_skip * u
    y = jax.nn.gelu(y)
    y = y * jax.nn.sigmoid(y @ w_glu)
    return y @ w_o

def swiglu(h, w_gate, w_up, w_down):
    return (jax.nn.silu(h @ w_gate) * (h @ w_up)) @ w_down

def moe_swiglu(h, w_router, w_gate, w_up, w_down):
    logits = (h @ w_router).astype(jnp.float32)
    top_val, top_idx = lax.top_k(logits, TOP_K)
    weights = jax.nn.softmax(top_val, axis=-1)
    gates = jnp.sum(jax.nn.one_hot(top_idx, N_EXPERTS, dtype=jnp.float32) * weights[..., None], axis=-2)
    out = jnp.zeros_like(h)
    for e in range(N_EXPERTS):
        out = out + gates[..., e:e + 1] * swiglu(h, w_gate[e], w_up[e], w_down[e])
    return out

def first_inputs(seed: int = 0) -> dict:
    key = jax.random.key(seed)
    ks = iter(jax.random.split(key, 64))
    f32 = jnp.float32

    def nrm(shape, scale):
        return jax.random.normal(next(ks), shape, f32) * scale

    def gain(shape):
        return 1.0 + 0.05 * jax.random.normal(next(ks), shape, f32)

    D = D_MODEL
    NE, NO = N_EVEN, N_ODD
    G, P, K = S5_GROUPS, S5_STATE, S5_GROUP
    mod_s = 0.5 * D ** -0.5
    inp = {}
    inp['x'] = nrm((BATCH, SEQ, D), 1.0)
    inp['c'] = nrm((BATCH, D), 1.0)
    inp['e_norm_mix'] = gain((NE, D))
    inp['e_mod_mix_w'] = nrm((NE, D, 3 * D), mod_s)
    inp['e_mod_mix_b'] = nrm((NE, 3 * D), 0.02)
    inp['e_w_in'] = nrm((NE, D, IN_COLS), D ** -0.5)
    inp['e_fox_fb'] = 2.0 + nrm((NE, FOX_HEADS), 0.5)
    inp['e_gla_w2'] = nrm((NE, GLA_RANK, GLA_QK), GLA_RANK ** -0.5)
    inp['e_gla_b2'] = nrm((NE, GLA_QK), 0.02)
    inp['e_gla_norm'] = gain((NE, GLA_DV))
    inp['e_w_o'] = nrm((NE, MIX_WIDTH, D), MIX_WIDTH ** -0.5)
    inp['e_norm_ffn'] = gain((NE, D))
    inp['e_mod_ffn_w'] = nrm((NE, D, 3 * D), mod_s)
    inp['e_mod_ffn_b'] = nrm((NE, 3 * D), 0.02)
    inp['e_ffn_gate'] = nrm((NE, D, D_FF), D ** -0.5)
    inp['e_ffn_up'] = nrm((NE, D, D_FF), D ** -0.5)
    inp['e_ffn_down'] = nrm((NE, D_FF, D), D_FF ** -0.5)
    inp['o_norm_mix'] = gain((NO, D))
    inp['o_mod_mix_w'] = nrm((NO, D, 3 * D), mod_s)
    inp['o_mod_mix_b'] = nrm((NO, 3 * D), 0.02)
    inp['o_w_in'] = nrm((NO, D, D), D ** -0.5)
    inp['o_lam_re'] = -0.5 + nrm((NO, G, P), 0.01)
    inp['o_lam_im'] = math.pi * jnp.arange(P, dtype=f32)[None, None, :] + nrm((NO, G, P), 0.01)
    inp['o_log_dt'] = jax.random.uniform(next(ks), (NO, G), f32, math.log(1e-3), math.log(1e-1))
    inp['o_b_re'] = nrm((NO, G, P, K), (2.0 * K) ** -0.5)
    inp['o_b_im'] = nrm((NO, G, P, K), (2.0 * K) ** -0.5)
    inp['o_c_re'] = nrm((NO, G, K, P), (2.0 / P) ** 0.5)
    inp['o_c_im'] = nrm((NO, G, K, P), (2.0 / P) ** 0.5)
    inp['o_d_skip'] = nrm((NO, D), 1.0)
    inp['o_w_glu'] = nrm((NO, D, D), D ** -0.5)
    inp['o_w_o'] = nrm((NO, D, D), D ** -0.5)
    inp['o_norm_ffn'] = gain((NO, D))
    inp['o_mod_ffn_w'] = nrm((NO, D, 3 * D), mod_s)
    inp['o_mod_ffn_b'] = nrm((NO, 3 * D), 0.02)
    inp['o_router'] = nrm((NO, D, N_EXPERTS), D ** -0.5)
    inp['o_exp_gate'] = nrm((NO, N_EXPERTS, D, EXPERT_FF), D ** -0.5)
    inp['o_exp_up'] = nrm((NO, N_EXPERTS, D, EXPERT_FF), D ** -0.5)
    inp['o_exp_down'] = nrm((NO, N_EXPERTS, EXPERT_FF, D), EXPERT_FF ** -0.5)
    inp['final_norm'] = gain((D,))
    return inp

def first_block(x, c,
              e_norm_mix, e_mod_mix_w, e_mod_mix_b, e_w_in, e_fox_fb, e_gla_w2, e_gla_b2,
              e_gla_norm, e_w_o, e_norm_ffn, e_mod_ffn_w, e_mod_ffn_b, e_ffn_gate, e_ffn_up,
              e_ffn_down,
              o_norm_mix, o_mod_mix_w, o_mod_mix_b, o_w_in, o_lam_re, o_lam_im, o_log_dt,
              o_b_re, o_b_im, o_c_re, o_c_im, o_d_skip, o_w_glu, o_w_o, o_norm_ffn,
              o_mod_ffn_w, o_mod_ffn_b, o_router, o_exp_gate, o_exp_up, o_exp_down,
              final_norm):
    for i in range(DEPTH):
        j = i // 2
        if i % 2 == 0:
            sh, sc, g = adaln(c, e_mod_mix_w[j], e_mod_mix_b[j])
            h = rmsnorm(x, e_norm_mix[j]) * (1.0 + sc) + sh
            y = even_mixer(h, e_w_in[j], e_fox_fb[j], e_gla_w2[j], e_gla_b2[j], e_gla_norm[j], e_w_o[j])
            x = x + (g * y).astype(x.dtype)
            sh, sc, g = adaln(c, e_mod_ffn_w[j], e_mod_ffn_b[j])
            h = rmsnorm(x, e_norm_ffn[j]) * (1.0 + sc) + sh
            y = swiglu(h, e_ffn_gate[j], e_ffn_up[j], e_ffn_down[j])
            x = x + (g * y).astype(x.dtype)
        else:
            sh, sc, g = adaln(c, o_mod_mix_w[j], o_mod_mix_b[j])
            h = rmsnorm(x, o_norm_mix[j]) * (1.0 + sc) + sh
            y = s5_mixer(h, o_w_in[j], o_lam_re[j], o_lam_im[j], o_log_dt[j], o_b_re[j], o_b_im[j],
                         o_c_re[j], o_c_im[j], o_d_skip[j], o_w_glu[j], o_w_o[j])
            x = x + (g * y).astype(x.dtype)
            sh, sc, g = adaln(c, o_mod_ffn_w[j], o_mod_ffn_b[j])
            h = rmsnorm(x, o_norm_ffn[j]) * (1.0 + sc) + sh
            y = moe_swiglu(h, o_router[j], o_exp_gate[j], o_exp_up[j], o_exp_down[j])
            x = x + (g * y).astype(x.dtype)
    return rmsnorm(x, final_norm).astype(x.dtype)


DEPTH_2 = 1

CTX_LEN = 256
GRID_W = 64
N_MOD = 6
DA_HEADS = 8
DA_QK = 64
DA_V = 2 * DA_QK
DA_QK_COLS = DA_HEADS * 2 * DA_QK
DA_WIDTH = DA_HEADS * DA_V
ROPE_THETA = 10000.0
ROPE_FREQS = DA_QK // 4
RW_HEADS = 16
RW_HEAD = 64
RW_WIDTH = RW_HEADS * RW_HEAD
RW_W_LORA = 64
RW_A_LORA = 64
RW_G_LORA = 128
RW_SHIFT_CH = 3 * RW_WIDTH + RW_W_LORA + RW_A_LORA + RW_G_LORA
RW_LN_EPS = 64e-5
L2_EPS = 1e-12
RW_SPLIT_IDX = (RW_WIDTH, 2 * RW_WIDTH, 3 * RW_WIDTH, 3 * RW_WIDTH + RW_W_LORA, 3 * RW_WIDTH + RW_W_LORA + RW_A_LORA)
N_BRANCH = 2
IN_SPLIT_IDX = (DA_QK_COLS, 2 * DA_QK_COLS, 2 * DA_QK_COLS + DA_WIDTH, 2 * DA_QK_COLS + DA_WIDTH + RW_SHIFT_CH)
IN_WIDTH = 2 * DA_QK_COLS + DA_WIDTH + RW_SHIFT_CH + N_BRANCH * D_MODEL
PEER_HEADS = 8
N_KEYS = 128
N_EXPERTS_2 = N_KEYS * N_KEYS
PEER_TOPK = 16
PEER_QDIM = 256
PEER_CHUNK = 128


def rmsnorm_2(x, g):
    xf = x.astype(jnp.float32)
    y = xf * lax.rsqrt(jnp.mean(xf * xf, axis=-1, keepdims=True) + EPS)
    return (y * g.astype(jnp.float32)).astype(x.dtype)

def modulate(h, shift, scale):
    return h * (1 + scale) + shift

def axial_angles(n_tokens):
    rows = n_tokens // GRID_W
    row = jnp.repeat(jnp.arange(rows, dtype=jnp.float32), GRID_W)
    col = jnp.tile(jnp.arange(GRID_W, dtype=jnp.float32), rows)
    inv = ROPE_THETA ** (-jnp.arange(ROPE_FREQS, dtype=jnp.float32) / ROPE_FREQS)
    return jnp.stack([row[:, None] * inv, col[:, None] * inv], axis=1)

def apply_axial_rope(x, ang):
    xs = x.reshape(x.shape[:-1] + (2, 2, ROPE_FREQS))
    cos = jnp.cos(ang)[:, None, None, :, None, :].astype(x.dtype)
    sin = jnp.sin(ang)[:, None, None, :, None, :].astype(x.dtype)
    x1, x2 = xs[..., 0:1, :], xs[..., 1:2, :]
    out = jnp.concatenate([x1 * cos - x2 * sin, x2 * cos + x1 * sin], axis=-2)
    return out.reshape(x.shape)

def diff_heads(q, k, v, q_g, k_g, ang):
    B, T, _ = q.shape
    q = rmsnorm_2(q.reshape(B, T, DA_HEADS, 2, DA_QK), q_g)
    k = rmsnorm_2(k.reshape(B, T, DA_HEADS, 2, DA_QK), k_g)
    if ang is not None:
        q = apply_axial_rope(q, ang)
        k = apply_axial_rope(k, ang)
    q = q.transpose(0, 3, 2, 1, 4)
    k = k.transpose(0, 3, 2, 1, 4)
    v = v.reshape(B, T, DA_HEADS, DA_V).transpose(0, 2, 1, 3)
    return q, k, v

def diff_attention(q, k, v, lam):
    B, _, H, T, d = q.shape
    nb = T // Q_BLOCK
    qb = q.reshape(B, 2, H, nb, Q_BLOCK, d).transpose(3, 0, 1, 2, 4, 5)
    scale = d ** -0.5

    def one_block(q_blk):
        s = jnp.einsum('bmhqd,bmhkd->bmhqk', q_blk, k).astype(jnp.float32) * scale
        p = jax.nn.softmax(s, axis=-1)
        pd = (p[:, 0] - lam * p[:, 1]).astype(v.dtype)
        return jnp.einsum('bhqk,bhkd->bhqd', pd, v)

    o = lax.map(one_block, qb)
    return o.transpose(1, 0, 3, 2, 4).reshape(B, T, H * v.shape[-1])

def diff_post(o, out_g, lam_init):
    B, T, _ = o.shape
    o = rmsnorm_2(o.reshape(B, T, DA_HEADS, DA_V), out_g) * (1 - lam_init)
    return o.reshape(B, T, DA_WIDTH)

def centred_shift(z, w):
    zp = jnp.pad(z, ((0, 0), (1, 1), (0, 0)))
    return w[0] * zp[:, :-2] + w[1] * zp[:, 1:-1] + w[2] * zp[:, 2:]

def head_l2norm(t):
    th = t.reshape(t.shape[:-1] + (RW_HEADS, RW_HEAD)).astype(jnp.float32)
    th = th * lax.rsqrt(jnp.sum(th * th, axis=-1, keepdims=True) + L2_EPS)
    return th.reshape(t.shape).astype(t.dtype)

def dual(t):
    return jnp.stack([t, t])

def to_scan(t):
    t = jnp.stack([t[0], t[1][:, ::-1]]).astype(jnp.float32)
    return t.reshape(t.shape[:3] + (RW_HEADS, RW_HEAD)).transpose(2, 0, 1, 3, 4)

def from_scan(y):
    y = y.transpose(1, 2, 0, 3, 4)
    return y[0] + y[1][:, ::-1]

def rwkv_prepare(z, shift_w, w0, w_up, a0, a_up, k_k, k_a):
    z = centred_shift(z, shift_w)
    r, k, v, wd, ad, gd = jnp.split(z, RW_SPLIT_IDX, axis=-1)
    w_log = -jax.nn.softplus(-(w0[:, None, None, :] + jnp.einsum('btr,drc->dbtc', jnp.tanh(wd), w_up))) - 0.5
    decay = jnp.exp(-jnp.exp(w_log.astype(jnp.float32)))
    a = jax.nn.sigmoid(a0[:, None, None, :] + jnp.einsum('btr,drc->dbtc', ad, a_up))
    kk = head_l2norm(k * k_k)
    k_eff = k[None] * (1 + (a - 1) * k_a)
    scan_in = (to_scan(decay), to_scan(dual(kk)), to_scan(a), to_scan(k_eff), to_scan(dual(v)), to_scan(dual(r)))
    return scan_in, (r, k, v, gd)

def wkv_scan(s0, scan_in):
    def step(s, inp):
        w, kk, a, k, v, r = inp
        sa = jnp.einsum('dbhij,dbhj->dbhi', s, kk)
        s = s * w[..., None, :] - sa[..., :, None] * (kk * a)[..., None, :] + v[..., :, None] * k[..., None, :]
        return s, jnp.einsum('dbhij,dbhj->dbhi', s, r)
    return lax.scan(step, s0, scan_in)

def rwkv_post(y, r, k, v, gd, g_up, r_k, ln_g, ln_b):
    B, T, C = r.shape
    mu = jnp.mean(y, axis=-1, keepdims=True)
    var = jnp.mean(jnp.square(y - mu), axis=-1, keepdims=True)
    yn = ((y - mu) * lax.rsqrt(var + RW_LN_EPS)).reshape(B, T, C) * ln_g + ln_b
    hs = lambda t: t.reshape(B, T, RW_HEADS, RW_HEAD)
    bonus = jnp.sum(hs(r) * hs(k) * r_k, axis=-1, keepdims=True) * hs(v)
    g = jax.nn.sigmoid(gd) @ g_up
    return (yn.astype(r.dtype) + bonus.reshape(B, T, C)) * g

def merge_branches(o_a, o_b, z_gate, w_branch_a, w_branch_b, w_out):
    g_a, g_b = jnp.split(jax.nn.sigmoid(z_gate), N_BRANCH, axis=-1)
    return (g_a * (o_a @ w_branch_a) + g_b * (o_b @ w_branch_b)) @ w_out

def peer_ffn(h, peer_wq, peer_keys, peer_u, peer_v):
    B, T, D = h.shape
    tok = h.reshape(-1, PEER_CHUNK, D)

    def one_chunk(xc):
        q = (xc @ peer_wq).reshape(PEER_CHUNK, PEER_HEADS, 2, PEER_QDIM // 2)
        s = jnp.einsum('chpd,hpkd->chpk', q, peer_keys).astype(jnp.float32)
        sv, si = lax.top_k(s, PEER_TOPK)
        cand = (sv[..., 0, :, None] + sv[..., 1, None, :]).reshape(PEER_CHUNK, PEER_HEADS, PEER_TOPK * PEER_TOPK)
        cidx = (si[..., 0, :, None] * N_KEYS + si[..., 1, None, :]).reshape(PEER_CHUNK, PEER_HEADS, PEER_TOPK * PEER_TOPK)
        top_s, pos = lax.top_k(cand, PEER_TOPK)
        eidx = jnp.take_along_axis(cidx, pos, axis=-1)
        gate = jax.nn.softmax(top_s, axis=-1)
        act = jax.nn.gelu(jnp.einsum('chkd,cd->chk', peer_u[eidx], xc))
        return jnp.einsum('chk,chkd->cd', (gate * act).astype(xc.dtype), peer_v[eidx])

    return lax.map(one_chunk, tok).reshape(B, T, D)

def hybrid_layer(x, ctx, c, c_ctx, w_mod, b_mod, norm1_g, w_in, q_norm_g, k_norm_g, diff_lambda, diff_out_g,
                 rw_shift, rw_w0, rw_w_up, rw_a0, rw_a_up, rw_g_up, rw_k_k, rw_k_a, rw_r_k, rw_ln_g, rw_ln_b,
                 w_branch_a, w_branch_b, w_out, norm2_g, peer_wq, peer_keys, peer_u, peer_v, layer_idx, update_ctx):
    B, S, _ = x.shape
    lam_init = 0.8 - 0.6 * math.exp(-0.3 * layer_idx)
    mod_x = jnp.split((jax.nn.silu(c) @ w_mod + b_mod)[:, None, :], N_MOD, axis=-1)
    mod_c = jnp.split((jax.nn.silu(c_ctx) @ w_mod + b_mod)[None, None, :], N_MOD, axis=-1)
    zx = jnp.split(modulate(rmsnorm_2(x, norm1_g), mod_x[0], mod_x[1]) @ w_in, IN_SPLIT_IDX, axis=-1)
    zc = jnp.split(modulate(rmsnorm_2(ctx, norm1_g), mod_c[0], mod_c[1]) @ w_in, IN_SPLIT_IDX, axis=-1)

    qx, kx, vx = diff_heads(zx[0], zx[1], zx[2], q_norm_g, k_norm_g, axial_angles(S))
    qc, kc, vc = diff_heads(zc[0], zc[1], zc[2], q_norm_g, k_norm_g, None)
    lam = jnp.exp(jnp.sum(diff_lambda[0] * diff_lambda[1])) - jnp.exp(jnp.sum(diff_lambda[2] * diff_lambda[3])) + lam_init
    k_all = jnp.concatenate([kc, kx], axis=3)
    v_all = jnp.concatenate([vc, vx], axis=2)
    o_ax = diff_post(diff_attention(qx, k_all, v_all, lam), diff_out_g, lam_init)

    scan_c, aux_c = rwkv_prepare(zc[3], rw_shift, rw_w0, rw_w_up, rw_a0, rw_a_up, rw_k_k, rw_k_a)
    scan_x, aux_x = rwkv_prepare(zx[3], rw_shift, rw_w0, rw_w_up, rw_a0, rw_a_up, rw_k_k, rw_k_a)
    s0 = jnp.zeros((2, B, RW_HEADS, RW_HEAD, RW_HEAD), jnp.float32)
    s_ctx, y_c = wkv_scan(s0, scan_c)
    _, y_x = wkv_scan(s_ctx, scan_x)
    o_bx = rwkv_post(from_scan(y_x), *aux_x, rw_g_up, rw_r_k, rw_ln_g, rw_ln_b)

    x = x + mod_x[2] * merge_branches(o_ax, o_bx, zx[4], w_branch_a, w_branch_b, w_out)
    x = x + mod_x[5] * peer_ffn(modulate(rmsnorm_2(x, norm2_g), mod_x[3], mod_x[4]), peer_wq, peer_keys, peer_u, peer_v)

    if update_ctx:
        o_ac = diff_post(diff_attention(qc, kc, vc, lam), diff_out_g, lam_init)
        o_bc = rwkv_post(from_scan(y_c), *aux_c, rw_g_up, rw_r_k, rw_ln_g, rw_ln_b)
        ctx = ctx + mod_c[2] * merge_branches(o_ac, o_bc, zc[4], w_branch_a, w_branch_b, w_out)
        ctx = ctx + mod_c[5] * peer_ffn(modulate(rmsnorm_2(ctx, norm2_g), mod_c[3], mod_c[4]), peer_wq, peer_keys, peer_u, peer_v)
    return x, ctx

def second_inputs(seed: int = 0) -> dict:
    key = jax.random.key(seed)
    ks = iter(jax.random.split(key, 40))
    nrm = lambda shape, s: jax.random.normal(next(ks), shape, jnp.float32) * s
    L, D = DEPTH_2, D_MODEL
    return {
        'x': nrm((BATCH, SEQ, D), 1.0),
        'c': nrm((BATCH, D), 1.0),
        'ctx': nrm((BATCH, CTX_LEN, D), 1.0),
        'c_ctx': nrm((D,), 1.0),
        'w_mod': nrm((L, D, N_MOD * D), D ** -0.5),
        'b_mod': nrm((L, N_MOD * D), 0.01),
        'norm1_g': 1.0 + nrm((L, D), 0.02),
        'w_in': nrm((L, D, IN_WIDTH), D ** -0.5),
        'q_norm_g': 1.0 + nrm((L, DA_QK), 0.02),
        'k_norm_g': 1.0 + nrm((L, DA_QK), 0.02),
        'diff_lambda': nrm((L, 4, DA_QK), 0.1),
        'diff_out_g': 1.0 + nrm((L, DA_V), 0.02),
        'rw_shift': jnp.array([0.25, 0.5, 0.25], jnp.float32)[None, :, None] + nrm((L, 3, RW_SHIFT_CH), 0.1),
        'rw_w0': -6.0 + 5.0 * jax.random.uniform(next(ks), (L, 2, RW_WIDTH), jnp.float32),
        'rw_w_up': nrm((L, 2, RW_W_LORA, RW_WIDTH), 0.1 * RW_W_LORA ** -0.5),
        'rw_a0': nrm((L, 2, RW_WIDTH), 0.5),
        'rw_a_up': nrm((L, 2, RW_A_LORA, RW_WIDTH), 0.1 * RW_A_LORA ** -0.5),
        'rw_g_up': nrm((L, RW_G_LORA, RW_WIDTH), RW_G_LORA ** -0.5),
        'rw_k_k': 0.85 + nrm((L, RW_WIDTH), 0.1),
        'rw_k_a': 1.0 + nrm((L, RW_WIDTH), 0.05),
        'rw_r_k': nrm((L, RW_HEADS, RW_HEAD), 0.1),
        'rw_ln_g': 1.0 + nrm((L, RW_WIDTH), 0.02),
        'rw_ln_b': nrm((L, RW_WIDTH), 0.01),
        'w_branch_a': nrm((L, DA_WIDTH, D), DA_WIDTH ** -0.5),
        'w_branch_b': nrm((L, RW_WIDTH, D), RW_WIDTH ** -0.5),
        'w_out': nrm((L, D, D), D ** -0.5),
        'norm2_g': 1.0 + nrm((L, D), 0.02),
        'peer_wq': nrm((L, D, PEER_HEADS * PEER_QDIM), D ** -0.5),
        'peer_keys': nrm((L, PEER_HEADS, 2, N_KEYS, PEER_QDIM // 2), (PEER_QDIM // 2) ** -0.5),
        'peer_u': nrm((L, N_EXPERTS_2, D), D ** -0.5),
        'peer_v': nrm((L, N_EXPERTS_2, D), PEER_HEADS ** -0.5),
    }

def second_block(x, c, ctx, c_ctx, w_mod, b_mod, norm1_g, w_in, q_norm_g, k_norm_g, diff_lambda, diff_out_g,
              rw_shift, rw_w0, rw_w_up, rw_a0, rw_a_up, rw_g_up, rw_k_k, rw_k_a, rw_r_k, rw_ln_g, rw_ln_b,
              w_branch_a, w_branch_b, w_out, norm2_g, peer_wq, peer_keys, peer_u, peer_v):
    for l in range(DEPTH_2):
        x, ctx = hybrid_layer(
            x, ctx, c, c_ctx, w_mod[l], b_mod[l], norm1_g[l], w_in[l], q_norm_g[l], k_norm_g[l], diff_lambda[l],
            diff_out_g[l], rw_shift[l], rw_w0[l], rw_w_up[l], rw_a0[l], rw_a_up[l], rw_g_up[l], rw_k_k[l], rw_k_a[l],
            rw_r_k[l], rw_ln_g[l], rw_ln_b[l], w_branch_a[l], w_branch_b[l], w_out[l], norm2_g[l], peer_wq[l],
            peer_keys[l], peer_u[l], peer_v[l], layer_idx=l, update_ctx=l < DEPTH_2 - 1)
    return x


def setup_inputs(seed=0):
    out = dict(first_inputs(seed))
    for name, value in second_inputs(seed + 1).items():
        if name != "x":
            out[name + "_2"] = value
    return out


def reference(
    x, c, e_norm_mix, e_mod_mix_w, e_mod_mix_b, e_w_in, e_fox_fb, e_gla_w2, e_gla_b2,
    e_gla_norm, e_w_o, e_norm_ffn, e_mod_ffn_w, e_mod_ffn_b, e_ffn_gate, e_ffn_up, e_ffn_down,
    o_norm_mix, o_mod_mix_w, o_mod_mix_b, o_w_in, o_lam_re, o_lam_im, o_log_dt, o_b_re, o_b_im,
    o_c_re, o_c_im, o_d_skip, o_w_glu, o_w_o, o_norm_ffn, o_mod_ffn_w, o_mod_ffn_b, o_router,
    o_exp_gate, o_exp_up, o_exp_down, final_norm, c_2, ctx_2, c_ctx_2, w_mod_2, b_mod_2,
    norm1_g_2, w_in_2, q_norm_g_2, k_norm_g_2, diff_lambda_2, diff_out_g_2, rw_shift_2, rw_w0_2,
    rw_w_up_2, rw_a0_2, rw_a_up_2, rw_g_up_2, rw_k_k_2, rw_k_a_2, rw_r_k_2, rw_ln_g_2,
    rw_ln_b_2, w_branch_a_2, w_branch_b_2, w_out_2, norm2_g_2, peer_wq_2, peer_keys_2, peer_u_2,
    peer_v_2,
):
    x = first_block(
        x, c, e_norm_mix, e_mod_mix_w, e_mod_mix_b, e_w_in, e_fox_fb, e_gla_w2, e_gla_b2,
        e_gla_norm, e_w_o, e_norm_ffn, e_mod_ffn_w, e_mod_ffn_b, e_ffn_gate, e_ffn_up,
        e_ffn_down, o_norm_mix, o_mod_mix_w, o_mod_mix_b, o_w_in, o_lam_re, o_lam_im, o_log_dt,
        o_b_re, o_b_im, o_c_re, o_c_im, o_d_skip, o_w_glu, o_w_o, o_norm_ffn, o_mod_ffn_w,
        o_mod_ffn_b, o_router, o_exp_gate, o_exp_up, o_exp_down, final_norm,
    )
    return second_block(
        x, c_2, ctx_2, c_ctx_2, w_mod_2, b_mod_2, norm1_g_2, w_in_2, q_norm_g_2, k_norm_g_2,
        diff_lambda_2, diff_out_g_2, rw_shift_2, rw_w0_2, rw_w_up_2, rw_a0_2, rw_a_up_2,
        rw_g_up_2, rw_k_k_2, rw_k_a_2, rw_r_k_2, rw_ln_g_2, rw_ln_b_2, w_branch_a_2,
        w_branch_b_2, w_out_2, norm2_g_2, peer_wq_2, peer_keys_2, peer_u_2, peer_v_2,
    )


_drawn_inputs = setup_inputs


def setup_inputs(seed=0):
    import zlib

    import numpy as np

    out = dict(_drawn_inputs(seed))
    spreads = {}
    factors = {'e_gla_b2': 7.483,
     'e_gla_norm': 3.203,
     'o_norm_mix': 4.398,
     'o_mod_mix_b': 3.004,
     'o_lam_re': 64.0,
     'o_b_re': 2.898,
     'o_c_im': 2.9,
     'b_mod_2': 2.897,
     'norm1_g_2': 4.469,
     'q_norm_g_2': 8.0,
     'k_norm_g_2': 8.0,
     'diff_out_g_2': 39.144,
     'rw_w_up_2': 22.558,
     'rw_a_up_2': 4.417,
     'rw_ln_g_2': 55.464,
     'rw_ln_b_2': 64.0,
     'norm2_g_2': 23.744,
     'diff_lambda_2': 2.7,
     'rw_k_a_2': 2.767}
    for name, (base, spread) in spreads.items():
        noise = np.random.default_rng([zlib.crc32(name.encode()), seed]).standard_normal(out[name].shape)
        drawn = base * np.exp(spread * noise) if base else spread * noise
        out[name] = jnp.asarray(drawn.astype(out[name].dtype))
    for name, factor in factors.items():
        out[name] = (out[name] * factor).astype(out[name].dtype)
    return out
```

```python
import math
from contextlib import ExitStack

import numpy as np

import concourse.bass as bass
import concourse.mybir as mybir
from concourse.alu_op_type import AluOpType as ALU

ACT = mybir.ActivationFunctionType
AX = mybir.AxisListType
F32 = mybir.dt.float32
U32 = mybir.dt.uint32
I32 = mybir.dt.int32

P = 128
D = 1024
DC = D // P
S = 256
TT = S // P
EPS = 1e-6
NEG = -1e30
C64 = 64
NSLOT = 6
SLOT = 2048
BANKS = 8
FF = 2816
FF_STEPS = FF // 256


class Signal:

    def __init__(self, sem):
        self.sem, self.n = sem, 0

    def up(self, k=1):
        self.n += k
        return self.sem, k

    def now(self):
        return self.sem, self.n


def constant_table():
    p = np.arange(P)[:, None]
    f = np.arange(P)[None, :]
    same = (p // C64) == (f // C64)
    pi, fi = p % C64, f % C64
    t = {}
    t["ident"] = p == f
    t["ones"] = np.ones((P, S))
    t["upto"] = p <= f
    t["head_ones"] = same
    t["incl"] = same & (pi <= fi)
    t["strict"] = same & (pi < fi)
    t["incl_rev"] = same & (pi <= C64 - 1 - fi)
    for n in range(6):
        m = 1 << n
        t[f"level{n}"] = same & (pi // (2 * m) == fi // (2 * m)) & (pi // m % 2 == 0) & (fi // m % 2 == 1)
    t["fox_mask"] = np.where(f <= p, 0.0, NEG)
    t["reset"] = np.tile((np.arange(512) % C64 != 0).astype(np.float32), (P, 1))
    t["iota"] = np.tile(np.arange(P), (P, 1))
    t["fold"] = pi == np.arange(C64)[None, :]
    tok = np.arange(S)
    inv = 10000.0 ** (-np.arange(16, dtype=np.float32) / np.float32(16))
    ang = np.stack([(tok // 64)[:, None] * inv, (tok % 64)[:, None] * inv], axis=1).astype(np.float32)
    for name, fn in (("rope_cos", np.cos), ("rope_sin", np.sin)):
        t[name] = fn(ang).reshape(TT, P, 32).transpose(1, 0, 2).reshape(P, TT * 32)
    return {k: np.asarray(v, np.float32) for k, v in t.items()}


def constant_places():
    at, places = 0, {}
    for name, v in constant_table().items():
        places[name] = (at, v.shape[1])
        at += v.shape[1]
    return places, at


class Core:

    def __init__(self, nc, ins, ctx):
        self.nc, self.ins, self.ctx = nc, ins, ctx
        self.ps = ctx.enter_context(nc.psum_tensor("ps", [P, BANKS, 512], F32))
        self.places, n_const = constant_places()
        self.const = self.sb("const", [P, n_const])
        self.x = self.sb("x", [P, TT, D])
        self.h = self.sb("h", [P, TT, D])
        self.hT = self.sb("hT", [P, DC, S])
        self.ring = self.sb("ring", [P, NSLOT, SLOT])
        self.gain = self.sb("gain", [P, D])
        self.shift = self.sb("shift", [P, D])
        self.gate = self.sb("gate", [P, D])
        self.stat = self.sb("stat", [P, 64])
        self.pe_done = Signal(self.sem("pe_done"))
        self.dve_done = Signal(self.sem("dve_done"))
        self.act_done = Signal(self.sem("act_done"))
        self.pool_done = Signal(self.sem("pool_done"))
        self.slot_used = Signal(self.sem("slot_used"))
        self.evac_dve = Signal(self.sem("evac_dve"))
        self.evac_act = Signal(self.sem("evac_act"))
        self.up_ready = Signal(self.sem("up_ready"))
        self.silu_ready = Signal(self.sem("silu_ready"))
        self.prod_ready = Signal(self.sem("prod_ready"))
        self.down_used = Signal(self.sem("down_used"))
        self.y_free = Signal(self.sem("y_free"))
        self.landed = [Signal(self.sem(f"landed{i}")) for i in range(NSLOT)]
        self.loaded = Signal(self.sem("loaded"))
        self.job = 0

    def sem(self, name):
        return self.ctx.enter_context(self.nc.semaphore(name))

    def sb(self, name, shape, dt=F32, ctx=None):
        return (ctx or self.ctx).enter_context(self.nc.sbuf_tensor(name, shape, dt))

    def c(self, name):
        at, n = self.places[name]
        return self.const[:, at:at + n]


def load(k, pairs):
    with k.nc.Block() as block:
        @block.sync
        def _(sp):
            for dst, src in pairs:
                sp.dma_start(dst, src).then_inc(*k.loaded.up(16))
            sp.wait_ge(*k.loaded.now())


def gemm(k, jobs):
    nc = k.nc
    first, base = k.job, k.slot_used.n
    loads = []
    block_of = []
    for j, job in enumerate(jobs):
        if job[0] is not None:
            loads.append(j)
        block_of.append(len(loads) - 1)
    last_user = [max(j for j in range(len(jobs)) if block_of[j] == n) for n in range(len(loads))]
    k.job += len(loads)
    slot = lambda n: (first + n) % NSLOT
    engine_of = [job[3] for job in jobs]
    evac = {"v": k.evac_dve, "s": k.evac_act}
    evac_base = {e: evac[e].n for e in evac}
    evac_count = lambda j: evac_base[engine_of[j]] + engine_of[:j + 1].count(engine_of[j])
    landed_at = [0] * len(loads)

    with nc.Block() as block:
        @block.sync
        def _(sp):
            for n, j in enumerate(loads):
                src = jobs[j][0]
                w = src.shape[2]
                if n >= NSLOT:
                    sp.wait_ge(k.slot_used.sem, base + last_user[n - NSLOT] + 1)
                dst = k.ring[:, slot(n), 0:DC * w].rearrange("p (c n) -> p c n", c=DC)
                sp.dma_start(dst, src).then_inc(*k.landed[slot(n)].up(16))
                landed_at[n] = k.landed[slot(n)].n

        @block.tensor
        def _(pe):
            for j, (_src, kind, op, *_rest) in enumerate(jobs):
                n = block_of[j]
                w = jobs[loads[n]][0].shape[2]
                bank = k.ps[:, j % BANKS, :]
                wt = k.ring[:, slot(n), 0:DC * w].rearrange("p (c n) -> p c n", c=DC)
                pe.wait_ge(k.landed[slot(n)].sem, landed_at[n])
                if j >= BANKS:
                    pe.wait_ge(evac[engine_of[j - BANKS]].sem, evac_count(j - BANKS))
                if kind == "feat":
                    for f in range(0, w, P):
                        m = min(P, w - f)
                        for c in range(DC):
                            mm = nc.tensor.matmul(bank[0:m, f // P * S:f // P * S + S], wt[:, c, f:f + m],
                                                  op[:, c, :], start=(c == 0), stop=(c == DC - 1))
                elif kind == "tok":
                    for t in range(TT):
                        for c in range(DC):
                            mm = nc.tensor.matmul(bank[:, t * w:(t + 1) * w], op[:, c, t * P:(t + 1) * P],
                                                  wt[:, c, :], start=(c == 0), stop=(c == DC - 1))
                else:
                    for c in range(DC):
                        mm = nc.tensor.matmul(bank[:, 0:w], op[:, c, :], wt[:, c, :],
                                              start=(c == 0), stop=(c == DC - 1))
                mm.then_inc(*k.slot_used.up())

        def evacuations(eng, name, done):
            def link(ins):
                ins.then_inc(*done.up())
                eng.wait_ge(*done.now())

            for j, (src, kind, op, e, evacuate) in enumerate(jobs):
                if e == name:
                    eng.wait_ge(k.slot_used.sem, base + j + 1)
                    evacuate(k.ps[:, j % BANKS, :], link).then_inc(*evac[e].up())
                    eng.wait_ge(*evac[e].now())

        @block.vector
        def _(dve):
            evacuations(dve, "v", k.dve_done)

        @block.scalar
        def _(act):
            evacuations(act, "s", k.act_done)


def columns(w, a, b):
    v = w.rearrange("(c p) n -> p c n", p=P)
    return [v[:, :, i:min(i + 256, b)] for i in range(a, b, 256)]


def adaln_rows(k, conds, w, bias, norm, want, ctx, tag):
    nc = k.nc
    cs = k.sb(f"cs_{tag}", [P, len(conds), DC], ctx=ctx)
    cb = k.sb(f"cb_{tag}", [P, len(conds), DC, P], ctx=ctx)
    nb = k.sb(f"nb_{tag}", [P, D], ctx=ctx)
    bb = k.sb(f"bb_{tag}", [P, len(want), D], ctx=ctx)
    load(k, [(cs[:, i], c) for i, c in enumerate(conds)] + [(nb[:], norm.partition_broadcast(P))]
         + [(bb[:, i], bias[at * D:(at + 1) * D].partition_broadcast(P)) for i, (at, _) in enumerate(want)])
    with nc.Block() as block:
        @block.scalar
        def _(act):
            nc.scalar.activation(cs[:], cs[:], ACT.Silu).then_inc(*k.act_done.up())

        @block.vector
        def _(dve):
            dve.wait_ge(*k.act_done.now())
            for i in range(len(conds)):
                nc.vector.tensor_copy(cb[:, i], cs[:, i].unsqueeze(2).to_broadcast([P, DC, P])).then_inc(
                    *k.dve_done.up())

    def evac(i, kind, dst, col):
        b = bb[:, i, col:col + 256]

        def run(bank, link):
            o = dst[:, col:col + 256]
            if kind != "gain":
                return nc.vector.tensor_tensor(o, bank[:, 0:256], b, ALU.add)
            link(nc.vector.scalar_tensor_tensor(o, bank[:, 0:256], 1.0, b, ALU.add, ALU.add))
            return nc.vector.tensor_tensor(o, o, nb[:, col:col + 256], ALU.mult)
        return run

    jobs = []
    for i, (at, kinds) in enumerate(want):
        for n, src in enumerate(columns(w, at * D, (at + 1) * D)):
            for q, (kind, dst) in enumerate(kinds):
                jobs.append((src if q == 0 else None, "row", cb[:, q], "v", evac(i, kind, dst, n * 256)))
    gemm(k, jobs)


def transpose_tokens(k, src, dst, pe_wait, block):
    nc = k.nc

    @block.tensor
    def _(pe):
        pe.wait_ge(*pe_wait)
        for b in range(4):
            for i in range(4):
                c, t = 2 * b + i // 2, i % 2
                mm = nc.tensor.transpose(k.ps[:, b, i * P:(i + 1) * P], src[:, t, c * P:(c + 1) * P], k.c("ident"))
            mm.then_inc(*k.pe_done.up())

    @block.vector
    def _(dve):
        for b in range(4):
            dve.wait_ge(k.pe_done.sem, k.pe_done.n - 3 + b)
            nc.vector.tensor_copy(dst[:, 2 * b:2 * b + 2, :],
                                  k.ps[:, b, :].rearrange("p (c n) -> p c n", c=2)).then_inc(*k.dve_done.up())


def norm_modulate(k, src, gain, shift, h, hT, sq):
    nc = k.nc
    ss = k.stat[:, 0:TT]
    with nc.Block() as block:
        @block.scalar
        def _(act):
            for t in range(TT):
                nc.scalar.activation(sq[:, t, :], src[:, t, :], ACT.Square,
                                     accum_out=ss[:, t:t + 1]).then_inc(*k.act_done.up())

        @block.vector
        def _(dve):
            dve.wait_ge(*k.act_done.now())
            nc.vector.tensor_scalar(ss, ss, 1.0 / D, EPS, ALU.mult, ALU.add).then_inc(*k.dve_done.up())

        @block.scalar
        def _(act):
            act.wait_ge(*k.dve_done.now())
            nc.scalar.activation(ss, ss, ACT.Sqrt).then_inc(*k.act_done.up())

        @block.vector
        def _(dve):
            def link(ins):
                ins.then_inc(*k.dve_done.up())
                dve.wait_ge(*k.dve_done.now())

            dve.wait_ge(*k.act_done.now())
            link(nc.vector.reciprocal(ss, ss))
            for t in range(TT):
                link(nc.vector.scalar_tensor_tensor(h[:, t, :], src[:, t, :], ss[:, t:t + 1], gain,
                                                    ALU.mult, ALU.mult) if gain is not None else
                     nc.vector.tensor_scalar(h[:, t, :], src[:, t, :], ss[:, t:t + 1], None, ALU.mult))
                if shift is not None:
                    link(nc.vector.tensor_tensor(h[:, t, :], h[:, t, :], shift, ALU.add))

        if hT is not None:
            transpose_tokens(k, h, hT, k.dve_done.now(), block)


def add_to_x(k, gate):
    def at(col):
        def run(bank, link):
            b = bank.rearrange("p (t n) -> p t n", t=TT)
            link(k.nc.vector.tensor_tensor(b, b, gate[:, col:col + 256].unsqueeze(1).to_broadcast([P, TT, 256]),
                                           ALU.mult))
            xs = k.x[:, :, col:col + 256]
            return k.nc.vector.tensor_tensor(xs, b, xs, ALU.add)
        return run
    return at


def copy_tok(k, dst, col, eng, func=None):
    def run(bank, link):
        n = min(256, dst.shape[2] - col)
        b = bank[:, 0:TT * n].rearrange("p (t n) -> p t n", t=TT)
        o = dst[:, :, col:col + n]
        if func is not None:
            return k.nc.scalar.activation(o, b, func)
        return k.nc.vector.tensor_copy(o, b) if eng == "v" else k.nc.scalar.copy(o, b)
    return run


def copy_feat(k, dst, chunk, eng):
    def run(bank, link):
        b = bank.rearrange("p (c n) -> p c n", c=2)
        o = dst[:, chunk:chunk + 2, :]
        return k.nc.vector.tensor_copy(o, b) if eng == "v" else k.nc.scalar.copy(o, b)
    return run


def feat_pad(k, dst, pair):
    def run(bank, link):
        b = bank.rearrange("p (c n) -> p c n", c=2)
        link(k.nc.vector.tensor_copy(dst[0:64, pair:pair + 2, 0, :], b[0:64]))
        return k.nc.vector.tensor_copy(dst[64:128, pair:pair + 2, 1, :], b[64:128])
    return run


def even_mixer(k):
    nc, I = k.nc, k.ins
    with ExitStack() as ctx:
        sb = lambda name, shape, dt=F32: k.sb(name, shape, dt, ctx)
        fq = sb("fq", [P, 4, 2, S])
        fk = sb("fk", [P, 4, S])
        fv = sb("fv", [P, TT, 512])
        gv = sb("gv", [P, TT, 512])
        gg = sb("gg", [P, TT, 512])
        gq = sb("gq", [P, 2, S])
        gk = sb("gk", [P, 2, S])
        mix = sb("mix", [P, TT, D])
        wsm = sb("wsm", [P, DC, 24])
        fb = sb("fb", [P, 8])
        w2 = sb("w2", [16, 256])
        b2 = sb("b2", [P, 2])
        logf = sb("logf", [P, TT, 8])
        lf1 = sb("lf1", [P, TT, 8])
        glrT = sb("glrT", [16, S])
        la = sb("la", [P, 2, S])
        la1 = sb("la1", [P, 2, S])
        gn = sb("gn", [P, P])
        load(k, [(wsm[:], I["w_small"].rearrange("(c p) n -> p c n", p=P)), (fb[:], I["e_fox_fb"].partition_broadcast(P)),
                 (w2[:], I["e_gla_w2"]), (b2[:], I["e_gla_b2"]),
                 (gn[:], I["e_gla_norm"].partition_broadcast(P))])
        with nc.Block() as block:
            @block.vector
            def _(dve):
                nc.vector.memset(fq[:], 0.0).then_inc(*k.dve_done.up())

        W = I["e_w_in"]
        jobs = []
        for n, src in enumerate(columns(W, 0, 512)):
            jobs.append((src, "feat", k.hT, "v", feat_pad(k, fq, 2 * n)))
        for n, src in enumerate(columns(W, 512, 1024)):
            jobs.append((src, "feat", k.hT, "s", copy_feat(k, fk, 2 * n, "s")))
        for n, src in enumerate(columns(W, 1024, 1536)):
            jobs.append((src, "tok", k.hT, "v", copy_tok(k, fv, n * 256, "v")))
        jobs.append((columns(W, 1544, 1800)[0], "feat", k.hT, "s", copy_feat(k, gq, 0, "s")))
        jobs.append((columns(W, 1800, 2056)[0], "feat", k.hT, "s", copy_feat(k, gk, 0, "s")))
        for n, src in enumerate(columns(W, 2056, 2568)):
            jobs.append((src, "tok", k.hT, "v", copy_tok(k, gv, n * 256, "v")))
        for n, src in enumerate(columns(W, 2568, 3080)):
            jobs.append((src, "tok", k.hT, "s", copy_tok(k, gg, n * 256, "s", ACT.Silu)))
        gemm(k, jobs)

        def log_sigmoid(block, z, scratch):
            @block.vector
            def _(dve):
                def link(ins):
                    ins.then_inc(*k.dve_done.up())
                    dve.wait_ge(*k.dve_done.now())
                link(nc.vector.scalar_tensor_tensor(scratch, z, -1.0, z, ALU.mult, ALU.max))

            @block.scalar
            def _(act):
                act.wait_ge(*k.dve_done.now())
                nc.scalar.activation(scratch, scratch, ACT.Exp, scale=-1.0).then_inc(*k.act_done.up())
                act.wait_ge(*k.act_done.now())
                nc.scalar.activation(scratch, scratch, ACT.Ln, bias=1.0).then_inc(*k.act_done.up())

            @block.vector
            def _(dve):
                dve.wait_ge(*k.act_done.now())
                nc.vector.scalar_tensor_tensor(z, z, 0.0, scratch, ALU.min, ALU.subtract).then_inc(*k.dve_done.up())
                dve.wait_ge(*k.dve_done.now())

        with nc.Block() as block:
            @block.tensor
            def _(pe):
                for t in range(TT):
                    for c in range(DC):
                        nc.tensor.matmul(k.ps[:, 0, 8 * t:8 * t + 8], k.hT[:, c, t * P:(t + 1) * P], wsm[:, c, 0:8],
                                         start=(c == 0), stop=(c == DC - 1))
                for c in range(DC):
                    mm = nc.tensor.matmul(k.ps[0:16, 1, 0:S], wsm[:, c, 8:24], k.hT[:, c, :],
                                          start=(c == 0), stop=(c == DC - 1))
                mm.then_inc(*k.pe_done.up())

            @block.vector
            def _(dve):
                dve.wait_ge(*k.pe_done.now())
                nc.vector.tensor_tensor(logf[:], k.ps[:, 0, 0:16].rearrange("p (t n) -> p t n", t=TT),
                                        fb[:].unsqueeze(1).to_broadcast([P, TT, 8]), ALU.add).then_inc(*k.dve_done.up())
                nc.vector.tensor_copy(glrT[:], k.ps[0:16, 1, 0:S]).then_inc(*k.dve_done.up())

            @block.tensor
            def _(pe):
                pe.wait_ge(*k.dve_done.now())
                for c in range(2):
                    mm = nc.tensor.matmul(k.ps[:, 2, c * S:(c + 1) * S], w2[:, c * P:(c + 1) * P], glrT[:],
                                          start=True, stop=True)
                mm.then_inc(*k.pe_done.up())

            @block.vector
            def _(dve):
                dve.wait_ge(*k.pe_done.now())
                for c in range(2):
                    nc.vector.tensor_scalar(la[:, c, :], k.ps[:, 2, c * S:(c + 1) * S], b2[:, c:c + 1], None,
                                            ALU.add).then_inc(*k.dve_done.up())
                dve.wait_ge(*k.dve_done.now())

            log_sigmoid(block, logf[:], lf1[:])
            log_sigmoid(block, la[:], la1[:])

        fox_attention(k, ctx, fq, fk, fv, logf, mix)
        gla_attention(k, ctx, gq, gk, gv, gg, la, gn, mix)

        with nc.Block() as block:
            transpose_tokens(k, mix, k.hT, k.dve_done.now(), block)
        add = add_to_x(k, k.gate)
        gemm(k, [(src, "tok", k.hT, "v", add(n * 256)) for n, src in enumerate(columns(I["e_w_o"], 0, D))])


def fox_attention(k, ctx, fq, fk, fv, logf, mix):
    nc = k.nc
    H = 8
    cum = k.sb("fox_cum", [1, H, S], ctx=ctx)
    ncum = k.sb("fox_ncum", [1, H, S], ctx=ctx)
    sm = k.sb("fox_sm", [P, 2, 384], ctx=ctx)
    pT = k.sb("fox_pT", [P, 2, 384], ctx=ctx)
    mx = k.sb("fox_mx", [P, 2, 2], ctx=ctx)
    rs = k.sb("fox_rs", [P, 2, 2], ctx=ctx)
    sem = lambda n: Signal(k.sem(n))
    scores_ready, masked, probs_ready, turned, turned_copied, out_ready, out_copied = map(
        sem, ("fox_scores", "fox_masked", "fox_probs", "fox_turned", "fox_turned_copied", "fox_out", "fox_out_copied"))

    with nc.Block() as block:
        @block.tensor
        def _(pe):
            for h in range(H):
                o = k.ps[0:1, h // 2, h % 2 * S:h % 2 * S + S]
                nc.tensor.matmul(o[:, 0:P], logf[:, 0, h:h + 1], k.c("upto"), start=True, stop=True)
                nc.tensor.matmul(o[:, P:S], logf[:, 0, h:h + 1], k.c("ones")[:, 0:P], start=True, stop=False)
                mm = nc.tensor.matmul(o[:, P:S], logf[:, 1, h:h + 1], k.c("upto"), start=False, stop=True)
            mm.then_inc(*k.pe_done.up())

        @block.vector
        def _(dve):
            dve.wait_ge(*k.pe_done.now())
            src = k.ps[0:1, 0:4, :].rearrange("p b (h n) -> p (b h) n", h=2)
            nc.vector.tensor_copy(cum[:], src).then_inc(*k.dve_done.up())
            nc.vector.tensor_scalar(ncum[:], src, -1.0, None, ALU.mult).then_inc(*k.dve_done.up())
            dve.wait_ge(*k.dve_done.now())
            nc.vector.tensor_scalar(fq[:], fq[:], 0.125, None, ALU.mult).then_inc(*k.dve_done.up())

    keys = lambda t: (t + 1) * P
    with nc.Block() as block:
        @block.tensor
        def _(pe):
            def scores(h):
                if h >= 2:
                    pe.wait_ge(masked.sem, h - 1)
                for t in range(TT):
                    o = k.ps[:, h % 2, t * P:t * P + keys(t)]
                    nc.tensor.matmul(o, fq[:, h // 2, h % 2, t * P:(t + 1) * P], fk[:, h // 2, 0:keys(t)],
                                     start=True, stop=False)
                    nc.tensor.matmul(o, cum[:, h, t * P:(t + 1) * P], k.c("ones")[0:1, 0:keys(t)],
                                     start=False, stop=False)
                    mm = nc.tensor.matmul(o, k.c("ones")[0:1, 0:P], ncum[:, h, 0:keys(t)], start=False, stop=True)
                mm.then_inc(*scores_ready.up())

            def turn(h):
                pe.wait_ge(probs_ready.sem, h + 1)
                if h >= 2:
                    pe.wait_ge(turned_copied.sem, h - 1)
                for i in range(3):
                    mm = nc.tensor.transpose(k.ps[:, 2 + h % 2, i * P:(i + 1) * P], sm[:, h % 2, i * P:(i + 1) * P],
                                             k.c("ident"))
                mm.then_inc(*turned.up())

            def values(h):
                pe.wait_ge(turned_copied.sem, h + 1)
                if h >= 2:
                    pe.wait_ge(out_copied.sem, h - 1)
                v = lambda t: fv[:, t, h * 64:(h + 1) * 64]
                b = k.ps[:, 4 + h % 2, :]
                nc.tensor.matmul(b[:, 0:64], pT[:, h % 2, 0:P], v(0), start=True, stop=True)
                nc.tensor.matmul(b[:, 64:128], pT[:, h % 2, P:2 * P], v(0), start=True, stop=False)
                nc.tensor.matmul(b[:, 64:128], pT[:, h % 2, 2 * P:3 * P], v(1), start=False,
                                 stop=True).then_inc(*out_ready.up())

            for i in range(H + 2):
                if i < H:
                    scores(i)
                if 1 <= i <= H:
                    turn(i - 1)
                if i >= 2:
                    values(i - 2)

        @block.vector
        def _(dve):
            def link(ins):
                ins.then_inc(*k.dve_done.up())
                dve.wait_ge(*k.dve_done.now())

            def mask(h):
                dve.wait_ge(scores_ready.sem, h + 1)
                if h >= 2:
                    dve.wait_ge(turned.sem, h - 1)
                b, m = k.ps[:, h % 2, :], k.c("fox_mask")
                nc.vector.tensor_tensor(sm[:, h % 2, 0:P], b[:, 0:P], m, ALU.add).then_inc(*k.dve_done.up())
                nc.vector.tensor_copy(sm[:, h % 2, P:2 * P], b[:, P:2 * P]).then_inc(*k.dve_done.up())
                link(nc.vector.tensor_tensor(sm[:, h % 2, 2 * P:3 * P], b[:, 2 * P:3 * P], m, ALU.add))
                link(nc.vector.tensor_reduce(mx[:, h % 2, 0:1], sm[:, h % 2, 0:P], AX.X, ALU.max))
                link(nc.vector.tensor_reduce(mx[:, h % 2, 1:2], sm[:, h % 2, P:3 * P], AX.X, ALU.max))
                nc.vector.tensor_scalar(mx[:, h % 2, :], mx[:, h % 2, :], -1.0, None, ALU.mult).then_inc(*masked.up())

            def copy_turned(h):
                dve.wait_ge(turned.sem, h + 1)
                if h >= 2:
                    dve.wait_ge(out_ready.sem, h - 1)
                nc.vector.tensor_copy(pT[:, h % 2, :], k.ps[:, 2 + h % 2, 0:384]).then_inc(*turned_copied.up())

            def copy_out(h):
                dve.wait_ge(out_ready.sem, h + 1)
                dve.wait_ge(probs_ready.sem, h + 1)
                link(nc.vector.reciprocal(rs[:, h % 2, :], rs[:, h % 2, :]))
                for t in range(TT):
                    ins = nc.vector.tensor_scalar(mix[:, t, h * 64:(h + 1) * 64],
                                                  k.ps[:, 4 + h % 2, t * 64:(t + 1) * 64],
                                                  rs[:, h % 2, t:t + 1], None, ALU.mult)
                    if t == 0:
                        link(ins)
                ins.then_inc(*out_copied.up())

            for i in range(H + 2):
                if i < H:
                    mask(i)
                if 1 <= i <= H:
                    copy_turned(i - 1)
                if i >= 2:
                    copy_out(i - 2)

        @block.scalar
        def _(act):
            for h in range(H):
                act.wait_ge(masked.sem, h + 1)
                if h >= 2:
                    act.wait_ge(out_copied.sem, h - 1)
                nc.scalar.activation(sm[:, h % 2, 0:P], sm[:, h % 2, 0:P], ACT.Exp, bias=mx[:, h % 2, 0:1],
                                     accum_out=rs[:, h % 2, 0:1]).then_inc(*k.act_done.up())
                nc.scalar.activation(sm[:, h % 2, P:3 * P], sm[:, h % 2, P:3 * P], ACT.Exp, bias=mx[:, h % 2, 1:2],
                                     accum_out=rs[:, h % 2, 1:2]).then_inc(*probs_ready.up())


def gla_attention(k, ctx, gq, gk, gv, gg, la, gn, mix):
    nc = k.nc
    sb = lambda name, shape: k.sb(name, shape, ctx=ctx)
    b = sb("gla_b", [P, 8, C64])
    e1 = sb("gla_e1", [P, 8, C64])
    e2 = sb("gla_e2", [P, 8, C64])
    qin = sb("gla_qin", [P, 2, 2, S])
    qst = sb("gla_qst", [P, 2, 2, S])
    kin = sb("gla_kin", [P, 2, S])
    kst = sb("gla_kst", [P, 2, S])
    kpad = sb("gla_kpad", [P, TT, 2, 2, 2, P])
    att = sb("gla_att", [P, TT, 4, P])
    state = sb("gla_state", [P, 2, P])
    el = sb("gla_el", [P, 8])
    o = sb("gla_o", [P, TT, 4, P])
    sq = sb("gla_sq", [P, TT, 4, P])
    ss = sb("gla_ss", [P, TT * 4])
    g8 = lambda ap: ap.rearrange("p a (c n) -> p (a c) n", n=C64)
    cb = lambda ap: ap.to_broadcast([P, 8, C64])

    with nc.Block() as block:
        def dve_link(dve):
            def link(ins):
                ins.then_inc(*k.dve_done.up())
                dve.wait_ge(*k.dve_done.now())
            return link

        @block.vector
        def _(dve):
            link = dve_link(dve)
            nc.vector.memset(qin[:], 0.0).then_inc(*k.dve_done.up())
            nc.vector.memset(qst[:], 0.0).then_inc(*k.dve_done.up())
            nc.vector.memset(kpad[:], 0.0).then_inc(*k.dve_done.up())
            nc.vector.memset(state[:], 0.0).then_inc(*k.dve_done.up())
            link(nc.vector.tensor_scalar(la[:], la[:], 1.0 / 16.0, None, ALU.mult))
            link(nc.vector.tensor_tensor_scan(b[:].rearrange("p a n -> p (a n)"), k.c("reset"),
                                              la[:].rearrange("p a n -> p (a n)"), 0.0, ALU.mult, ALU.add))
            link(nc.vector.tensor_tensor(e1[:], b[:], cb(b[:, :, 31:32]), ALU.subtract))
            link(nc.vector.tensor_scalar(e2[:], e1[:], -1.0, 43.0, ALU.mult, ALU.min))
            link(nc.vector.tensor_scalar(e1[:], e1[:], 43.0, None, ALU.min))

        @block.scalar
        def _(act):
            act.wait_ge(*k.dve_done.now())
            nc.scalar.activation(e1[:], e1[:], ACT.Exp).then_inc(*k.act_done.up())
            nc.scalar.activation(e2[:], e2[:], ACT.Exp).then_inc(*k.act_done.up())
            nc.scalar.activation(el[:], b[:, :, 63], ACT.Exp).then_inc(*k.act_done.up())

        def scaled_q(dst, e):
            for h in range(2):
                r = slice(64 * h, 64 * h + 64)
                for p in range(2):
                    nc.vector.scalar_tensor_tensor(
                        dst[r, p, h, :], gq[r, p, :], 0.125, e[r, 4 * p:4 * p + 4, :].rearrange("p a n -> p (a n)"),
                        ALU.mult, ALU.mult).then_inc(*k.dve_done.up())

        @block.vector
        def _(dve):
            link = dve_link(dve)
            dve.wait_ge(*k.act_done.now())
            scaled_q(qin, e1)
            link(nc.vector.tensor_tensor(g8(kin[:]), g8(gk[:]), e2[:], ALU.mult))
            link(nc.vector.tensor_tensor(e2[:], cb(b[:, :, 63:64]), b[:], ALU.subtract))

        @block.scalar
        def _(act):
            act.wait_ge(*k.dve_done.now())
            nc.scalar.activation(e1[:], b[:], ACT.Exp).then_inc(*k.act_done.up())
            nc.scalar.activation(e2[:], e2[:], ACT.Exp).then_inc(*k.act_done.up())

        @block.vector
        def _(dve):
            link = dve_link(dve)
            dve.wait_ge(*k.act_done.now())
            scaled_q(qst, e1)
            link(nc.vector.tensor_tensor(g8(kst[:]), g8(gk[:]), e2[:], ALU.mult))

        @block.tensor
        def _(pe):
            pe.wait_ge(*k.dve_done.now())
            for t in range(TT):
                for h in range(4):
                    mm = nc.tensor.matmul(k.ps[:, t, h * P:(h + 1) * P], kin[:, h // 2, t * P:(t + 1) * P],
                                          qin[:, h // 2, h % 2, t * P:(t + 1) * P], start=True, stop=True)
                mm.then_inc(*k.pe_done.up())
            for t in range(TT):
                for p in range(2):
                    i = t * 2 + p
                    mm = nc.tensor.transpose(k.ps[:, 2, i * P:(i + 1) * P], kst[:, p, t * P:(t + 1) * P], k.c("ident"))
            mm.then_inc(*k.pe_done.up())

        @block.vector
        def _(dve):
            link = dve_link(dve)
            dve.wait_ge(*k.pe_done.now())
            for t in range(TT):
                nc.vector.tensor_tensor(att[:, t], k.ps[:, t, :].rearrange("p (h n) -> p h n", h=4),
                                        k.c("incl").unsqueeze(1).to_broadcast([P, 4, P]),
                                        ALU.mult).then_inc(*k.dve_done.up())
            for t in range(TT):
                for cc in range(2):
                    for h in range(2):
                        r = slice(64 * cc, 64 * cc + 64)
                        src = k.ps[r, 2, t * 256:(t + 1) * 256].rearrange("p (a n) -> p a n", a=2)
                        nc.vector.tensor_copy(kpad[r, t, cc, :, h, 64 * h:64 * h + 64],
                                              src[:, :, 64 * h:64 * h + 64]).then_inc(*k.dve_done.up())

        for c in range(4):
            t, cc = c // 2, c % 2

            @block.tensor
            def _(pe):
                pe.wait_ge(*k.dve_done.now())
                for h in range(4):
                    out = k.ps[64 * cc:64 * cc + 64, 4 + t, h * P:(h + 1) * P]
                    nc.tensor.matmul(out, qst[:, h // 2, h % 2, c * 64:(c + 1) * 64], state[:, h // 2, :],
                                     start=True, stop=False)
                    nc.tensor.matmul(out, att[:, t, h, 64 * cc:64 * cc + 64], gv[:, t, h * P:(h + 1) * P],
                                     start=False, stop=True)
                for p in range(2):
                    for h in range(2):
                        mm = nc.tensor.matmul(k.ps[:, 6, p * P:(p + 1) * P], kpad[:, t, cc, p, h, :],
                                              gv[:, t, (2 * p + h) * P:(2 * p + h + 1) * P],
                                              start=(h == 0), stop=(h == 1))
                mm.then_inc(*k.pe_done.up())

            @block.vector
            def _(dve):
                dve.wait_ge(*k.pe_done.now())
                for p in range(2):
                    nc.vector.scalar_tensor_tensor(state[:, p, :], state[:, p, :], el[:, 4 * p + c:4 * p + c + 1],
                                                   k.ps[:, 6, p * P:(p + 1) * P], ALU.mult,
                                                   ALU.add).then_inc(*k.dve_done.up())
                if cc:
                    nc.vector.tensor_copy(o[:, t], k.ps[:, 4 + t, :].rearrange("p (h n) -> p h n", h=4)).then_inc(
                        *k.dve_done.up())

        @block.scalar
        def _(act):
            act.wait_ge(*k.dve_done.now())
            nc.scalar.activation(sq[:], o[:], ACT.Square).then_inc(*k.act_done.up())

        @block.vector
        def _(dve):
            link = dve_link(dve)
            dve.wait_ge(*k.act_done.now())
            link(nc.vector.tensor_reduce(ss[:], sq[:].rearrange("p t h n -> p (t h) n"), AX.X, ALU.add))
            link(nc.vector.tensor_scalar(ss[:], ss[:], 1.0 / P, EPS, ALU.mult, ALU.add))

        @block.scalar
        def _(act):
            act.wait_ge(*k.dve_done.now())
            nc.scalar.activation(ss[:], ss[:], ACT.Sqrt).then_inc(*k.act_done.up())

        @block.vector
        def _(dve):
            link = dve_link(dve)
            dve.wait_ge(*k.act_done.now())
            link(nc.vector.reciprocal(ss[:], ss[:]))
            o8 = o[:].rearrange("p t h n -> p (t h) n")
            link(nc.vector.tensor_tensor(o8, o8, ss[:].unsqueeze(2).to_broadcast([P, 8, P]), ALU.mult))
            link(nc.vector.tensor_tensor(o8, o8, gn[:].unsqueeze(1).to_broadcast([P, 8, P]), ALU.mult))
            for t in range(TT):
                link(nc.vector.tensor_tensor(mix[:, t, 512:D], o[:, t].rearrange("p h n -> p (h n)"), gg[:, t, :],
                                             ALU.mult))


def feed_forward(k, w_gate, w_up, w_down, gates, acc, ctx, tag):
    nc = k.nc
    E = w_gate.shape[0]
    sg = k.sb(f"sg_{tag}", [P, 2, 2, S], ctx=ctx)
    prod = k.sb(f"prod_{tag}", [P, 2, 2, S], ctx=ctx)
    up0, silu0, prod0, down0, free0 = (s.n for s in (k.up_ready, k.silu_ready, k.prod_ready, k.down_used, k.y_free))
    land0 = [s.n for s in k.landed]
    per = min(E, 2)
    steps = per * FF_STEPS
    turns = E // per
    wv = {"g": w_gate.rearrange("e (c p) n -> e p c n", p=P), "u": w_up.rearrange("e (c p) n -> e p c n", p=P),
          "d": w_down.rearrange("e (c p) n -> e p c n", p=P)}

    def over_turns(eng, body):
        if turns == 1:
            body(0)
        else:
            with eng.Fori(0, turns) as i:
                body(i)

    loads_before = lambda n: (n + 1) // 2

    with nc.Block() as block:
        @block.sync
        def _(sp):
            def body(i):
                for n in range(steps):
                    e, s = i * per + n // FF_STEPS, n % FF_STEPS
                    past = turns > 1 or n >= 2
                    if past:
                        sp.wait_ge(k.up_ready.sem, i * steps + (up0 + n - 1))
                    for kind, at in (("g", 0), ("u", 2)):
                        dst = k.ring[:, at + n % 2, :].rearrange("p (c n) -> p c n", c=DC)
                        sp.dma_start(dst, wv[kind][e, :, :, s * 256:(s + 1) * 256]).then_inc(
                            k.landed[at + n % 2].sem, 16)
                    if past:
                        sp.wait_ge(k.down_used.sem, i * steps + (down0 + n - 1))
                    dst = k.ring[:, 4 + n % 2, :].rearrange("p (c n) -> p c n", c=2)
                    sp.dma_start(dst, wv["d"][e, :, 2 * s:2 * s + 2, :]).then_inc(k.landed[4 + n % 2].sem, 16)
            over_turns(sp, body)

        @block.tensor
        def _(pe):
            def body(i):
                def landed(slot, n):
                    pe.wait_ge(k.landed[slot].sem, i * (16 * (steps // 2)) + (land0[slot] + 16 * (n // 2 + 1)))

                def hidden(n):
                    landed(n % 2, n)
                    landed(2 + n % 2, n)
                    if turns > 1 or n >= 2:
                        pe.wait_ge(k.prod_ready.sem, i * steps + (prod0 + n - 1))
                    for at, b in ((0, 0), (2, 1)):
                        w = k.ring[:, at + n % 2, :].rearrange("p (c n) -> p c n", c=DC)
                        for f in range(2):
                            for c in range(DC):
                                mm = nc.tensor.matmul(k.ps[:, 2 * (n % 2) + b, f * S:(f + 1) * S],
                                                      w[:, c, f * P:(f + 1) * P], k.hT[:, c, :],
                                                      start=(c == 0), stop=(c == DC - 1))
                    mm.then_inc(k.up_ready.sem, 1)

                def down(n):
                    s = n % FF_STEPS
                    landed(4 + n % 2, n)
                    pe.wait_ge(k.prod_ready.sem, i * steps + (prod0 + n + 1))
                    if s == 0 and (turns > 1 or n):
                        pe.wait_ge(k.y_free.sem, i * per + (free0 + n // FF_STEPS))
                    w = k.ring[:, 4 + n % 2, :].rearrange("p (c n) -> p c n", c=2)
                    for t in range(TT):
                        for half in range(2):
                            for f in range(2):
                                mm = nc.tensor.matmul(k.ps[:, 4 + 2 * t + half, :], prod[:, n % 2, f, t * P:(t + 1) * P],
                                                      w[:, f, half * 512:(half + 1) * 512],
                                                      start=(s == 0 and f == 0), stop=(s == FF_STEPS - 1 and f == 1))
                    mm.then_inc(k.down_used.sem, 1)

                for n in range(steps):
                    hidden(n)
                    if n:
                        down(n - 1)
                down(steps - 1)
            over_turns(pe, body)

        @block.scalar
        def _(act):
            def body(i):
                for n in range(steps):
                    act.wait_ge(k.up_ready.sem, i * steps + (up0 + n + 1))
                    if turns > 1 or n >= 2:
                        act.wait_ge(k.prod_ready.sem, i * steps + (prod0 + n - 1))
                    nc.scalar.activation(sg[:, n % 2], k.ps[:, 2 * (n % 2), :].rearrange("p (f n) -> p f n", f=2),
                                         ACT.Silu).then_inc(k.silu_ready.sem, 1)
            over_turns(act, body)

        @block.vector
        def _(dve):
            def body(i):
                for n in range(steps):
                    dve.wait_ge(k.silu_ready.sem, i * steps + (silu0 + n + 1))
                    if turns > 1 or n >= 2:
                        dve.wait_ge(k.down_used.sem, i * steps + (down0 + n - 1))
                    nc.vector.tensor_tensor(prod[:, n % 2], sg[:, n % 2],
                                            k.ps[:, 2 * (n % 2) + 1, :].rearrange("p (f n) -> p f n", f=2),
                                            ALU.mult).then_inc(k.prod_ready.sem, 1)
                    if n % FF_STEPS == FF_STEPS - 1:
                        dve.wait_ge(k.down_used.sem, i * steps + (down0 + n + 1))
                        e = i * per + n // FF_STEPS
                        for t in range(TT):
                            for half in range(2):
                                a = acc[:, t, half * 512:(half + 1) * 512]
                                ins = nc.vector.scalar_tensor_tensor(
                                    a, k.ps[:, 4 + 2 * t + half, :], gates[:, t, bass.ds(e, 1)], a, ALU.mult, ALU.add)
                        ins.then_inc(k.y_free.sem, 1)
            over_turns(dve, body)

    for s in (k.up_ready, k.silu_ready, k.prod_ready, k.down_used):
        s.n += E * FF_STEPS
    k.y_free.n += E
    for i, s in enumerate(k.landed):
        s.n += 16 * turns * ((steps + 1 - i % 2) // 2)
    k.job += (-k.job) % NSLOT


def add_gated(k, acc, gate):
    nc = k.nc
    with nc.Block() as block:
        @block.vector
        def _(dve):
            nc.vector.tensor_tensor(acc[:], acc[:], gate.unsqueeze(1).to_broadcast([P, TT, D]),
                                    ALU.mult).then_inc(*k.dve_done.up())
            dve.wait_ge(*k.dve_done.now())
            nc.vector.tensor_tensor(k.x[:], k.x[:], acc[:], ALU.add).then_inc(*k.dve_done.up())


def even_ffn(k):
    nc, I = k.nc, k.ins
    with ExitStack() as ctx:
        acc = k.sb("ffn_acc", [P, TT, D], ctx=ctx)
        one = k.sb("ffn_one", [P, TT, 1], ctx=ctx)
        with nc.Block() as block:
            @block.vector
            def _(dve):
                nc.vector.memset(acc[:], 0.0).then_inc(*k.dve_done.up())
                nc.vector.memset(one[:], 1.0).then_inc(*k.dve_done.up())
        feed_forward(k, I["e_ffn_gate"], I["e_ffn_up"], I["e_ffn_down"], one, acc, ctx, "ffn")
        add_gated(k, acc, k.gate[:])


def s5_mixer(k):
    nc, I = k.nc, k.ins
    NT = 32
    with ExitStack() as ctx:
        sb = lambda name, shape, dt=F32: k.sb("s5_" + name, shape, dt, ctx)
        uT = sb("uT", [P, DC, S])
        par = sb("par", [P, 3, NT])
        m = {n: sb(n, [P, NT]) for n in ("dt", "mag", "th", "sin", "cos", "den", "nr", "f_re", "f_im", "t0", "t1")}
        ti = sb("ti", [P, NT], I32)
        braw = sb("braw", [P, 2, NT, 16])
        craw = sb("craw", [P, 2, NT, 16])
        cpad = sb("cpad", [P, 2, NT, 32])
        w = sb("w", [P, 2, 2, NT])
        dsk = sb("dsk", [P, DC])
        e_im = sb("e_im", [P, NT, S])
        e_re = k.ring[:].rearrange("p a n -> p (a n)")[:, 0:NT * S].rearrange("p (j n) -> p j n", j=NT)
        spare = k.ring[:].rearrange("p a n -> p (a n)")[:, NT * S:].rearrange("p (a n) -> p a n", a=2)
        tmp_v = spare[:, 0, 0:1024]
        tmp_p = spare[:, 0, 1024:2048]
        bpad = spare[:, 1, 0:1024].rearrange("p (r j n) -> p r j n", r=2, j=4)
        bT = spare[:, 1, 1024:2048].rearrange("p (r j n) -> p r j n", r=2, j=4)
        z = sb("z", [P, 2, 4, S])
        t4 = sb("t4", [P, 2, 4, S])
        load(k, [(par[:], I["s5_par"]), (braw[:], I["s5_b"]), (craw[:], I["s5_c"]), (dsk[:], I["s5_dskip"])])
        gemm(k, [(src, "feat", k.hT, "s", copy_feat(k, uT, 2 * n, "s")) for n, src in enumerate(columns(I["o_w_in"], 0, D))])

        V = nc.vector
        tt = lambda o, a, b, op: V.tensor_tensor(o, a, b, op)
        TWO_PI_HI = 6.28125
        TWO_PI_LO = 2 * math.pi - TWO_PI_HI

        with nc.Block() as block:
            def linker(eng, done):
                def link(ins):
                    ins.then_inc(*done.up())
                    eng.wait_ge(*done.now())
                return link

            @block.scalar
            def _(act):
                nc.scalar.activation(m["dt"][:], par[:, 2, :], ACT.Exp).then_inc(*k.act_done.up())

            @block.vector
            def _(dve):
                link = linker(dve, k.dve_done)
                dve.wait_ge(*k.act_done.now())
                link(tt(m["th"][:], par[:, 1, :], m["dt"][:], ALU.mult))
                link(tt(m["mag"][:], par[:, 0, :], m["dt"][:], ALU.mult))
                for name, turn, quarter in (("sin", 0.0, 0.0), ("cos", 0.25, math.pi / 2)):
                    a, t0 = m[name][:], m["t0"][:]
                    link(V.tensor_scalar(ti[:], m["th"][:], 1 / (2 * math.pi), turn, ALU.mult, ALU.add))
                    link(V.tensor_copy(t0, ti[:]))
                    link(V.scalar_tensor_tensor(a, t0, -TWO_PI_HI, m["th"][:], ALU.mult, ALU.add))
                    link(V.scalar_tensor_tensor(a, t0, -TWO_PI_LO, a, ALU.mult, ALU.add))
                    link(V.tensor_scalar(a, a, quarter, 3.1415925, ALU.add, ALU.min))
                    link(V.tensor_scalar(a, a, -3.1415925, None, ALU.max))

            @block.scalar
            def _(act):
                act.wait_ge(*k.dve_done.now())
                nc.scalar.activation(m["mag"][:], m["mag"][:], ACT.Exp).then_inc(*k.act_done.up())
                nc.scalar.activation(m["sin"][:], m["sin"][:], ACT.Sin).then_inc(*k.act_done.up())
                nc.scalar.activation(m["cos"][:], m["cos"][:], ACT.Sin).then_inc(*k.act_done.up())

            @block.vector
            def _(dve):
                link = linker(dve, k.dve_done)
                dve.wait_ge(*k.act_done.now())
                lre, lim = par[:, 0, :], par[:, 1, :]
                nr, ni, t0, t1, den = (m[x][:] for x in ("nr", "th", "t0", "t1", "den"))
                link(tt(nr, m["mag"][:], m["cos"][:], ALU.mult))
                link(V.tensor_scalar(nr, nr, -1.0, None, ALU.add))
                link(tt(ni, m["mag"][:], m["sin"][:], ALU.mult))
                link(tt(t0, lre, lre, ALU.mult))
                link(tt(t1, lim, lim, ALU.mult))
                link(tt(den, t0, t1, ALU.add))
                link(V.reciprocal(den, den))
                for f, a, b, op in ((m["f_re"][:], nr, ni, ALU.add), (m["f_im"][:], ni, nr, ALU.subtract)):
                    link(tt(t0, a, lre, ALU.mult))
                    link(tt(t1, b, lim, ALU.mult))
                    link(tt(t0, t0, t1, op))
                    link(tt(f, t0, den, ALU.mult))
                fb = lambda f: m[f][:].unsqueeze(2).to_broadcast([P, NT, 16])
                s = [t4[:, 0, a, :].rearrange("p (j n) -> p j n", n=16) for a in range(4)]
                s = [t4[:].rearrange("p r a n -> p (r a n)")[:, i * 512:(i + 1) * 512].rearrange(
                    "p (j n) -> p j n", n=16) for i in range(4)]
                for i, (f, b) in enumerate((("f_re", 0), ("f_im", 1), ("f_re", 1), ("f_im", 0))):
                    link(tt(s[i], fb(f), braw[:, b], ALU.mult))
                link(tt(braw[:, 0], s[0], s[1], ALU.subtract))
                link(tt(braw[:, 1], s[2], s[3], ALU.add))
                link(V.memset(cpad[:], 0.0))
                for r, sign in ((0, 1.0), (1, -1.0)):
                    for g in range(2):
                        q = slice(64 * g, 64 * g + 64)
                        link(V.tensor_scalar(cpad[q, r, :, 16 * g:16 * g + 16], craw[q, r], sign, None, ALU.mult))
                link(V.memset(bpad, 0.0))
                link(V.memset(e_re[:, :, 0:1], 1.0))
                link(V.memset(e_im[:, :, 0:1], 0.0))
                link(V.tensor_copy(w[:, 0, 0, :], m["cos"][:]))
                link(V.tensor_copy(w[:, 0, 1, :], m["sin"][:]))

            for level in range(8):
                n = 1 << level
                a, b = level % 2, 1 - level % 2

                @block.gpsimd
                def _(pool):
                    link = linker(pool, k.pool_done)
                    pool.wait_ge(*k.dve_done.now())
                    for g in range(0, NT, 8):
                        wr, wi = (w[:, a, r, g:g + 8].unsqueeze(2).to_broadcast([P, 8, n]) for r in range(2))
                        o, t = e_im[:, g:g + 8, n:2 * n], tmp_p[:, 0:8 * n].rearrange("p (j n) -> p j n", j=8)
                        link(nc.gpsimd.tensor_tensor(o, e_im[:, g:g + 8, 0:n], wr, ALU.mult))
                        link(nc.gpsimd.tensor_tensor(t, e_re[:, g:g + 8, 0:n], wi, ALU.mult))
                        link(nc.gpsimd.tensor_tensor(o, o, t, ALU.add))

                @block.vector
                def _(dve):
                    link = linker(dve, k.dve_done)
                    for g in range(0, NT, 8):
                        wr, wi = (w[:, a, r, g:g + 8].unsqueeze(2).to_broadcast([P, 8, n]) for r in range(2))
                        o, t = e_re[:, g:g + 8, n:2 * n], tmp_v[:, 0:8 * n].rearrange("p (j n) -> p j n", j=8)
                        link(tt(o, e_re[:, g:g + 8, 0:n], wr, ALU.mult))
                        link(tt(t, e_im[:, g:g + 8, 0:n], wi, ALU.mult))
                        link(tt(o, o, t, ALU.subtract))
                    wr, wi, t0, t1 = w[:, a, 0, :], w[:, a, 1, :], m["t0"][:], m["t1"][:]
                    link(tt(t0, wr, wr, ALU.mult))
                    link(tt(t1, wi, wi, ALU.mult))
                    link(tt(w[:, b, 0, :], t0, t1, ALU.subtract))
                    link(V.scalar_tensor_tensor(w[:, b, 1, :], wr, 2.0, wi, ALU.mult, ALU.mult))
                    dve.wait_ge(*k.pool_done.now())

        sem = lambda n: Signal(k.sem("s5_" + n))
        b_laid, b_turned, bT_ready, bu_ready, bu_read, z_ready, xr_ready, xi_ready, y_ready, y_read, x_used = map(
            sem, ("b_laid", "b_turned", "bT_ready", "bu_ready", "bu_read", "z_ready", "xr_ready", "xi_ready",
                  "y_ready", "y_read", "x_used"))
        yT = k.hT
        with nc.Block() as block:
            @block.scalar
            def _(act):
                for c in range(DC):
                    if c:
                        act.wait_ge(b_turned.sem, c)
                    for r in range(2):
                        for j in range(4):
                            for g in range(2):
                                q = slice(64 * g, 64 * g + 64)
                                ins = nc.scalar.copy(bpad[q, r, j, 32 * j + 16 * g:32 * j + 16 * g + 16],
                                                     braw[q, r, 4 * c + j, :])
                    ins.then_inc(*b_laid.up())
                    act.wait_ge(b_turned.sem, c + 1)
                    if c:
                        act.wait_ge(bu_ready.sem, c)
                    nc.scalar.copy(bT[:], k.ps[:, 4:6, :].rearrange("p r (j n) -> p r j n", j=4)).then_inc(*bT_ready.up())

            @block.tensor
            def _(pe):
                def prepare(c):
                    pe.wait_ge(b_laid.sem, c + 1)
                    if c:
                        pe.wait_ge(bT_ready.sem, c)
                    for r in range(2):
                        for j in range(4):
                            mm = nc.tensor.transpose(k.ps[:, 4 + r, j * P:(j + 1) * P], bpad[:, r, j, :], k.c("ident"))
                    mm.then_inc(*b_turned.up())
                    pe.wait_ge(bT_ready.sem, c + 1)
                    if c:
                        pe.wait_ge(bu_read.sem, c)
                    for r in range(2):
                        for j in range(4):
                            mm = nc.tensor.matmul(k.ps[:, 2 * r + j // 2, j % 2 * S:j % 2 * S + S], bT[:, r, j, :],
                                                  uT[:, c, :], start=True, stop=True)
                    mm.then_inc(*bu_ready.up())

                def outputs(c):
                    pe.wait_ge(xr_ready.sem, c + 1)
                    pe.wait_ge(xi_ready.sem, c + 1)
                    if c >= 2:
                        pe.wait_ge(y_read.sem, c - 1)
                    for j in range(4):
                        o = k.ps[32 * j:32 * j + 32, 6 + c % 2, 0:S]
                        for r in range(2):
                            mm = nc.tensor.matmul(o, cpad[:, r, 4 * c + j, :], t4[:, r, j, :], start=(r == 0), stop=(r == 1))
                    mm.then_inc(*y_ready.up())

                prepare(0)
                for c in range(DC):
                    if c + 1 < DC:
                        prepare(c + 1)
                    outputs(c)

            flat = lambda ap: ap.rearrange("p a n -> p (a n)")

            @block.vector
            def _(dve):
                link = linker(dve, k.dve_done)
                for c in range(DC):
                    dve.wait_ge(bu_ready.sem, c + 1)
                    br, bi = (flat(k.ps[:, 2 * r:2 * r + 2, :]) for r in range(2))
                    er, ei = flat(e_re[:, 4 * c:4 * c + 4, :]), flat(e_im[:, 4 * c:4 * c + 4, :])
                    zr, zi = flat(z[:, 0]), flat(z[:, 1])
                    if c:
                        dve.wait_ge(xi_ready.sem, c)
                    link(tt(zr, br, er, ALU.mult))
                    link(tt(tmp_v, bi, ei, ALU.mult))
                    link(tt(zr, zr, tmp_v, ALU.add))
                    link(tt(zi, bi, er, ALU.mult))
                    tt(tmp_v, br, ei, ALU.mult).then_inc(*bu_read.up())
                    dve.wait_ge(bu_read.sem, c + 1)
                    link(tt(zi, zi, tmp_v, ALU.subtract))
                    for r in range(2):
                        for j in range(4):
                            V.tensor_tensor_scan(z[:, r, j, :], m["mag"][:, 4 * c + j:4 * c + j + 1].to_broadcast([P, S]),
                                                 z[:, r, j, :], 0.0, ALU.mult, ALU.add).then_inc(*z_ready.up())
                    dve.wait_ge(*z_ready.now())
                    if c:
                        dve.wait_ge(y_ready.sem, c)
                        V.scalar_tensor_tensor(yT[:, c - 1, :], uT[:, c - 1, :], dsk[:, c - 1:c],
                                               k.ps[:, 6 + (c - 1) % 2, 0:S], ALU.mult, ALU.add).then_inc(*y_read.up())
                    xr = flat(t4[:, 0])
                    link(tt(xr, zr, er, ALU.mult))
                    link(tt(tmp_v, zi, ei, ALU.mult))
                    tt(xr, xr, tmp_v, ALU.subtract).then_inc(*xr_ready.up())
                c = DC - 1
                dve.wait_ge(y_ready.sem, DC)
                V.scalar_tensor_tensor(yT[:, c, :], uT[:, c, :], dsk[:, c:c + 1], k.ps[:, 6 + c % 2, 0:S],
                                       ALU.mult, ALU.add).then_inc(*y_read.up())

            @block.gpsimd
            def _(pool):
                link = linker(pool, k.pool_done)
                for c in range(DC):
                    er, ei = flat(e_re[:, 4 * c:4 * c + 4, :]), flat(e_im[:, 4 * c:4 * c + 4, :])
                    zr, zi, xi = flat(z[:, 0]), flat(z[:, 1]), flat(t4[:, 1])
                    pool.wait_ge(z_ready.sem, 8 * (c + 1))
                    if c:
                        pool.wait_ge(y_ready.sem, c)
                    link(nc.gpsimd.tensor_tensor(xi, zi, er, ALU.mult))
                    link(nc.gpsimd.tensor_tensor(tmp_p, zr, ei, ALU.mult))
                    nc.gpsimd.tensor_tensor(xi, xi, tmp_p, ALU.add).then_inc(*xi_ready.up())

        with nc.Block() as block:
            @block.scalar
            def _(act):
                nc.scalar.activation(yT[:], yT[:], ACT.Gelu_apprx_tanh).then_inc(*k.act_done.up())

        def glu(n):
            def run(bank, link):
                b = bank.rearrange("p (c n) -> p c n", c=2)
                return nc.scalar.activation(uT[:, 2 * n:2 * n + 2, :], b, ACT.Sigmoid)
            return run

        gemm(k, [(src, "feat", yT, "s", glu(n)) for n, src in enumerate(columns(I["o_w_glu"], 0, D))])
        with nc.Block() as block:
            @block.vector
            def _(dve):
                tt(uT[:], uT[:], yT[:], ALU.mult).then_inc(*k.dve_done.up())
        add = add_to_x(k, k.gate)
        gemm(k, [(src, "tok", uT, "v", add(n * 256)) for n, src in enumerate(columns(I["o_w_o"], 0, D))])


NE = 8
LIST = 96


def moe(k):
    nc, I = k.nc, k.ins
    V = nc.vector
    with ExitStack() as ctx:
        sb = lambda name, shape, dt=F32: k.sb("moe_" + name, shape, dt, ctx)
        acc = sb("acc", [P, TT, D])
        wr = sb("wr", [P, DC, 8])
        logits = sb("logits", [P, TT, 8])
        top = sb("top", [P, TT, 8])
        idx = sb("idx", [P, TT, 8], U32)
        idf = sb("idf", [P, TT, 8])
        e = sb("e", [P, TT, 1])
        w0 = sb("w0", [P, TT, 1])
        w1 = sb("w1", [P, TT, 1])
        picked = sb("picked", [P, TT, 8])
        gates = sb("gates", [P, TT, NE + 2])
        place = sb("place", [P, TT, NE + 2])
        busy = sb("busy", [P, NE], I32)
        load(k, [(wr[:], I["o_router"].rearrange("(c p) n -> p c n", p=P))])
        with nc.Block() as block:
            @block.tensor
            def _(pe):
                for t in range(TT):
                    for c in range(DC):
                        mm = nc.tensor.matmul(k.ps[:, 0, 8 * t:8 * t + 8], k.hT[:, c, t * P:(t + 1) * P], wr[:, c, :],
                                              start=(c == 0), stop=(c == DC - 1))
                mm.then_inc(*k.pe_done.up())

            @block.vector
            def _(dve):
                def link(ins):
                    ins.then_inc(*k.dve_done.up())
                    dve.wait_ge(*k.dve_done.now())
                dve.wait_ge(*k.pe_done.now())
                link(V.memset(acc[:], 0.0))
                link(V.tensor_copy(logits[:], k.ps[:, 0, 0:16].rearrange("p (t n) -> p t n", t=TT)))
                for t in range(TT):
                    link(V.max(top[:, t, :], logits[:, t, :]))
                    link(V.max_index(idx[:, t, :], top[:, t, :], logits[:, t, :]))
                link(V.tensor_copy(idf[:], idx[:]))
                link(V.tensor_tensor(e[:], top[:, :, 1:2], top[:, :, 0:1], ALU.subtract))

            @block.scalar
            def _(act):
                act.wait_ge(*k.dve_done.now())
                nc.scalar.activation(e[:], e[:], ACT.Exp).then_inc(*k.act_done.up())

            @block.vector
            def _(dve):
                def link(ins):
                    ins.then_inc(*k.dve_done.up())
                    dve.wait_ge(*k.dve_done.now())
                dve.wait_ge(*k.act_done.now())
                link(V.tensor_scalar(w0[:], e[:], 1.0, None, ALU.add))
                link(V.reciprocal(w0[:], w0[:]))
                link(V.tensor_tensor(w1[:], w0[:], e[:], ALU.mult))
                iota = k.c("iota")[:, 0:NE]
                link(V.memset(gates[:], 0.0))
                link(V.memset(place[:], -1.0))
                for t in range(TT):
                    first, second = idf[:, t, 0:1], idf[:, t, 1:2]
                    link(V.tensor_scalar(picked[:, t, :], iota, second, w1[:, t, :], ALU.is_equal, ALU.mult))
                    link(V.tensor_scalar(gates[:, t, 0:NE], iota, first, w0[:, t, :], ALU.is_equal, ALU.mult))
                    link(V.tensor_tensor(gates[:, t, 0:NE], gates[:, t, 0:NE], picked[:, t, :], ALU.add))
                    link(V.tensor_scalar(picked[:, t, :], iota, second, None, ALU.is_equal))
                    link(V.scalar_tensor_tensor(picked[:, t, :], iota, first, picked[:, t, :], ALU.is_equal, ALU.add))

            @block.tensor
            def _(pe):
                pe.wait_ge(*k.dve_done.now())
                ones = k.c("ones")[:, 0:P]
                nc.tensor.matmul(k.ps[:, 1, 0:NE], k.c("upto"), picked[:, 0, :], start=True, stop=True)
                nc.tensor.matmul(k.ps[:, 1, NE:2 * NE], ones, picked[:, 0, :], start=True, stop=False)
                nc.tensor.matmul(k.ps[:, 1, NE:2 * NE], k.c("upto"), picked[:, 1, :], start=False, stop=True)
                nc.tensor.matmul(k.ps[:, 1, 2 * NE:3 * NE], ones, picked[:, 0, :], start=True, stop=False)
                nc.tensor.matmul(k.ps[:, 1, 2 * NE:3 * NE], ones, picked[:, 1, :], start=False, stop=True).then_inc(
                    *k.pe_done.up())

            @block.vector
            def _(dve):
                link = linker(dve, k.dve_done)
                dve.wait_ge(*k.pe_done.now())
                for t in range(TT):
                    link(V.tensor_tensor(place[:, t, 0:NE], picked[:, t, :], k.ps[:, 1, t * NE:(t + 1) * NE], ALU.mult))
                    link(V.tensor_scalar(place[:, t, 0:NE], place[:, t, 0:NE], -1.0, None, ALU.add))
                link(V.tensor_scalar(busy[:], k.ps[:, 1, 2 * NE:3 * NE], float(LIST), None, ALU.is_gt))

        routed_experts(k, I["o_exp_gate"], I["o_exp_up"], I["o_exp_down"], gates, place, busy, acc, ctx)
        add_gated(k, acc, k.gate[:])


def routed_experts(k, w_gate, w_up, w_down, gates, place, busy, acc, ctx):
    nc = k.nc
    V = nc.vector
    sb = lambda name, shape: k.sb("moe_" + name, shape, F32, ctx)
    sg = sb("sg", [P, 2, 2, S])
    prod = sb("prod", [P, 2, 2, S])
    prod_list = sb("prod_list", [P, 2, 2, P])
    h_list = sb("h_list", [P, DC, LIST])
    y_list = sb("y_list", [P, D])
    take = sb("take", [P, TT, LIST])
    give = sb("give", [P, TT, P])
    giveT = sb("giveT", [P, TT, P])
    sem = lambda n: Signal(k.sem("moe_" + n))
    hots_ready, give_turned, list_taken, list_ready, y_kept, spread = map(
        sem, ("hots_ready", "give_turned", "list_taken", "list_ready", "y_kept", "spread"))
    steps = 2 * FF_STEPS
    turns = NE // 2
    wv = {"g": w_gate.rearrange("e (c p) n -> e p c n", p=P), "u": w_up.rearrange("e (c p) n -> e p c n", p=P),
          "d": w_down.rearrange("e (c p) n -> e p c n", p=P)}
    iota = k.c("iota")

    def take_list(bank):
        for c in range(DC):
            o = k.ps[:, bank + c // 4, c % 4 * LIST:(c % 4 + 1) * LIST]
            for t in range(TT):
                mm = nc.tensor.matmul(o, k.h[:, t, c * P:(c + 1) * P], take[:, t, :], start=(t == 0), stop=(t == TT - 1))
        mm.then_inc(list_taken.sem, 1)

    def keep_list(bank):
        nc.scalar.copy(h_list[:].rearrange("p (b c) n -> p b (c n)", b=2),
                       k.ps[:, bank:bank + 2, 0:4 * LIST]).then_inc(list_ready.sem, 1)

    with nc.Block() as block:
        @block.vector
        def _(dve):
            V.memset(prod_list[:], 0.0).then_inc(*spread.up())
            for t in range(TT):
                V.tensor_scalar(take[:, t, :], iota[:, 0:LIST], place[:, t, 0:1], None, ALU.is_equal).then_inc(
                    *k.dve_done.up())

        @block.tensor
        def _(pe):
            pe.wait_ge(*k.dve_done.now())
            take_list(2)
            list_taken.n += 1

        @block.scalar
        def _(act):
            act.wait_ge(*list_taken.now())
            keep_list(2)
            list_ready.n += 1

    up0, silu0, prod0, down0, free0 = (s.n for s in (k.up_ready, k.silu_ready, k.prod_ready, k.down_used, k.y_free))
    land0 = [s.n for s in k.landed]

    with nc.Block() as block:
        @block.sync
        def _(sp):
            with sp.Fori(0, turns) as i:
                def down_weights(n):
                    sp.wait_ge(k.down_used.sem, i * steps + (down0 + n - 1))
                    dst = k.ring[:, 4 + n % 2, :].rearrange("p (c n) -> p c n", c=2)
                    e, s = i * 2 + n // FF_STEPS, n % FF_STEPS
                    sp.dma_start(dst, wv["d"][e, :, 2 * s:2 * s + 2, :]).then_inc(k.landed[4 + n % 2].sem, 16)

                for n in range(steps):
                    e, s = i * 2 + n // FF_STEPS, n % FF_STEPS
                    sp.wait_ge(k.up_ready.sem, i * steps + (up0 + n - 1))
                    for kind, at in (("g", 0), ("u", 2)):
                        dst = k.ring[:, at + n % 2, :].rearrange("p (c n) -> p c n", c=DC)
                        sp.dma_start(dst, wv[kind][e, :, :, s * 256:(s + 1) * 256]).then_inc(
                            k.landed[at + n % 2].sem, 16)
                    if n:
                        down_weights(n - 1)
                down_weights(steps - 1)

        def over_experts(eng, body):
            with eng.Fori(0, turns) as i:
                for q in range(2):
                    long = eng.value_load(busy[0:1, bass.ds(i * 2 + q, 1)], min_val=0, max_val=1)
                    with eng.If(long > 0):
                        body(i, q, False)
                    with eng.Else():
                        body(i, q, True)

        @block.tensor
        def _(pe):
            def body(i, q, short):
                width = LIST if short else S

                def landed(slot, n):
                    pe.wait_ge(k.landed[slot].sem, i * (16 * (steps // 2)) + (land0[slot] + 16 * (n // 2 + 1)))

                def hidden(n):
                    landed(n % 2, n)
                    landed(2 + n % 2, n)
                    pe.wait_ge(k.prod_ready.sem, i * steps + (prod0 + n - 1))
                    for at, b in ((0, 0), (2, 1)):
                        w = k.ring[:, at + n % 2, :].rearrange("p (c n) -> p c n", c=DC)
                        for f in range(2):
                            for c in range(DC):
                                mm = nc.tensor.matmul(k.ps[:, 2 * (n % 2) + b, f * width:(f + 1) * width],
                                                      w[:, c, f * P:(f + 1) * P],
                                                      h_list[:, c, :] if short else k.hT[:, c, :],
                                                      start=(c == 0), stop=(c == DC - 1))
                    mm.then_inc(k.up_ready.sem, 1)

                def down(n):
                    s = n % FF_STEPS
                    landed(4 + n % 2, n)
                    pe.wait_ge(k.prod_ready.sem, i * steps + (prod0 + n + 1))
                    w = k.ring[:, 4 + n % 2, :].rearrange("p (c n) -> p c n", c=2)
                    for t in range(1 if short else TT):
                        for half in range(2):
                            for f in range(2):
                                a = prod_list[:, n % 2, f, :] if short else prod[:, n % 2, f, t * P:(t + 1) * P]
                                mm = nc.tensor.matmul(k.ps[:, 4 + 2 * t + half, :], a,
                                                      w[:, f, half * 512:(half + 1) * 512],
                                                      start=(s == 0 and f == 0), stop=(s == FF_STEPS - 1 and f == 1))
                    mm.then_inc(k.down_used.sem, 1)

                first, last = q * FF_STEPS, (q + 1) * FF_STEPS - 1
                pe.wait_ge(list_ready.sem, i * 2 + (list_ready.n + q))
                hidden(first)
                pe.wait_ge(k.y_free.sem, i * 2 + (free0 + q))
                for n in range(first + 1, last + 1):
                    hidden(n)
                    down(n - 1)
                pe.wait_ge(hots_ready.sem, i * 2 + (q + 1))
                if short:
                    for t in range(TT):
                        mm = nc.tensor.transpose(k.ps[:, 6, t * P:(t + 1) * P], give[:, t, :], k.c("ident"))
                    mm.then_inc(give_turned.sem, 1)
                take_list(2 * (1 - last % 2))
                down(last)
                if short:
                    pe.wait_ge(y_kept.sem, i * 4 + (2 * q + 2))
                    for t in range(TT):
                        for half in range(2):
                            mm = nc.tensor.matmul(k.ps[:, 6 - 2 * t + half, :], giveT[:, t, :],
                                                  y_list[:, half * 512:(half + 1) * 512], start=True, stop=True)
                    mm.then_inc(spread.sem, 1)
                else:
                    pe.sem_inc(give_turned.sem, 1)
                    pe.sem_inc(spread.sem, 1)
            over_experts(pe, body)

        @block.scalar
        def _(act):
            def body(i, q, short):
                width = LIST if short else S
                last = (q + 1) * FF_STEPS - 1
                for n in range(q * FF_STEPS, last + 1):
                    act.wait_ge(k.up_ready.sem, i * steps + (up0 + n + 1))
                    act.wait_ge(k.prod_ready.sem, i * steps + (prod0 + n - 1))
                    nc.scalar.activation(sg[:, n % 2, :, 0:width], k.ps[:, 2 * (n % 2), 0:2 * width].rearrange(
                        "p (f n) -> p f n", f=2), ACT.Silu).then_inc(k.silu_ready.sem, 1)
                if short:
                    act.wait_ge(give_turned.sem, i * 2 + (q + 1))
                    act.wait_ge(spread.sem, i * 2 + (spread.n + q))
                    nc.scalar.copy(giveT[:], k.ps[:, 6, 0:TT * P].rearrange("p (t n) -> p t n", t=TT)).then_inc(
                        y_kept.sem, 1)
                else:
                    act.sem_inc(y_kept.sem, 2)
                act.wait_ge(list_taken.sem, i * 2 + (list_taken.n + q + 1))
                keep_list(2 * (1 - last % 2))
                if short:
                    act.wait_ge(k.down_used.sem, i * steps + (down0 + last + 1))
                    nc.scalar.copy(y_list[:].rearrange("p (b n) -> p b n", b=2), k.ps[:, 4:6, :]).then_inc(y_kept.sem, 1)
            over_experts(act, body)

        @block.vector
        def _(dve):
            def body(i, q, short):
                width = LIST if short else S
                first, last = q * FF_STEPS, (q + 1) * FF_STEPS - 1
                for n in range(first, last + 1):
                    dve.wait_ge(k.silu_ready.sem, i * steps + (silu0 + n + 1))
                    dve.wait_ge(k.down_used.sem, i * steps + (down0 + n - 1))
                    V.tensor_tensor(prod_list[:, n % 2, :, 0:LIST] if short else prod[:, n % 2],
                                    sg[:, n % 2, :, 0:width],
                                    k.ps[:, 2 * (n % 2) + 1, 0:2 * width].rearrange("p (f n) -> p f n", f=2),
                                    ALU.mult).then_inc(k.prod_ready.sem, 1)
                    if n == first:
                        dve.wait_ge(list_taken.sem, i * 2 + (list_taken.n + q))
                        for t in range(TT):
                            V.tensor_scalar(give[:, t, :], iota, place[:, t, bass.ds(i * 2 + q, 1)],
                                            gates[:, t, bass.ds(i * 2 + q, 1)], ALU.is_equal, ALU.mult)
                            ins = V.tensor_scalar(take[:, t, :], iota[:, 0:LIST],
                                                  place[:, t, bass.ds(i * 2 + (q + 1), 1)], None, ALU.is_equal)
                        ins.then_inc(hots_ready.sem, 1)
                dve.wait_ge(k.down_used.sem, i * steps + (down0 + last + 1))
                if short:
                    dve.wait_ge(spread.sem, i * 2 + (spread.n + q + 1))
                for t in range(TT):
                    for half in range(2):
                        a = acc[:, t, half * 512:(half + 1) * 512]
                        if short:
                            ins = V.tensor_tensor(a, k.ps[:, 6 - 2 * t + half, :], a, ALU.add)
                        else:
                            ins = V.scalar_tensor_tensor(a, k.ps[:, 4 + 2 * t + half, :],
                                                         gates[:, t, bass.ds(i * 2 + q, 1)], a, ALU.mult, ALU.add)
                ins.then_inc(k.y_free.sem, 1)
            over_experts(dve, body)

    for s in (k.up_ready, k.silu_ready, k.prod_ready, k.down_used):
        s.n += NE * FF_STEPS
    k.y_free.n += NE
    for s in k.landed:
        s.n += 16 * turns * FF_STEPS
    k.job += (-k.job) % NSLOT


def final_norm(k):
    with ExitStack() as ctx:
        sq = k.sb("fin_sq", [P, TT, D], ctx=ctx)
        load(k, [(k.gain[:], k.ins["final_norm"].partition_broadcast(P))])
        norm_modulate(k, k.x, k.gain[:], None, k.x, None, sq)


LAM_INIT = 0.8 - 0.6 * math.exp(-0.3 * 0)
W_Q, W_K, W_V, W_Z, W_G = 0, D, 2 * D, 3 * D, 3 * D + 3328


def linker(eng, done):
    def link(ins):
        ins.then_inc(*done.up())
        eng.wait_ge(*done.now())
    return link


def hybrid_mixer(k):
    nc, I = k.nc, k.ins
    with ExitStack() as ctx:
        sb = lambda name, shape, dt=F32: k.sb("hy_" + name, shape, dt, ctx)
        oaT = sb("oaT", [P, DC, S])
        obT = sb("obT", [P, DC, S])
        hcT = obT
        with ExitStack() as c2:
            gain_c = k.sb("gain_c", [P, D], ctx=c2)
            shift_c = k.sb("shift_c", [P, D], ctx=c2)
            ctxt = k.sb("ctxt", [P, TT, D], ctx=c2)
            sq = k.sb("hy_sq", [P, TT, D], ctx=c2)
            adaln_rows(k, [I["c_2"], I["c_ctx_2"]], I["w_mod_2"], I["b_mod_2"], I["norm1_g_2"],
                       [(0, [("shift", k.shift), ("shift", shift_c)]), (1, [("gain", k.gain), ("gain", gain_c)]),
                        (2, [("gate", k.gate)])], c2, "mod2a")
            load(k, [(ctxt[:], I["ctx_2"].rearrange("(t p) d -> p t d", p=P))])
            norm_modulate(k, ctxt, gain_c[:], shift_c[:], ctxt, hcT, sq)
            norm_modulate(k, k.x, k.gain[:], k.shift[:], k.h, k.hT, sq)
        diff_branch(k, hcT, oaT)
        rwkv_branch(k, hcT, obT)

        ga = sb("ga", [P, DC, S])
        gb = sb("gb", [P, DC, S])
        tmp = sb("tmp", [P, 2, S])

        def sig(dst, n):
            return lambda bank, link: nc.scalar.activation(dst[:, 2 * n:2 * n + 2, :],
                                                           bank.rearrange("p (c n) -> p c n", c=2), ACT.Sigmoid)

        W = I["w_in_2"]
        gemm(k, [(src, "feat", k.hT, "s", sig(dst, n)) for at, dst in ((W_G, ga), (W_G + D, gb))
                 for n, src in enumerate(columns(W, at, at + D))])

        def gated(n, g, add):
            def run(bank, link):
                b, o = bank.rearrange("p (c n) -> p c n", c=2), ga[:, 2 * n:2 * n + 2, :]
                if not add:
                    return nc.vector.tensor_tensor(o, b, o, ALU.mult)
                link(nc.vector.tensor_tensor(tmp[:], b, g[:, 2 * n:2 * n + 2, :], ALU.mult))
                return nc.vector.tensor_tensor(o, o, tmp[:], ALU.add)
            return run

        gemm(k, [(src, "feat", o, "v", gated(n, g, add))
                 for w, o, g, add in (("w_branch_a_2", oaT, ga, False), ("w_branch_b_2", obT, gb, True))
                 for n, src in enumerate(columns(I[w], 0, D))])
        add = add_to_x(k, k.gate)
        gemm(k, [(src, "tok", ga, "v", add(n * 256)) for n, src in enumerate(columns(I["w_out_2"], 0, D))])


def diff_branch(k, hcT, oaT):
    nc, I = k.nc, k.ins
    V = nc.vector
    H = 8
    with ExitStack() as ctx:
        sb = lambda name, shape, dt=F32: k.sb("da_" + name, shape, dt, ctx)
        q = sb("q", [P, TT, D])
        kx = sb("kx", [P, 4, D])
        v = sb("v", [P, 4, D])
        gq = sb("gq", [P, 64])
        gk = sb("gk", [P, 64])
        lam4 = sb("lam4", [P, 4, 64])
        lam = sb("lam", [P, 4])
        og = sb("og", [P, P])
        ss = sb("ss", [P, 32])
        ctx2 = ExitStack()
        sq = k.sb("da_sq", [P, 2, D], ctx=ctx2)
        load(k, [(gq[:], I["q_norm_g_2"].partition_broadcast(P)), (gk[:], I["k_norm_g_2"].partition_broadcast(P)),
                 (lam4[:], I["diff_lambda_2"].partition_broadcast(P)), (og[:], I["diff_out_g_2"].partition_broadcast(P))])
        W = I["w_in_2"]
        jobs = []
        for n, src in enumerate(columns(W, W_Q, W_Q + D)):
            jobs.append((src, "tok", k.hT, "v" if n % 2 else "s", copy_tok(k, q, n * 256, "v" if n % 2 else "s")))
        for at, dst in ((W_K, kx), (W_V, v)):
            for n, src in enumerate(columns(W, at, at + D)):
                jobs.append((src, "tok", k.hT, "v", copy_tok(k, dst[:, 2:4], n * 256, "v")))
                jobs.append((None, "tok", hcT, "s", copy_tok(k, dst[:, 0:2], n * 256, "s")))
        gemm(k, jobs)

        def head_norm(buf, g, n, width):
            groups = TT * D // width
            view = buf.rearrange("p t (g n) -> p (t g) n", n=width)
            with nc.Block() as block:
                @block.scalar
                def _(act):
                    nc.scalar.activation(sq[:], buf, ACT.Square).then_inc(*k.act_done.up())

                @block.vector
                def _(dve):
                    link = linker(dve, k.dve_done)
                    dve.wait_ge(*k.act_done.now())
                    link(V.tensor_reduce(ss[:, 0:groups], sq[:].rearrange("p t (g n) -> p (t g) n", n=width), AX.X, ALU.add))
                    link(V.tensor_scalar(ss[:, 0:groups], ss[:, 0:groups], 1.0 / width, EPS, ALU.mult, ALU.add))

                @block.scalar
                def _(act):
                    act.wait_ge(*k.dve_done.now())
                    nc.scalar.activation(ss[:, 0:groups], ss[:, 0:groups], ACT.Sqrt).then_inc(*k.act_done.up())

                @block.vector
                def _(dve):
                    link = linker(dve, k.dve_done)
                    dve.wait_ge(*k.act_done.now())
                    link(V.reciprocal(ss[:, 0:groups], ss[:, 0:groups]))
                    link(V.tensor_tensor(view, view, ss[:, 0:groups].unsqueeze(2).to_broadcast([P, groups, width]), ALU.mult))
                    link(V.tensor_tensor(view, view, g.unsqueeze(1).to_broadcast([P, groups, width]), ALU.mult))

        head_norm(q[:], gq[:], 64, 64)
        head_norm(kx[:, 0:2], gk[:], 64, 64)
        head_norm(kx[:, 2:4], gk[:], 64, 64)

        with nc.Block() as block:
            @block.vector
            def _(dve):
                link = linker(dve, k.dve_done)
                s4 = sq[:].rearrange("p t n -> p (t n)")
                s = [s4[:, i * 512:(i + 1) * 512].rearrange("p (g a f) -> p g a f", g=16, a=2) for i in range(4)]
                for buf, tiles in ((q, 0), (kx, 2)):
                    for t in range(TT):
                        xs = buf[:, tiles + t, :].rearrange("p (g a h f) -> p g a h f", g=16, a=2, h=2)
                        x1, x2 = xs[:, :, :, 0, :], xs[:, :, :, 1, :]
                        cos, sin = (k.c(n)[:, t * 32:(t + 1) * 32].rearrange("p (a f) -> p a f", a=2).unsqueeze(1)
                                    .to_broadcast([P, 16, 2, 16]) for n in ("rope_cos", "rope_sin"))
                        for o, x, cs in ((s[0], x1, cos), (s[1], x2, sin), (s[2], x2, cos), (s[3], x1, sin)):
                            link(V.tensor_tensor(o, x, cs, ALU.mult))
                        link(V.tensor_tensor(x1, s[0], s[1], ALU.subtract))
                        link(V.tensor_tensor(x2, s[2], s[3], ALU.add))
                link(V.tensor_tensor(lam4[:, 0, :], lam4[:, 0, :], lam4[:, 1, :], ALU.mult))
                link(V.tensor_tensor(lam4[:, 2, :], lam4[:, 2, :], lam4[:, 3, :], ALU.mult))
                link(V.tensor_reduce(lam[:, 0:1], lam4[:, 0, :], AX.X, ALU.add))
                link(V.tensor_reduce(lam[:, 1:2], lam4[:, 2, :], AX.X, ALU.add))

            @block.scalar
            def _(act):
                act.wait_ge(*k.dve_done.now())
                nc.scalar.activation(lam[:, 0:2], lam[:, 0:2], ACT.Exp).then_inc(*k.act_done.up())

            @block.vector
            def _(dve):
                link = linker(dve, k.dve_done)
                dve.wait_ge(*k.act_done.now())
                link(V.tensor_tensor(lam[:, 2:3], lam[:, 1:2], lam[:, 0:1], ALU.subtract))
                link(V.tensor_scalar(lam[:, 2:3], lam[:, 2:3], -LAM_INIT, None, ALU.add))
        ctx2.close()

        qT = sb("qT", [P, H, 2, S])
        kT = k.h[:].rearrange("p t n -> p (t n)")
        kT2 = sb("kT2", [P, 4, 512])
        kT_of = lambda h: (kT.rearrange("p (h n) -> p h n", h=4) if h < 4 else kT2[:])[:, h % 4, :]
        e = sb("e", [P, 2, 2, 512])
        pd = sb("pd", [P, 2, 512])
        pdT = sb("pdT", [P, 2, 512])
        st = sb("st", [P, 2, 2, 2])
        o = q
        sem = lambda n: Signal(k.sem("da_" + n))
        scores_ready, maxed, exps_ready, diffed, turned, turned_copied, out_ready, out_copied = map(
            sem, ("scores", "maxed", "exps", "diffed", "turned", "turned_copied", "out", "out_copied"))
        with nc.Block() as block:
            @block.vector
            def _(dve):
                V.memset(qT[:], 0.0).then_inc(*k.dve_done.up())

            @block.tensor
            def _(pe):
                for b in range(4):
                    for i in range(4):
                        h, t = 2 * b + i // 2, i % 2
                        mm = nc.tensor.transpose(k.ps[:, b, i * P:(i + 1) * P], q[:, t, h * P:(h + 1) * P], k.c("ident"))
                mm.then_inc(*k.pe_done.up())
                for b in range(4):
                    for t in range(4):
                        mm = nc.tensor.transpose(k.ps[:, 4 + b, t * P:(t + 1) * P], kx[:, t, b * P:(b + 1) * P], k.c("ident"))
                mm.then_inc(*k.pe_done.up())

            @block.vector
            def _(dve):
                dve.wait_ge(k.dve_done.sem, k.dve_done.n)
                dve.wait_ge(k.pe_done.sem, k.pe_done.n - 1)
                for b in range(4):
                    for m in range(2):
                        r = slice(64 * m, 64 * m + 64)
                        V.tensor_copy(qT[r, 2 * b:2 * b + 2, m, :],
                                      k.ps[r, b, :].rearrange("p (h n) -> p h n", h=2)).then_inc(*k.dve_done.up())
                dve.wait_ge(*k.pe_done.now())
                for b in range(4):
                    V.tensor_copy(kT_of(b), k.ps[:, 4 + b, :]).then_inc(*k.dve_done.up())

            @block.tensor
            def _(pe):
                pe.wait_ge(*k.dve_done.now())
                for b in range(4):
                    for t in range(4):
                        mm = nc.tensor.transpose(k.ps[:, b, t * P:(t + 1) * P], kx[:, t, (4 + b) * P:(5 + b) * P],
                                                 k.c("ident"))
                mm.then_inc(*k.pe_done.up())

            @block.vector
            def _(dve):
                dve.wait_ge(*k.pe_done.now())
                for b in range(4):
                    V.tensor_copy(kT_of(4 + b), k.ps[:, b, :]).then_inc(*k.dve_done.up())

        N = H * TT
        with nc.Block() as block:
            @block.tensor
            def _(pe):
                def scores(i):
                    h, t = i // 2, i % 2
                    if i >= 2:
                        pe.wait_ge(exps_ready.sem, i - 1)
                    for m in range(2):
                        mm = nc.tensor.matmul(k.ps[:, 2 * (i % 2) + m, :], qT[:, h, m, t * P:(t + 1) * P], kT_of(h),
                                              start=True, stop=True)
                    mm.then_inc(*scores_ready.up())

                def turn(i):
                    pe.wait_ge(diffed.sem, i + 1)
                    if i >= 2:
                        pe.wait_ge(turned_copied.sem, i - 1)
                    for c in range(4):
                        mm = nc.tensor.transpose(k.ps[:, 4 + i % 2, c * P:(c + 1) * P], pd[:, i % 2, c * P:(c + 1) * P],
                                                 k.c("ident"))
                    mm.then_inc(*turned.up())

                def values(i):
                    h = i // 2
                    pe.wait_ge(turned_copied.sem, i + 1)
                    if i >= 2:
                        pe.wait_ge(out_copied.sem, i - 1)
                    for c in range(4):
                        mm = nc.tensor.matmul(k.ps[:, 6 + i % 2, 0:P], pdT[:, i % 2, c * P:(c + 1) * P],
                                              v[:, c, h * P:(h + 1) * P], start=(c == 0), stop=(c == 3))
                    mm.then_inc(*out_ready.up())

                for i in range(N + 2):
                    if i < N:
                        scores(i)
                    if 1 <= i <= N:
                        turn(i - 1)
                    if i >= 2:
                        values(i - 2)

            @block.vector
            def _(dve):
                link = linker(dve, k.dve_done)

                def maxima(i):
                    dve.wait_ge(scores_ready.sem, i + 1)
                    for m in range(2):
                        link(V.tensor_reduce(st[:, i % 2, 0, m:m + 1], k.ps[:, 2 * (i % 2) + m, :], AX.X, ALU.max))
                    V.tensor_scalar(st[:, i % 2, 0, :], st[:, i % 2, 0, :], -0.125, None, ALU.mult).then_inc(*maxed.up())

                def difference(i):
                    dve.wait_ge(exps_ready.sem, i + 1)
                    if i >= 2:
                        dve.wait_ge(turned.sem, i - 1)
                    link(V.reciprocal(st[:, i % 2, 1, :], st[:, i % 2, 1, :]))
                    link(V.tensor_tensor(st[:, i % 2, 1, 1:2], st[:, i % 2, 1, 1:2], lam[:, 2:3], ALU.mult))
                    link(V.tensor_scalar(pd[:, i % 2, :], e[:, i % 2, 0, :], st[:, i % 2, 1, 0:1], None, ALU.mult))
                    V.scalar_tensor_tensor(pd[:, i % 2, :], e[:, i % 2, 1, :], st[:, i % 2, 1, 1:2], pd[:, i % 2, :],
                                           ALU.mult, ALU.add).then_inc(*diffed.up())

                def copy_out(i):
                    h, t = i // 2, i % 2
                    dve.wait_ge(out_ready.sem, i + 1)
                    V.tensor_copy(o[:, t, h * P:(h + 1) * P], k.ps[:, 6 + i % 2, 0:P]).then_inc(*out_copied.up())

                for i in range(N + 2):
                    if i < N:
                        maxima(i)
                    if 1 <= i <= N:
                        difference(i - 1)
                    if i >= 2:
                        copy_out(i - 2)

            @block.scalar
            def _(act):
                def exps(i):
                    act.wait_ge(maxed.sem, i + 1)
                    if i >= 2:
                        act.wait_ge(diffed.sem, i - 1)
                    for m in range(2):
                        nc.scalar.activation(e[:, i % 2, m, :], k.ps[:, 2 * (i % 2) + m, :], ACT.Exp,
                                             bias=st[:, i % 2, 0, m:m + 1], scale=0.125,
                                             accum_out=st[:, i % 2, 1, m:m + 1]).then_inc(
                                                 *(exps_ready.up() if m else k.act_done.up()))

                def copy_turned(i):
                    act.wait_ge(turned.sem, i + 1)
                    if i >= 2:
                        act.wait_ge(out_ready.sem, i - 1)
                    nc.scalar.copy(pdT[:, i % 2, :], k.ps[:, 4 + i % 2, :]).then_inc(*turned_copied.up())

                for i in range(N + 1):
                    if i < N:
                        exps(i)
                    if i >= 1:
                        copy_turned(i - 1)

        sq = kx[:, 0:2]
        head_norm(o[:], og[:], 128, 128)
        with nc.Block() as block:
            @block.vector
            def _(dve):
                link = linker(dve, k.dve_done)
                link(V.tensor_scalar(o[:], o[:], 1.0 - LAM_INIT, None, ALU.mult))
            transpose_tokens(k, o, oaT, k.dve_done.now(), block)


ROW_KK, ROW_KA, ROW_RK, ROW_G, ROW_B, ROW_W0, ROW_A0 = 0, 1, 2, 3, 4, 5, 7
L2_EPS = 1e-12
RW_LN_EPS = 64e-5
LOG_DECAY = -math.exp(-0.5)


def rwkv_branch(k, hcT, obT):
    nc, I = k.nc, k.ins
    V, G = nc.vector, nc.gpsimd
    with ExitStack() as ctx:
        sb = lambda name, shape, dt=F32: k.sb("rw_" + name, shape, dt, ctx)
        zx = sb("zx", [P, 26, S])
        zc = sb("zc", [P, 17, S])
        kk = {"c": sb("kkc", [P, DC, S]), "x": sb("kkx", [P, DC, S])}
        zl = {s: sb("zl" + s, [P, 2, S]) for s in "cx"}
        y = sb("y", [P, DC, 4, C64])
        shw = sb("shw", [P, 3, 26])
        rows = sb("rows", [P, 9, DC])
        ka1 = sb("ka1", [P, DC])
        lora = [k.gain, k.shift]
        load(k, [(shw[:], I["rw_shift_2"]), (rows[:], I["rw_rows"]), (lora[0][:], I["rw_lora"][:, 0, :]),
                 (lora[1][:], I["rw_lora"][:, 1, :])])

        def shifted(dst, at, chunk, n):
            def run(bank, link):
                for i in range(n):
                    b, o, c = bank[:, i * S:(i + 1) * S], dst[:, at + i, :], chunk + i
                    link(V.tensor_scalar(o, b, shw[:, 1, c:c + 1], None, ALU.mult))
                    link(V.scalar_tensor_tensor(o[:, 1:S], b[:, 0:S - 1], shw[:, 0, c:c + 1], o[:, 1:S], ALU.mult, ALU.add))
                    ins = V.scalar_tensor_tensor(o[:, 0:S - 1], b[:, 1:S], shw[:, 2, c:c + 1], o[:, 0:S - 1],
                                                 ALU.mult, ALU.add)
                    if i < n - 1:
                        link(ins)
                return ins
            return run

        jobs = []
        for n, src in enumerate(columns(I["w_in_2"], W_Z, W_Z + 3328)):
            jobs.append((src, "feat", k.hT, "v", shifted(zx, 2 * n, 2 * n, 2)))
            if 4 <= n < 12:
                jobs.append((None, "feat", hcT, "v", shifted(zc, 2 * n - 8, 2 * n, 2)))
            elif n == 12:
                jobs.append((None, "feat", hcT, "v", shifted(zc, 16, 24, 1)))
        gemm(k, jobs)

        ring = k.ring[:].rearrange("p a n -> p (a n)")
        keys = {"c": zc[:, 0:8], "x": zx[:, 8:16]}
        vals = {"c": zc[:, 8:16], "x": zx[:, 16:24]}
        two = lambda n: ring[:, n * 2048:(n + 1) * 2048].rearrange("p (c n) -> p c n", c=DC)
        wide = lambda ap: ap.to_broadcast([P, DC, S])

        with nc.Block() as block:
            @block.vector
            def _(dve):
                for s in "cx":
                    V.memset(zl[s][:], 0.0).then_inc(*k.dve_done.up())
                V.tensor_scalar(ka1[:], rows[:, ROW_KA, :], -1.0, 1.0, ALU.mult, ALU.add).then_inc(*k.dve_done.up())
                dve.wait_ge(*k.dve_done.now())
                for s in "cx":
                    V.tensor_tensor(kk[s][:], keys[s], wide(rows[:, ROW_KK, :].unsqueeze(2)), ALU.mult).then_inc(
                        *k.dve_done.up())

            @block.scalar
            def _(act):
                act.wait_ge(*k.dve_done.now())
                for s, z in (("c", zc[:, 16]), ("x", zx[:, 24])):
                    nc.scalar.activation(zl[s][0:64, 0, :], z[0:64], ACT.Tanh).then_inc(*k.act_done.up())
                    nc.scalar.copy(zl[s][64:128, 1, :], z[64:128]).then_inc(*k.act_done.up())
                for i, s in enumerate("cx"):
                    nc.scalar.activation(two(i), kk[s][:], ACT.Square).then_inc(*k.act_done.up())

            @block.tensor
            def _(pe):
                pe.wait_ge(*k.act_done.now())
                for i in range(2):
                    for b in range(4):
                        mm = nc.tensor.matmul(k.ps[:, 4 * i + b, :], k.c("head_ones"),
                                              two(i)[:, 2 * b:2 * b + 2, :].rearrange("p c n -> p (c n)"),
                                              start=True, stop=True)
                mm.then_inc(*k.pe_done.up())

            @block.vector
            def _(dve):
                dve.wait_ge(*k.pe_done.now())
                for i in range(2):
                    V.tensor_scalar(two(i), k.ps[:, 4 * i:4 * i + 4, :].rearrange("p b (c n) -> p (b c) n", c=2),
                                    L2_EPS, None, ALU.add).then_inc(*k.dve_done.up())

            @block.scalar
            def _(act):
                act.wait_ge(*k.dve_done.now())
                nc.scalar.activation(ring[:, 0:4096], ring[:, 0:4096], ACT.Sqrt).then_inc(*k.act_done.up())

            @block.vector
            def _(dve):
                link = linker(dve, k.dve_done)
                dve.wait_ge(*k.act_done.now())
                link(V.reciprocal(ring[:, 0:4096], ring[:, 0:4096]))
                for i, s in enumerate("cx"):
                    link(V.tensor_tensor(kk[s][:], kk[s][:], two(i), ALU.mult))

        class Lane:
            pass
        lanes = []
        for d in range(2):
            n = Lane()
            n.d = d
            n.pe, n.dve, n.act, n.pool = (Signal(k.sem(f"rw{d}_{e}")) for e in ("pe", "dve", "act", "pool"))
            at = [d * 6144, d * 1024]

            def cut(*shape, where=0):
                size = int(np.prod(shape))
                src = (ring, k.h[:].rearrange("p t n -> p (t n)"))[where]
                ap = src[:, at[where]:at[where] + size]
                at[where] += size
                if len(shape) == 2:
                    return ap.rearrange("p (a n) -> p a n", a=shape[0])
                return ap.rearrange("p (a b n) -> p a b n", a=shape[0], b=shape[1])

            n.ep, n.en, n.ak, n.ke = (cut(2, S) for _ in range(4))
            n.ar = cut(2, 2, P)
            n.b, n.kb, n.v = (cut(2, P) for _ in range(3))
            n.lt, n.mt, n.rbt, n.rkt = (cut(2, P) for _ in range(4))
            n.xx = cut(2, 2, P)
            n.p = cut(2, P)
            n.bst, n.kst = cut(2, P), cut(2, P)
            n.off = [cut(2, P), cut(2, P, where=1)]
            n.state, n.vst, n.g, n.u = (cut(2, C64, where=1) for _ in range(4))
            n.bank = lambda b, d=d: k.ps[:, 4 * d + b, :]
            n.scan = (lambda ap: ap) if d == 0 else (lambda ap: ap[:, :, ::-1])
            lanes.append(n)

        b2 = lambda ap: ap.unsqueeze(1).to_broadcast([P, 2, P])
        halves = [slice(0, 64), slice(64, 128)]

        def each(step):
            for n in lanes:
                step(n)

        for q in range(4):
            with nc.Block() as block:
                def start(n):
                    @block.gpsimd
                    def _(pool):
                        if q == 0:
                            for t in (n.ar, n.b, n.kb, n.v):
                                linker(pool, n.pool)(G.memset(t, 0.0))
                        linker(pool, n.pool)(G.memset(n.state, 0.0))
                each(start)

                for s in "cx":
                    pr = slice(2 * q, 2 * q + 2)

                    def prep_pe(n):
                        @block.tensor
                        def _(pe):
                            pe.wait_ge(*n.dve.now())
                            pe.wait_ge(*n.act.now())
                            for b in range(2):
                                for i in range(2):
                                    col = (2 * q + i) * P
                                    mm = nc.tensor.matmul(n.bank(b)[:, i * S:(i + 1) * S], lora[n.d][:, col:col + P],
                                                          zl[s][:, b, :], start=True, stop=True)
                            mm.then_inc(*n.pe.up())

                    def prep_act(n):
                        @block.scalar
                        def _(act):
                            act.wait_ge(*n.pe.now())
                            act.wait_ge(*n.dve.now())
                            act.wait_ge(*n.pool.now())
                            for b, dst, row in ((0, n.en, ROW_W0 + n.d), (1, n.ak, ROW_A0 + n.d)):
                                for i in range(2):
                                    o = dst[:, i:i + 1, :]
                                    nc.scalar.activation(n.scan(o), n.bank(b)[:, i * S:(i + 1) * S].unsqueeze(1),
                                                         ACT.Sigmoid,
                                                         bias=rows[:, row, 2 * q + i:2 * q + i + 1]).then_inc(*n.act.up())

                    def prep_dve(n):
                        @block.vector
                        def _(dve):
                            link = linker(dve, n.dve)
                            dve.wait_ge(*n.act.now())
                            flat = lambda ap: ap.rearrange("p a n -> p (a n)")
                            link(V.tensor_scalar(n.en, n.en, LOG_DECAY, None, ALU.mult))
                            link(V.tensor_tensor_scan(flat(n.ep), k.c("reset"), flat(n.en), 0.0, ALU.mult, ALU.add))
                            for i in range(2):
                                link(V.tensor_scalar(n.ke[:, i, :], n.ak[:, i, :], rows[:, ROW_KA, 2 * q + i:2 * q + i + 1],
                                                     ka1[:, 2 * q + i:2 * q + i + 1], ALU.mult, ALU.add))
                            link(V.tensor_tensor(n.ke, n.ke, n.scan(keys[s][:, pr, :]), ALU.mult))
                            link(V.tensor_tensor(n.ak, n.ak, n.scan(kk[s][:, pr, :]), ALU.mult))

                    def prep_exp(n):
                        @block.scalar
                        def _(act):
                            act.wait_ge(*n.dve.now())
                            nc.scalar.activation(n.en, n.ep, ACT.Exp, scale=-1.0).then_inc(*n.act.up())
                            act.wait_ge(*n.act.now())
                            nc.scalar.activation(n.ep, n.ep, ACT.Exp).then_inc(*n.act.up())

                    for step in (prep_pe, prep_act, prep_dve, prep_exp):
                        each(step)

                    for c in range(4):
                        def here(n, ap):
                            r = c if n.d == 0 else 3 - c
                            return n.scan(ap[:, :, r * C64:(r + 1) * C64])

                        at = slice(c * C64, (c + 1) * C64)
                        wanted = s == "x"

                        def build(n):
                            @block.vector
                            def _(dve):
                                dve.wait_ge(*n.act.now())
                                dve.wait_ge(*n.pe.now())
                                dve.wait_ge(*n.pool.now())
                                kk_h = here(n, kk[s][:, pr, :])
                                for hh, r in enumerate(halves):
                                    o = slice(64 * hh, 64 * hh + 64)
                                    V.tensor_copy(n.ar[r, :, 0, 64 * hh:64 * hh + 1], kk_h[r, :, 0:1]).then_inc(*n.dve.up())
                                    V.tensor_tensor(n.ar[r, :, 0, 64 * hh + 1:64 * hh + 64], kk_h[r, :, 1:C64],
                                                    n.ep[r, :, c * C64:c * C64 + C64 - 1], ALU.mult).then_inc(*n.dve.up())
                                    V.tensor_tensor(n.b[r, :, o], n.ak[r, :, at], n.en[r, :, at], ALU.mult).then_inc(
                                        *n.dve.up())
                                    if wanted:
                                        rc = c if n.d == 0 else 3 - c
                                        V.tensor_tensor(n.ar[r, :, 1, o], zx[r, pr, rc * C64:(rc + 1) * C64],
                                                        n.scan(n.ep[r, :, at]), ALU.mult).then_inc(*n.dve.up())

                            @block.gpsimd
                            def _(pool):
                                pool.wait_ge(*n.act.now())
                                pool.wait_ge(*n.pe.now())
                                v_h = here(n, vals[s][:, pr, :])
                                for hh, r in enumerate(halves):
                                    o = slice(64 * hh, 64 * hh + 64)
                                    linker(pool, n.pool)(G.tensor_tensor(n.kb[r, :, o], n.ke[r, :, at], n.en[r, :, at], ALU.mult))
                                    linker(pool, n.pool)(G.tensor_copy(n.v[r, :, o], v_h[r]))

                        def products(n):
                            @block.tensor
                            def _(pe):
                                pe.wait_ge(*n.dve.now())
                                pe.wait_ge(*n.pool.now())
                                w = 2 * P if wanted else P
                                for b, t in ((0, n.b), (1, n.kb)):
                                    for i in range(2):
                                        nc.tensor.matmul(n.bank(b)[:, i * 256:i * 256 + w], t[:, i, :],
                                                         n.ar[:, i, :, :].rearrange("p a n -> p (a n)")[:, 0:w],
                                                         start=True, stop=True)
                                for i in range(2):
                                    nc.tensor.matmul(n.bank(2)[:, i * C64:(i + 1) * C64], n.v[:, i, :], k.c("fold"),
                                                     start=True, stop=True)
                                for j, t in enumerate((n.b, n.kb)):
                                    for i in range(2):
                                        mm = nc.tensor.transpose(n.bank(3)[:, (2 * j + i) * P:(2 * j + i + 1) * P],
                                                                 t[:, i, :], k.c("ident"))
                                mm.then_inc(*n.pe.up())

                        def masks(n):
                            @block.vector
                            def _(dve):
                                link = linker(dve, n.dve)
                                dve.wait_ge(*n.pe.now())
                                dve.wait_ge(*n.pool.now())
                                bb, kb = (n.bank(b).rearrange("p (i w n) -> p i w n", i=2, w=2) for b in range(2))
                                incl = b2(k.c("incl" if n.d == 0 else "incl_rev"))
                                link(V.tensor_tensor(n.lt, bb[:, :, 0, :], b2(k.c("strict")), ALU.mult))
                                link(V.tensor_tensor(n.off[0], n.lt, b2(k.c("level0")), ALU.mult))
                                link(V.tensor_tensor(n.xx[:, 1], b2(k.c("ident")), n.off[0], ALU.subtract))
                                V.tensor_tensor(n.mt, kb[:, :, 0, :], b2(k.c("strict")), ALU.mult).then_inc(*n.dve.up())
                                if wanted:
                                    V.tensor_tensor(n.rbt, bb[:, :, 1, :], incl, ALU.mult).then_inc(*n.dve.up())
                                    V.tensor_tensor(n.rkt, kb[:, :, 1, :], incl, ALU.mult).then_inc(*n.dve.up())

                            @block.scalar
                            def _(act):
                                act.wait_ge(*n.pe.now())
                                nc.scalar.copy(n.vst, n.bank(2)[:, 0:2 * C64].rearrange("p (i n) -> p i n", i=2)).then_inc(
                                    *n.act.up())
                                for j, t in enumerate((n.bst, n.kst)):
                                    nc.scalar.copy(t, n.bank(3)[:, 2 * j * P:2 * (j + 1) * P].rearrange(
                                        "p (i n) -> p i n", i=2)).then_inc(*n.act.up())

                        def turn_x(n):
                            @block.tensor
                            def _(pe):
                                pe.wait_ge(*n.dve.now())
                                pe.wait_ge(*n.act.now())
                                for i in range(2):
                                    mm = nc.tensor.transpose(n.bank(2)[:, i * P:(i + 1) * P], n.xx[:, 1, i, :], k.c("ident"))
                                mm.then_inc(*n.pe.up())

                            @block.gpsimd
                            def _(pool):
                                pool.wait_ge(*n.dve.now())
                                linker(pool, n.pool)(G.tensor_tensor(n.off[1], n.lt, b2(k.c("level1")), ALU.mult))

                        def copy_x(n):
                            @block.scalar
                            def _(act):
                                act.wait_ge(*n.pe.now())
                                nc.scalar.copy(n.xx[:, 0], n.bank(2)[:, 0:2 * P].rearrange("p (i n) -> p i n", i=2)).then_inc(
                                    *n.act.up())

                        for step in (build, products, masks, turn_x, copy_x):
                            each(step)

                        for level in range(1, 6):
                            last = level == 5

                            def off_x(n):
                                @block.tensor
                                def _(pe):
                                    pe.wait_ge(*n.act.now())
                                    pe.wait_ge(*n.dve.now())
                                    pe.wait_ge(*n.pool.now())
                                    for i in range(2):
                                        mm = nc.tensor.matmul(n.bank(2)[:, i * P:(i + 1) * P], n.off[level % 2][:, i, :],
                                                              n.xx[:, 0, i, :], start=True, stop=True)
                                    mm.then_inc(*n.pe.up())

                                @block.scalar
                                def _(act):
                                    act.wait_ge(*n.pe.now())
                                    nc.scalar.copy(n.p, n.bank(2)[:, 0:2 * P].rearrange("p (i n) -> p i n", i=2)).then_inc(
                                        *n.act.up())
                                if not last:
                                    @block.gpsimd
                                    def _(pool):
                                        pool.wait_ge(*n.pe.now())
                                        linker(pool, n.pool)(G.tensor_tensor(n.off[(level + 1) % 2], n.lt, b2(k.c(f"level{level + 1}")),
                                                        ALU.mult))

                            def x_off_x(n):
                                @block.tensor
                                def _(pe):
                                    pe.wait_ge(*n.act.now())
                                    pe.wait_ge(*n.dve.now())
                                    for i in range(2):
                                        if not last:
                                            nc.tensor.matmul(n.bank(3)[:, i * P:(i + 1) * P], n.xx[:, 1, i, :],
                                                             n.p[:, i, :], start=True, stop=True)
                                        mm = nc.tensor.matmul(n.bank(3)[:, (2 + i) * P:(3 + i) * P], n.p[:, i, :],
                                                              n.xx[:, 1, i, :], start=True, stop=True)
                                    mm.then_inc(*n.pe.up())

                                @block.vector
                                def _(dve):
                                    dve.wait_ge(*n.pe.now())
                                    which = slice(1, 2) if last else slice(0, 2)
                                    x = n.xx[:, which].rearrange("p w i n -> p (w i n)")
                                    V.tensor_tensor(x, x, n.bank(3)[:, 2 * P if last else 0:4 * P],
                                                    ALU.subtract).then_inc(*n.dve.up())

                            each(off_x)
                            each(x_off_x)

                        def right_side(n):
                            @block.tensor
                            def _(pe):
                                pe.wait_ge(*n.dve.now())
                                pe.wait_ge(*n.pool.now())
                                pe.wait_ge(*n.act.now())
                                for i in range(2):
                                    o = n.bank(2)[:, i * C64:(i + 1) * C64]
                                    nc.tensor.matmul(o, n.ar[:, i, 0, :], n.state[:, i, :], start=True, stop=False)
                                    mm = nc.tensor.matmul(o, n.mt[:, i, :], n.vst[:, i, :], start=False, stop=True)
                                mm.then_inc(*n.pe.up())

                            @block.scalar
                            def _(act):
                                act.wait_ge(*n.pe.now())
                                nc.scalar.mul(n.g, n.bank(2)[:, 0:2 * C64].rearrange("p (i n) -> p i n", i=2),
                                              -1.0).then_inc(*n.act.up())

                        def solve(n):
                            @block.tensor
                            def _(pe):
                                pe.wait_ge(*n.act.now())
                                for i in range(2):
                                    mm = nc.tensor.matmul(n.bank(3)[:, i * C64:(i + 1) * C64], n.xx[:, 1, i, :],
                                                          n.g[:, i, :], start=True, stop=True)
                                mm.then_inc(*n.pe.up())

                            @block.scalar
                            def _(act):
                                act.wait_ge(*n.pe.now())
                                nc.scalar.copy(n.u, n.bank(3)[:, 0:2 * C64].rearrange("p (i n) -> p i n", i=2)).then_inc(
                                    *n.act.up())

                        def results(n):
                            @block.tensor
                            def _(pe):
                                pe.wait_ge(*n.act.now())
                                for i in range(2):
                                    o = n.bank(1)[:, i * C64:(i + 1) * C64]
                                    nc.tensor.matmul(o, n.bst[:, i, :], n.u[:, i, :], start=True, stop=False)
                                    nc.tensor.matmul(o, n.kst[:, i, :], n.vst[:, i, :], start=False,
                                                     stop=True).then_inc(*n.pe.up())
                                if wanted:
                                    for i in range(2):
                                        o = n.bank(2)[:, i * C64:(i + 1) * C64]
                                        nc.tensor.matmul(o, n.ar[:, i, 1, :], n.state[:, i, :], start=True, stop=False)
                                        nc.tensor.matmul(o, n.rbt[:, i, :], n.u[:, i, :], start=False, stop=False)
                                        nc.tensor.matmul(o, n.rkt[:, i, :], n.vst[:, i, :], start=False,
                                                         stop=True).then_inc(*n.pe.up())

                            @block.vector
                            def _(dve):
                                link = linker(dve, n.dve)
                                dve.wait_ge(*n.pe.now())
                                link(V.tensor_tensor(n.state, n.state, n.bank(1)[:, 0:2 * C64].rearrange(
                                    "p (i n) -> p i n", i=2), ALU.add))
                                V.tensor_tensor(n.state, n.state, n.ep[:, :, c * C64 + C64 - 1:c * C64 + C64].to_broadcast(
                                    [P, 2, C64]), ALU.mult).then_inc(*n.dve.up())
                                if wanted:
                                    o = y[:, pr, c if n.d == 0 else 3 - c, :]
                                    b = n.bank(2)[:, 0:2 * C64].rearrange("p (i n) -> p i n", i=2)
                                    if c < 2:
                                        V.tensor_copy(o, b).then_inc(*n.dve.up())
                                    else:
                                        V.tensor_tensor(o, o, b, ALU.add).then_inc(*n.dve.up())

                        if wanted and c == 2:
                            for a, b in ((0, 1), (1, 0)):
                                n, other = lanes[a], lanes[b]

                                @block.vector
                                def _(dve):
                                    dve.wait_ge(*other.dve.now())
                        for step in (right_side, solve, results):
                            each(step)

        rwkv_post(k, ctx, zx, y, rows, ring, obT)


def rwkv_post(k, ctx, zx, y, rows, ring, obT):
    nc, I = k.nc, k.ins
    V = nc.vector
    st = k.sb("rw_st", [P, 2, 32], ctx=ctx)
    y32 = y[:].rearrange("p a c n -> p (a c) n")
    wide = lambda ap: ap.to_broadcast([P, 32, C64])
    sq = ring[:, 0:2048].rearrange("p (g n) -> p g n", g=32)
    ybd = ring[:, 2048:2048 + 4096].rearrange("p (g n) -> p g n", g=32)
    bon = ring[:, 6144:8192].rearrange("p (c n) -> p c n", c=DC)
    g_up = ring[:, 8192:9216]
    sg = ring[:, 9216:9472]
    gate = ring[:, 10240:12288].rearrange("p (c n) -> p c n", c=DC)
    load(k, [(g_up, I["rw_g_up_2"])])
    with nc.Block() as block:
        @block.vector
        def _(dve):
            link = linker(dve, k.dve_done)
            link(V.tensor_reduce(st[:, 0, :], y32, AX.X, ALU.add))
            link(V.tensor_scalar(st[:, 0, :], st[:, 0, :], 1.0 / C64, None, ALU.mult))
            link(V.tensor_tensor(y32, y32, wide(st[:, 0, :].unsqueeze(2)), ALU.subtract))

        @block.scalar
        def _(act):
            nc.scalar.activation(sg, zx[:, 25, :], ACT.Sigmoid).then_inc(*k.act_done.up())
            act.wait_ge(*k.dve_done.now())
            nc.scalar.activation(sq, y32, ACT.Square).then_inc(*k.act_done.up())

        @block.tensor
        def _(pe):
            pe.wait_ge(*k.act_done.now())
            for c in range(DC):
                mm = nc.tensor.matmul(k.ps[:, c // 2, c % 2 * S:c % 2 * S + S], g_up[:, c * P:(c + 1) * P], sg,
                                      start=True, stop=True)
            mm.then_inc(*k.pe_done.up())

        @block.vector
        def _(dve):
            link = linker(dve, k.dve_done)
            dve.wait_ge(*k.act_done.now())
            link(V.tensor_reduce(st[:, 1, :], sq, AX.X, ALU.add))
            link(V.tensor_scalar(st[:, 1, :], st[:, 1, :], 1.0 / C64, RW_LN_EPS, ALU.mult, ALU.add))
            link(V.memset(ybd, 0.0))
            for c in range(DC):
                link(V.scalar_tensor_tensor(bon[:, c, :], zx[:, c, :], rows[:, ROW_RK, c:c + 1], zx[:, 8 + c, :],
                                            ALU.mult, ALU.mult))
            dve.wait_ge(*k.pe_done.now())
            link(V.tensor_copy(gate, k.ps[:, 0:4, :].rearrange("p b (c n) -> p (b c) n", c=2)))

        @block.scalar
        def _(act):
            act.wait_ge(*k.dve_done.now())
            nc.scalar.activation(st[:, 1, :], st[:, 1, :], ACT.Sqrt).then_inc(*k.act_done.up())

        @block.tensor
        def _(pe):
            pe.wait_ge(*k.dve_done.now())
            for b in range(4):
                mm = nc.tensor.matmul(k.ps[:, 4 + b, :], k.c("head_ones"),
                                      bon[:, 2 * b:2 * b + 2, :].rearrange("p c n -> p (c n)"), start=True, stop=True)
            mm.then_inc(*k.pe_done.up())

        @block.vector
        def _(dve):
            link = linker(dve, k.dve_done)
            dve.wait_ge(*k.act_done.now())
            link(V.reciprocal(st[:, 1, :], st[:, 1, :]))
            for hh in range(2):
                r = slice(64 * hh, 64 * hh + 64)
                link(V.tensor_tensor(ybd[r, :, 64 * hh:64 * hh + 64], y32[r],
                                     st[r, 1, :].unsqueeze(2).to_broadcast([64, 32, C64]), ALU.mult))

        @block.tensor
        def _(pe):
            pe.wait_ge(*k.dve_done.now())
            for c in range(DC):
                for n in range(4):
                    mm = nc.tensor.matmul(k.ps[:, c // 2, c % 2 * S + n * C64:c % 2 * S + (n + 1) * C64],
                                          ybd[:, 4 * c + n, :], k.c("fold"), start=True, stop=True)
            mm.then_inc(*k.pe_done.up())

        @block.vector
        def _(dve):
            link = linker(dve, k.dve_done)
            dve.wait_ge(*k.pe_done.now())
            link(V.tensor_tensor(bon, k.ps[:, 4:8, :].rearrange("p b (c n) -> p (b c) n", c=2), zx[:, 16:24, :], ALU.mult))
            for c in range(DC):
                link(V.tensor_scalar(obT[:, c, :], k.ps[:, c // 2, c % 2 * S:c % 2 * S + S], rows[:, ROW_G, c:c + 1],
                                     rows[:, ROW_B, c:c + 1], ALU.mult, ALU.add))
            link(V.tensor_tensor(obT[:], obT[:], bon, ALU.add))
            link(V.tensor_tensor(obT[:], obT[:], gate, ALU.mult))


PH = 8
TOPK = 16
SLOTS = PH * TOPK
NBUF = 8


def peer(k):
    nc, I = k.nc, k.ins
    V = nc.vector
    with ExitStack() as ctx:
        sb = lambda name, shape, dt=F32: k.sb("pr_" + name, shape, dt, ctx)
        qT = sb("qT", [P, 2 * PH, S])
        keysT = sb("keysT", [P, 2 * PH, P])
        idxT = sb("idxT", [P, S], U32)
        gateT = sb("gateT", [P, S])
        load(k, [(keysT[:], I["peer_keysT"])])
        gemm(k, [(src, "feat", k.hT, "v" if n % 2 else "s", copy_feat(k, qT, 2 * n, "v" if n % 2 else "s"))
                 for n, src in enumerate(columns(I["peer_wq_2"], 0, 2 * D))])
        with ExitStack() as c2:
            picks(k, c2, qT, keysT, idxT, gateT)
        with ExitStack() as c2:
            gathers(k, c2, idxT, gateT)


def picks(k, ctx, qT, keysT, idxT, gateT):
    nc = k.nc
    V = nc.vector
    sb = lambda name, shape, dt=F32: k.sb("pk_" + name, shape, dt, ctx)
    sc = sb("sc", [P, 2 * PH, P])
    sv = sb("sv", [P, PH, 2, TOPK])
    si = sb("si", [P, PH, 2, TOPK], U32)
    sif = sb("sif", [P, PH, 2, TOPK])
    cand = sb("cand", [P, PH, TOPK * TOPK])
    ts = sb("ts", [P, PH, TOPK])
    tp = sb("tp", [P, PH, TOPK], U32)
    ij = sb("ij", [P, PH * TOPK], U32)
    ijf = sb("ijf", [P, PH * TOPK])
    big = sb("big", [P, PH * TOPK, TOPK])
    part = sb("part", [P, 2, PH * TOPK])
    den = sb("den", [P, PH])

    def top16(link, values, indices, data):
        link(V.max(values[:, 0:8], data))
        link(V.max_index(indices[:, 0:8], values[:, 0:8], data))
        link(V.match_replace(data, values[:, 0:8], data, NEG))
        link(V.max(values[:, 8:16], data))
        link(V.max_index(indices[:, 8:16], values[:, 8:16], data))

    for t in range(TT):
        with nc.Block() as block:
            @block.tensor
            def _(pe):
                for hp in range(2 * PH):
                    mm = nc.tensor.matmul(k.ps[:, hp // 4, hp % 4 * P:(hp % 4 + 1) * P], qT[:, hp, t * P:(t + 1) * P],
                                          keysT[:, hp, :], start=True, stop=True)
                mm.then_inc(*k.pe_done.up())

            @block.vector
            def _(dve):
                link = linker(dve, k.dve_done)
                dve.wait_ge(*k.pe_done.now())
                link(V.tensor_copy(sc[:], k.ps[:, 0:4, :].rearrange("p b (h n) -> p (b h) n", h=4)))
                for hp in range(2 * PH):
                    top16(link, sv[:, hp // 2, hp % 2, :], si[:, hp // 2, hp % 2, :], sc[:, hp, :])
                link(V.tensor_copy(sif[:], si[:]))
                link(V.tensor_tensor(cand[:].rearrange("p h (i j) -> p h i j", i=TOPK),
                                     sv[:, :, 0, :].unsqueeze(3).to_broadcast([P, PH, TOPK, TOPK]),
                                     sv[:, :, 1, :].unsqueeze(2).to_broadcast([P, PH, TOPK, TOPK]), ALU.add))
                for h in range(PH):
                    top16(link, ts[:, h, :], tp[:, h, :], cand[:, h, :])
                tpf = tp[:].rearrange("p h n -> p (h n)")
                iota = k.c("iota")[:, 0:TOPK].unsqueeze(1).to_broadcast([P, PH * TOPK, TOPK])
                for side in range(2):
                    link(V.tensor_scalar(ij[:], tpf, 4, None, ALU.logical_shift_right) if side == 0 else
                         V.tensor_scalar(ij[:], tpf, TOPK - 1, None, ALU.bitwise_and))
                    link(V.tensor_copy(ijf[:], ij[:]))
                    link(V.tensor_tensor(big[:], iota, ijf[:].unsqueeze(2).to_broadcast([P, PH * TOPK, TOPK]),
                                         ALU.is_equal))
                    b4 = big[:].rearrange("p (h s) n -> p h s n", h=PH)
                    link(V.tensor_tensor(b4, b4, sif[:, :, side, :].unsqueeze(2).to_broadcast([P, PH, TOPK, TOPK]),
                                         ALU.mult))
                    link(V.tensor_reduce(part[:, side, :], big[:], AX.X, ALU.add))
                link(V.scalar_tensor_tensor(part[:, 0, :], part[:, 0, :], float(P), part[:, 1, :], ALU.mult, ALU.add))
                link(V.tensor_tensor(cand[:, :, 0:TOPK], ts[:], ts[:, :, 0:1].to_broadcast([P, PH, TOPK]),
                                     ALU.subtract))

            @block.scalar
            def _(act):
                act.wait_ge(*k.dve_done.now())
                nc.scalar.activation(ts[:], cand[:, :, 0:TOPK], ACT.Exp).then_inc(*k.act_done.up())

            @block.vector
            def _(dve):
                link = linker(dve, k.dve_done)
                dve.wait_ge(*k.act_done.now())
                link(V.tensor_reduce(den[:], ts[:], AX.X, ALU.add))
                link(V.reciprocal(den[:], den[:]))
                link(V.tensor_tensor(ts[:], ts[:], den[:].unsqueeze(2).to_broadcast([P, PH, TOPK]), ALU.mult))

            @block.tensor
            def _(pe):
                pe.wait_ge(*k.dve_done.now())
                nc.tensor.transpose(k.ps[:, 4, 0:P], part[:, 0, :], k.c("ident"))
                nc.tensor.transpose(k.ps[:, 4, P:2 * P], ts[:].rearrange("p h n -> p (h n)"), k.c("ident")).then_inc(
                    *k.pe_done.up())

            @block.vector
            def _(dve):
                dve.wait_ge(*k.pe_done.now())
                V.tensor_copy(idxT[:, t * P:(t + 1) * P], k.ps[:, 4, 0:P]).then_inc(*k.dve_done.up())
                V.tensor_copy(gateT[:, t * P:(t + 1) * P], k.ps[:, 4, P:2 * P]).then_inc(*k.dve_done.up())


def gathers(k, ctx, idxT, gateT):
    nc, I = k.nc, k.ins
    V = nc.vector
    sb = lambda name, shape, dt=F32: k.sb("ga_" + name, shape, dt, ctx)
    rows = k.ring[:].rearrange("p a n -> p (a n)")[:, 0:NBUF * D].rearrange("p (j n) -> p j n", j=NBUF)
    num = sb("num", [P, NBUF], U32)
    sel = sb("sel", [P, 4, P])
    dots = sb("dots", [P, S])
    dot8 = sb("dot8", [P, NBUF])
    junk = sb("junk", [P, D])
    window = sb("window", [P, 2 * P - 1])
    zero = sb("zero", [P, P])
    wcol = sb("wcol", [P, 4, P])
    acc = sb("acc", [P, TT, D])
    sem = lambda n: Signal(k.sem("ga_" + n))
    landed = [sem(f"landed{j}") for j in range(NBUF)]
    num_ready, sel_ready, bcast_ready, dot_done, dots_kept, wcol_ready, v_used = map(
        sem, ("num_ready", "sel_ready", "bcast_ready", "dot_done", "dots_kept", "wcol_ready", "v_used"))
    TURNS = P // NBUF
    CREDIT = NBUF

    def gather(pool, j, table, turn, base, freed, freed_base):
        pool.sem_clear(num_ready.sem)
        pool.wait_ge(freed.sem, turn * NBUF + (freed_base + j + 1))
        nc.gpsimd.tensor_copy(num[:, j:j + 1], idxT[:, bass.ds(turn * NBUF + (base + j), 1)]).then_inc(num_ready.sem, 1)
        pool.wait_ge(num_ready.sem, 1)
        nc.gpsimd.indirect_dma_start(rows[:, j, :], None, table, bass.IndirectOffsetOnAxis(ap=num[:, j:j + 1], axis=0)
                                     ).then_inc(landed[j].sem, 16)

    with nc.Block() as block:
        @block.vector
        def _(dve):
            V.memset(window[:], 0.0).then_inc(*k.dve_done.up())
            V.memset(zero[:], 0.0).then_inc(*k.dve_done.up())
            dve.wait_ge(*k.dve_done.now())
            V.memset(window[:, P - 1:P], 1.0).then_inc(dot_done.sem, CREDIT)
            dot_done.n += CREDIT

        @block.tensor
        def _(pe):
            pe.wait_ge(*dot_done.now())
            nc.tensor.matmul(k.ps[:, 0, 0:P], zero[:], zero[:], start=True, stop=True).then_inc(bcast_ready.sem, CREDIT)
            bcast_ready.n += CREDIT

    for t in range(TT):
        with nc.Block() as block:
            @block.gpsimd
            def _(pool):
                with pool.Fori(0, TURNS) as i:
                    for j in range(NBUF):
                        gather(pool, j, I["peer_u_2"], i, t * P, dot_done, dot_done.n - NBUF)

            @block.scalar
            def _(act):
                with act.Fori(0, TURNS) as i:
                    for j in range(NBUF):
                        act.wait_ge(bcast_ready.sem, i * NBUF + (bcast_ready.n + j - 3))
                        nc.scalar.copy(sel[:, j % 4, :], k.c("ident")[:, bass.ds(i * NBUF + j, 1)].to_broadcast([P, P])
                                       ).then_inc(sel_ready.sem, 1)

            @block.tensor
            def _(pe):
                with pe.Fori(0, TURNS) as i:
                    for j in range(NBUF):
                        pe.wait_ge(sel_ready.sem, i * NBUF + (sel_ready.n + j + 1))
                        pe.wait_ge(dot_done.sem, i * NBUF + (dot_done.n + j - 3))
                        for half in range(2):
                            mm = nc.tensor.matmul(k.ps[:, 2 * (j % 4) + half, :], sel[:, j % 4, :],
                                                  k.h[:, t, half * 512:(half + 1) * 512], start=True, stop=True)
                        mm.then_inc(bcast_ready.sem, 1)

            @block.vector
            def _(dve):
                with dve.Fori(0, TURNS) as i:
                    for j in range(NBUF):
                        dve.wait_ge(bcast_ready.sem, i * NBUF + (bcast_ready.n + j + 1))
                        dve.wait_ge(landed[j].sem, i * 16 + (landed[j].n + 16))
                        V.scalar_tensor_tensor(junk[:], rows[:, j, :], 1.0,
                                               k.ps[:, 2 * (j % 4):2 * (j % 4) + 2, :].rearrange("p b n -> p (b n)"),
                                               ALU.mult, ALU.mult, accum_out=dot8[:, j:j + 1]).then_inc(dot_done.sem, 1)
                        dve.wait_ge(dot_done.sem, i * NBUF + (dot_done.n + j + 1))
                    V.tensor_copy(dots[:, bass.ds(i * NBUF + t * P, NBUF)], dot8[:]).then_inc(dots_kept.sem, 1)
                    dve.wait_ge(dots_kept.sem, i + (dots_kept.n + 1))
        for s in [sel_ready, bcast_ready, dot_done]:
            s.n += P
        dots_kept.n += TURNS
        for s in landed:
            s.n += 16 * TURNS

    with nc.Block() as block:
        @block.scalar
        def _(act):
            nc.scalar.activation(dots[:], dots[:], ACT.Gelu_apprx_tanh).then_inc(*k.act_done.up())

        @block.vector
        def _(dve):
            dve.wait_ge(*k.act_done.now())
            V.tensor_tensor(dots[:], dots[:], gateT[:], ALU.mult).then_inc(*k.dve_done.up())

        @block.tensor
        def _(pe):
            pe.wait_ge(*k.dve_done.now())
            for b in range(4):
                mm = nc.tensor.matmul(k.ps[:, b, :], zero[:], rows[:, 0, 0:512], start=True, stop=False)
            mm.then_inc(v_used.sem, CREDIT)
            v_used.n += CREDIT

    for t in range(TT):
        with nc.Block() as block:
            @block.gpsimd
            def _(pool):
                with pool.Fori(0, TURNS) as i:
                    for j in range(NBUF):
                        gather(pool, j, I["peer_v_2"], i, t * P, v_used, v_used.n - NBUF)

            @block.vector
            def _(dve):
                with dve.Fori(0, TURNS) as i:
                    for j in range(NBUF):
                        dve.wait_ge(v_used.sem, i * NBUF + (v_used.n + j - 3))
                        V.tensor_scalar(wcol[:, j % 4, :], window[:, bass.ds(i * -NBUF + (P - 1 - j), P)],
                                        dots[:, bass.ds(i * NBUF + (t * P + j), 1)], None, ALU.mult).then_inc(
                                            wcol_ready.sem, 1)

            @block.tensor
            def _(pe):
                with pe.Fori(0, TURNS) as i:
                    for j in range(NBUF):
                        pe.wait_ge(wcol_ready.sem, i * NBUF + (wcol_ready.n + j + 1))
                        pe.wait_ge(landed[j].sem, i * 16 + (landed[j].n + 16))
                        for half in range(2):
                            mm = nc.tensor.matmul(k.ps[:, 2 * t + half, :], wcol[:, j % 4, :],
                                                  rows[:, j, half * 512:(half + 1) * 512], start=False, stop=False)
                        mm.then_inc(v_used.sem, 1)
        for s in [v_used, wcol_ready]:
            s.n += P
        for s in landed:
            s.n += 16 * TURNS

    with nc.Block() as block:
        @block.tensor
        def _(pe):
            for b in range(4):
                mm = nc.tensor.matmul(k.ps[:, b, :], zero[:], rows[:, 0, 0:512], start=False, stop=True)
            mm.then_inc(*k.pe_done.up())

        @block.vector
        def _(dve):
            dve.wait_ge(*k.pe_done.now())
            V.tensor_copy(acc[:].rearrange("p t n -> p (t n)"), k.ps[:, 0:4, :].rearrange("p b n -> p (b n)")).then_inc(
                *k.dve_done.up())
    add_gated(k, acc, k.gate[:])


def modulation(k, c, w, b, norm):
    with ExitStack() as ctx:
        adaln_rows(k, [k.ins[c]], k.ins[w], k.ins[b], k.ins[norm],
                   [(0, [("shift", k.shift)]), (1, [("gain", k.gain)]), (2, [("gate", k.gate)])], ctx, w)


def program(nc, ins, out):
    with ExitStack() as ctx:
        k = Core(nc, ins, ctx)
        load(k, [(k.const[:], ins["const_table"]), (k.x[:], ins["x"].rearrange("(t p) d -> p t d", p=P))])

        def normed(src=None):
            with ExitStack() as c2:
                sq = k.sb(f"sq{k.dve_done.n}", [P, TT, D], ctx=c2)
                norm_modulate(k, k.x, k.gain[:], k.shift[:], k.h, k.hT, sq)

        def even_a():
            modulation(k, "c", "e_mod_mix_w", "e_mod_mix_b", "e_norm_mix")
            normed()
            even_mixer(k)

        def even_b():
            modulation(k, "c", "e_mod_ffn_w", "e_mod_ffn_b", "e_norm_ffn")
            normed()
            even_ffn(k)

        def odd_a():
            modulation(k, "c", "o_mod_mix_w", "o_mod_mix_b", "o_norm_mix")
            normed()
            s5_mixer(k)

        def odd_b():
            modulation(k, "c", "o_mod_ffn_w", "o_mod_ffn_b", "o_norm_ffn")
            normed()
            moe(k)
            final_norm(k)

        def second_a():
            hybrid_mixer(k)

        def second_b():
            with ExitStack() as ctx:
                adaln_rows(k, [k.ins["c_2"]], k.ins["w_mod_2"], k.ins["b_mod_2"], k.ins["norm2_g_2"],
                           [(3, [("shift", k.shift)]), (4, [("gain", k.gain)]), (5, [("gate", k.gate)])], ctx, "mod2b")
            normed()
            peer(k)

        stages = [even_a, even_b, odd_a, odd_b, second_a, second_b]
        for stage in stages:
            stage()
        with nc.Block() as block:
            @block.sync
            def _(sp):
                sp.dma_start(out.rearrange("(t p) d -> p t d", p=P), k.x[:]).then_inc(*k.loaded.up(16))
                sp.wait_ge(*k.loaded.now())


def _laid_out(i):
    d = {}
    for name in ("e_norm_mix e_mod_mix_w e_mod_mix_b e_w_in e_fox_fb e_gla_w2 e_gla_norm e_w_o e_norm_ffn e_mod_ffn_w "
                 "e_mod_ffn_b o_norm_mix o_mod_mix_w o_mod_mix_b o_w_in o_w_glu o_w_o o_norm_ffn o_mod_ffn_w "
                 "o_mod_ffn_b o_router o_exp_gate o_exp_up o_exp_down x w_mod_2 b_mod_2 norm1_g_2 w_in_2 q_norm_g_2 "
                 "k_norm_g_2 diff_lambda_2 diff_out_g_2 rw_g_up_2 w_branch_a_2 w_branch_b_2 w_out_2 norm2_g_2 "
                 "peer_wq_2 peer_u_2 peer_v_2 ctx_2").split():
        d[name] = i[name][0]
    for name in "e_ffn_gate e_ffn_up e_ffn_down final_norm".split():
        d[name] = i[name]

    def features(a):
        return a.reshape(-1, P).T

    def states(a):
        return a.reshape(32, P, -1).transpose(1, 0, 2)

    for name in ("c", "c_2", "c_ctx_2", "e_gla_b2"):
        d[name] = features(i[name])
    d["w_small"] = np.concatenate([i["e_w_in"][0][:, 1536:1544], i["e_w_in"][0][:, 3080:3096]], 1)
    log_dt = np.repeat(i["o_log_dt"][0][:, None], 64, 1)
    d["s5_par"] = np.stack([states(a)[:, :, 0] for a in (i["o_lam_re"][0], i["o_lam_im"][0], log_dt)], 1)
    d["s5_b"] = np.stack([states(i["o_b_re"][0]), states(i["o_b_im"][0])], 1)
    d["s5_c"] = np.stack([states(i[n][0].transpose(0, 2, 1)) for n in ("o_c_re", "o_c_im")], 1)
    d["s5_dskip"] = features(i["o_d_skip"])
    d["rw_shift_2"] = i["rw_shift_2"][0].reshape(3, 26, P).transpose(2, 0, 1)
    d["rw_rows"] = np.stack([features(a) for a in (
        i["rw_k_k_2"], i["rw_k_a_2"], i["rw_r_k_2"], i["rw_ln_g_2"], i["rw_ln_b_2"], i["rw_w0_2"][0, 0],
        i["rw_w0_2"][0, 1], i["rw_a0_2"][0, 0], i["rw_a0_2"][0, 1])], 1)
    d["rw_lora"] = np.concatenate([i["rw_w_up_2"][0].transpose(1, 0, 2), i["rw_a_up_2"][0].transpose(1, 0, 2)], 0)
    d["peer_keysT"] = i["peer_keys_2"][0].transpose(3, 0, 1, 2).reshape(P, 2 * PH, P)
    d["const_table"] = np.concatenate(list(constant_table().values()), 1)
    return {n: np.ascontiguousarray(a) for n, a in d.items()}


def kernel(**inputs):
    import concourse.bacc as _bacc
    from concourse.bass_utils import run_bass_kernel_spmd as _run

    nc = _bacc.Bacc("TRN2", target_bir_lowering=False, num_devices=1)
    laid = _laid_out({n: np.asarray(a) for n, a in inputs.items()})
    ins = {n: nc.dram_tensor(f"in_{n}", list(a.shape), mybir.dt.from_np(a.dtype), kind="ExternalInput").ap()
           for n, a in laid.items()}
    out = nc.dram_tensor("out_x", [S, D], F32, kind="ExternalOutput").ap()
    program(nc, ins, out)
    r = _run(nc, [{f"in_{n}": a for n, a in laid.items()}], core_ids=[0])
    return r.results[0]["out_x"].reshape(1, S, D)
```

```python
import math
from contextlib import ExitStack

import numpy as np

import concourse.bass as bass
import concourse.mybir as mybir
from concourse.alu_op_type import AluOpType as ALU

ACT = mybir.ActivationFunctionType
AX = mybir.AxisListType
F32 = mybir.dt.float32
U32 = mybir.dt.uint32
I32 = mybir.dt.int32
BF16 = mybir.dt.bfloat16

P = 128
D = 1024
DC = D // P
S = 256
TT = S // P
EPS = 1e-6
NEG = -1e30
C64 = 64
NSLOT = 6
SLOT = 2048
BANKS = 8
FF = 2816
FF_STEPS = FF // 256


class Signal:

    def __init__(self, sem):
        self.sem, self.n = sem, 0

    def up(self, k=1):
        self.n += k
        return self.sem, k

    def now(self):
        return self.sem, self.n


def constant_table():
    p = np.arange(P)[:, None]
    f = np.arange(P)[None, :]
    same = (p // C64) == (f // C64)
    pi, fi = p % C64, f % C64
    t = {}
    t["ident"] = p == f
    t["ones"] = np.ones((P, S))
    t["upto"] = p <= f
    t["head_ones"] = same
    t["incl"] = same & (pi <= fi)
    t["strict"] = same & (pi < fi)
    t["incl_rev"] = same & (pi <= C64 - 1 - fi)
    for n in range(6):
        m = 1 << n
        level = same & (pi // (2 * m) == fi // (2 * m)) & (pi // m % 2 == 0) & (fi // m % 2 == 1)
        t[f"level{n}"] = level.T if n else level
    t["fox_mask"] = np.where(f <= p, 0.0, NEG)
    t["reset"] = np.tile((np.arange(512) % C64 != 0).astype(np.float32), (P, 1))
    t["iota"] = np.tile(np.arange(P), (P, 1))
    t["fold"] = pi == np.arange(C64)[None, :]
    tok = np.arange(S)
    inv = 10000.0 ** (-np.arange(16, dtype=np.float32) / np.float32(16))
    ang = np.stack([(tok // 64)[:, None] * inv, (tok % 64)[:, None] * inv], axis=1).astype(np.float32)
    for name, fn in (("rope_cos", np.cos), ("rope_sin", np.sin)):
        t[name] = fn(ang).reshape(TT, P, 32).transpose(1, 0, 2).reshape(P, TT * 32)
    return {k: np.asarray(v, np.float32) for k, v in t.items()}


def constant_places():
    at, places = 0, {}
    for name, v in constant_table().items():
        places[name] = (at, v.shape[1])
        at += v.shape[1]
    return places, at


class Core:

    def __init__(self, nc, ins, ctx):
        self.nc, self.ins, self.ctx = nc, ins, ctx
        self.ps = ctx.enter_context(nc.psum_tensor("ps", [P, BANKS, 512], F32))
        self.places, n_const = constant_places()
        self.const = self.sb("const", [P, n_const])
        self.x = self.sb("x", [P, TT, D])
        self.h = self.sb("h", [P, TT, D])
        self.hT = self.sb("hT", [P, DC, S])
        self.ring = self.sb("ring", [P, NSLOT, SLOT])
        self.gain = self.sb("gain", [P, D])
        self.shift = self.sb("shift", [P, D])
        self.gate = self.sb("gate", [P, D])
        self.stat = self.sb("stat", [P, 64])
        self.pe_done = Signal(self.sem("pe_done"))
        self.dve_done = Signal(self.sem("dve_done"))
        self.act_done = Signal(self.sem("act_done"))
        self.pool_done = Signal(self.sem("pool_done"))
        self.slot_used = Signal(self.sem("slot_used"))
        self.evac_dve = Signal(self.sem("evac_dve"))
        self.evac_act = Signal(self.sem("evac_act"))
        self.up_ready = Signal(self.sem("up_ready"))
        self.silu_ready = Signal(self.sem("silu_ready"))
        self.prod_ready = Signal(self.sem("prod_ready"))
        self.down_used = Signal(self.sem("down_used"))
        self.y_free = Signal(self.sem("y_free"))
        self.landed = [Signal(self.sem(f"landed{i}")) for i in range(NSLOT)]
        self.loaded = Signal(self.sem("loaded"))
        self.job = 0
        self.ahead = 0

    def sem(self, name):
        return self.ctx.enter_context(self.nc.semaphore(name))

    def sb(self, name, shape, dt=F32, ctx=None):
        return (ctx or self.ctx).enter_context(self.nc.sbuf_tensor(name, shape, dt))

    def c(self, name):
        at, n = self.places[name]
        return self.const[:, at:at + n]


def load(k, pairs, ahead=()):
    with k.nc.Block() as block:
        @block.sync
        def _(sp):
            for dst, src in pairs:
                sp.dma_start(dst, src).then_inc(*k.loaded.up(16))
            for n, src in enumerate(ahead[:NSLOT]):
                slot = (k.job + n) % NSLOT
                sp.dma_start(ring_block(k, slot, src.shape[2]), src).then_inc(*k.landed[slot].up(16))
                k.ahead += 1
            sp.wait_ge(*k.loaded.now())


def ring_block(k, slot, w):
    return k.ring[:, slot, 0:DC * w].rearrange("p (c n) -> p c n", c=DC)


def gemm(k, jobs, beside=None, then=()):
    nc = k.nc
    first, base = k.job, k.slot_used.n
    loads = []
    block_of = []
    for j, job in enumerate(jobs):
        if job[0] is not None:
            loads.append(j)
        block_of.append(len(loads) - 1)
    last_user = [max(j for j in range(len(jobs)) if block_of[j] == n) for n in range(len(loads))]
    k.job += len(loads)
    slot = lambda n: (first + n) % NSLOT
    engine_of = [job[3] for job in jobs]
    evac = {"v": k.evac_dve, "s": k.evac_act}
    evac_base = {e: evac[e].n for e in evac}
    evac_count = lambda j: evac_base[engine_of[j]] + engine_of[:j + 1].count(engine_of[j])
    landed_at = [0] * len(loads)
    ahead, k.ahead = k.ahead, 0

    with nc.Block() as block:
        @block.sync
        def _(sp):
            sources = [jobs[j][0] for j in loads] + list(then[:NSLOT])
            for n, src in enumerate(sources):
                if n >= NSLOT:
                    sp.wait_ge(k.slot_used.sem, base + last_user[n - NSLOT] + 1)
                if n >= ahead:
                    sp.dma_start(ring_block(k, slot(n), src.shape[2]), src).then_inc(*k.landed[slot(n)].up(16))
                if n < len(loads):
                    landed_at[n] = k.landed[slot(n)].n
                else:
                    k.ahead += 1

        @block.tensor
        def _(pe):
            for j, (_src, kind, op, *_rest) in enumerate(jobs):
                n = block_of[j]
                w = jobs[loads[n]][0].shape[2]
                bank = k.ps[:, j % BANKS, :]
                wt = ring_block(k, slot(n), w)
                pe.wait_ge(k.landed[slot(n)].sem, landed_at[n])
                if j >= BANKS:
                    pe.wait_ge(evac[engine_of[j - BANKS]].sem, evac_count(j - BANKS))
                if kind == "feat":
                    for f in range(0, w, P):
                        m = min(P, w - f)
                        for c in range(DC):
                            mm = nc.tensor.matmul(bank[0:m, f // P * S:f // P * S + S], wt[:, c, f:f + m],
                                                  op[:, c, :], start=(c == 0), stop=(c == DC - 1))
                elif kind == "tok":
                    for t in range(TT):
                        for c in range(DC):
                            mm = nc.tensor.matmul(bank[:, t * w:(t + 1) * w], op[:, c, t * P:(t + 1) * P],
                                                  wt[:, c, :], start=(c == 0), stop=(c == DC - 1))
                else:
                    for c in range(DC):
                        mm = nc.tensor.matmul(bank[:, 0:w], op[:, c, :], wt[:, c, :],
                                              start=(c == 0), stop=(c == DC - 1))
                mm.then_inc(*k.slot_used.up())

        if beside is not None:
            beside(block)

        def evacuations(eng, name, done):
            def link(ins):
                ins.then_inc(*done.up())
                eng.wait_ge(*done.now())

            for j, (src, kind, op, e, evacuate) in enumerate(jobs):
                if e == name:
                    eng.wait_ge(k.slot_used.sem, base + j + 1)
                    evacuate(k.ps[:, j % BANKS, :], link).then_inc(*evac[e].up())
                    eng.wait_ge(*evac[e].now())

        @block.vector
        def _(dve):
            evacuations(dve, "v", k.dve_done)

        @block.scalar
        def _(act):
            evacuations(act, "s", k.act_done)


def columns(w, a, b):
    v = w.rearrange("(c p) n -> p c n", p=P)
    return [v[:, :, i:min(i + 256, b)] for i in range(a, b, 256)]


def adaln_rows(k, conds, w, bias, norm, want, ctx, tag, then=()):
    nc = k.nc
    cs = k.sb(f"cs_{tag}", [P, len(conds), DC], ctx=ctx)
    cb = k.sb(f"cb_{tag}", [P, len(conds), DC, P], ctx=ctx)
    nb = k.sb(f"nb_{tag}", [P, D], ctx=ctx)
    bb = k.sb(f"bb_{tag}", [P, len(want), D], ctx=ctx)
    load(k, [(cs[:, i], c) for i, c in enumerate(conds)] + [(nb[:], norm.partition_broadcast(P))]
         + [(bb[:, i], bias[at * D:(at + 1) * D].partition_broadcast(P)) for i, (at, _) in enumerate(want)],
         ahead=[src for at, _ in want for src in columns(w, at * D, (at + 1) * D)])
    with nc.Block() as block:
        @block.scalar
        def _(act):
            nc.scalar.activation(cs[:], cs[:], ACT.Silu).then_inc(*k.act_done.up())

        @block.vector
        def _(dve):
            dve.wait_ge(*k.act_done.now())
            for i in range(len(conds)):
                nc.vector.tensor_copy(cb[:, i], cs[:, i].unsqueeze(2).to_broadcast([P, DC, P])).then_inc(
                    *k.dve_done.up())

    def evac(i, kind, dst, col):
        b = bb[:, i, col:col + 256]

        def run(bank, link):
            o = dst[:, col:col + 256]
            if kind != "gain":
                return nc.vector.tensor_tensor(o, bank[:, 0:256], b, ALU.add)
            link(nc.vector.scalar_tensor_tensor(o, bank[:, 0:256], 1.0, b, ALU.add, ALU.add))
            return nc.vector.tensor_tensor(o, o, nb[:, col:col + 256], ALU.mult)
        return run

    jobs = []
    for i, (at, kinds) in enumerate(want):
        for n, src in enumerate(columns(w, at * D, (at + 1) * D)):
            for q, (kind, dst) in enumerate(kinds):
                jobs.append((src if q == 0 else None, "row", cb[:, q], "v", evac(i, kind, dst, n * 256)))
    gemm(k, jobs, then=then)


def transpose_tokens(k, src, dst, pe_wait, block):
    nc = k.nc

    @block.tensor
    def _(pe):
        pe.wait_ge(*pe_wait)
        for b in range(4):
            for i in range(4):
                c, t = 2 * b + i // 2, i % 2
                mm = nc.tensor.transpose(k.ps[:, b, i * P:(i + 1) * P], src[:, t, c * P:(c + 1) * P], k.c("ident"))
            mm.then_inc(*k.pe_done.up())

    @block.vector
    def _(dve):
        for b in range(4):
            dve.wait_ge(k.pe_done.sem, k.pe_done.n - 3 + b)
            nc.vector.tensor_copy(dst[:, 2 * b:2 * b + 2, :],
                                  k.ps[:, b, :].rearrange("p (c n) -> p c n", c=2)).then_inc(*k.dve_done.up())


def norm_modulate(k, src, gain, shift, h, hT, sq):
    nc = k.nc
    ss = k.stat[:, 0:TT]
    with nc.Block() as block:
        @block.scalar
        def _(act):
            for t in range(TT):
                nc.scalar.activation(sq[:, t, :], src[:, t, :], ACT.Square,
                                     accum_out=ss[:, t:t + 1]).then_inc(*k.act_done.up())

        @block.vector
        def _(dve):
            dve.wait_ge(*k.act_done.now())
            nc.vector.tensor_scalar(ss, ss, 1.0 / D, EPS, ALU.mult, ALU.add).then_inc(*k.dve_done.up())

        @block.scalar
        def _(act):
            act.wait_ge(*k.dve_done.now())
            nc.scalar.activation(ss, ss, ACT.Sqrt).then_inc(*k.act_done.up())

        @block.vector
        def _(dve):
            def link(ins):
                ins.then_inc(*k.dve_done.up())
                dve.wait_ge(*k.dve_done.now())

            dve.wait_ge(*k.act_done.now())
            link(nc.vector.reciprocal(ss, ss))
            for t in range(TT):
                link(nc.vector.scalar_tensor_tensor(h[:, t, :], src[:, t, :], ss[:, t:t + 1], gain,
                                                    ALU.mult, ALU.mult) if gain is not None else
                     nc.vector.tensor_scalar(h[:, t, :], src[:, t, :], ss[:, t:t + 1], None, ALU.mult))
                if shift is not None:
                    link(nc.vector.tensor_tensor(h[:, t, :], h[:, t, :], shift, ALU.add))

        if hT is not None:
            transpose_tokens(k, h, hT, k.dve_done.now(), block)


def add_to_x(k, gate):
    def at(col):
        def run(bank, link):
            b = bank.rearrange("p (t n) -> p t n", t=TT)
            link(k.nc.vector.tensor_tensor(b, b, gate[:, col:col + 256].unsqueeze(1).to_broadcast([P, TT, 256]),
                                           ALU.mult))
            xs = k.x[:, :, col:col + 256]
            return k.nc.vector.tensor_tensor(xs, b, xs, ALU.add)
        return run
    return at


def copy_tok(k, dst, col, eng, func=None):
    def run(bank, link):
        n = min(256, dst.shape[2] - col)
        b = bank[:, 0:TT * n].rearrange("p (t n) -> p t n", t=TT)
        o = dst[:, :, col:col + n]
        if func is not None:
            return k.nc.scalar.activation(o, b, func)
        return k.nc.vector.tensor_copy(o, b) if eng == "v" else k.nc.scalar.copy(o, b)
    return run


def copy_feat(k, dst, chunk, eng):
    def run(bank, link):
        b = bank.rearrange("p (c n) -> p c n", c=2)
        o = dst[:, chunk:chunk + 2, :]
        return k.nc.vector.tensor_copy(o, b) if eng == "v" else k.nc.scalar.copy(o, b)
    return run


def feat_pad(k, dst, pair):
    def run(bank, link):
        b = bank.rearrange("p (c n) -> p c n", c=2)
        link(k.nc.vector.tensor_copy(dst[0:64, pair:pair + 2, 0, :], b[0:64]))
        return k.nc.vector.tensor_copy(dst[64:128, pair:pair + 2, 1, :], b[64:128])
    return run


def even_mixer(k):
    nc, I = k.nc, k.ins
    with ExitStack() as ctx:
        sb = lambda name, shape, dt=F32: k.sb(name, shape, dt, ctx)
        fq = sb("fq", [P, 4, 2, S])
        fk = sb("fk", [P, 4, S])
        fv = sb("fv", [P, TT, 512])
        gv = sb("gv", [P, TT, 512])
        gg = sb("gg", [P, TT, 512])
        gq = sb("gq", [P, 2, S])
        gk = sb("gk", [P, 2, S])
        mix = sb("mix", [P, TT, D])
        wsm = sb("wsm", [P, DC, 24])
        fb = sb("fb", [P, 8])
        w2 = sb("w2", [16, 256])
        b2 = sb("b2", [P, 2])
        logf = sb("logf", [P, TT, 8])
        lf1 = sb("lf1", [P, TT, 8])
        glrT = sb("glrT", [16, S])
        la = sb("la", [P, 2, S])
        la1 = sb("la1", [P, 2, S])
        gn = sb("gn", [P, P])
        load(k, [(wsm[:], I["w_small"].rearrange("(c p) n -> p c n", p=P)), (fb[:], I["e_fox_fb"].partition_broadcast(P)),
                 (w2[:], I["e_gla_w2"]), (b2[:], I["e_gla_b2"]),
                 (gn[:], I["e_gla_norm"].partition_broadcast(P))])
        with nc.Block() as block:
            @block.vector
            def _(dve):
                nc.vector.memset(fq[:], 0.0).then_inc(*k.dve_done.up())

        W = I["e_w_in"]
        jobs = []
        for n, src in enumerate(columns(W, 0, 512)):
            jobs.append((src, "feat", k.hT, "v", feat_pad(k, fq, 2 * n)))
        for n, src in enumerate(columns(W, 512, 1024)):
            jobs.append((src, "feat", k.hT, "s", copy_feat(k, fk, 2 * n, "s")))
        for n, src in enumerate(columns(W, 1024, 1536)):
            jobs.append((src, "tok", k.hT, "v", copy_tok(k, fv, n * 256, "v")))
        jobs.append((columns(W, 1544, 1800)[0], "feat", k.hT, "s", copy_feat(k, gq, 0, "s")))
        jobs.append((columns(W, 1800, 2056)[0], "feat", k.hT, "s", copy_feat(k, gk, 0, "s")))
        for n, src in enumerate(columns(W, 2056, 2568)):
            jobs.append((src, "tok", k.hT, "v", copy_tok(k, gv, n * 256, "v")))
        for n, src in enumerate(columns(W, 2568, 3080)):
            jobs.append((src, "tok", k.hT, "s", copy_tok(k, gg, n * 256, "s", ACT.Silu)))
        gemm(k, jobs)

        def log_sigmoid(block, z, scratch):
            @block.vector
            def _(dve):
                def link(ins):
                    ins.then_inc(*k.dve_done.up())
                    dve.wait_ge(*k.dve_done.now())
                link(nc.vector.scalar_tensor_tensor(scratch, z, -1.0, z, ALU.mult, ALU.max))

            @block.scalar
            def _(act):
                act.wait_ge(*k.dve_done.now())
                nc.scalar.activation(scratch, scratch, ACT.Exp, scale=-1.0).then_inc(*k.act_done.up())
                act.wait_ge(*k.act_done.now())
                nc.scalar.activation(scratch, scratch, ACT.Ln, bias=1.0).then_inc(*k.act_done.up())

            @block.vector
            def _(dve):
                dve.wait_ge(*k.act_done.now())
                nc.vector.scalar_tensor_tensor(z, z, 0.0, scratch, ALU.min, ALU.subtract).then_inc(*k.dve_done.up())
                dve.wait_ge(*k.dve_done.now())

        with nc.Block() as block:
            @block.tensor
            def _(pe):
                for t in range(TT):
                    for c in range(DC):
                        nc.tensor.matmul(k.ps[:, 0, 8 * t:8 * t + 8], k.hT[:, c, t * P:(t + 1) * P], wsm[:, c, 0:8],
                                         start=(c == 0), stop=(c == DC - 1))
                for c in range(DC):
                    mm = nc.tensor.matmul(k.ps[0:16, 1, 0:S], wsm[:, c, 8:24], k.hT[:, c, :],
                                          start=(c == 0), stop=(c == DC - 1))
                mm.then_inc(*k.pe_done.up())

            @block.vector
            def _(dve):
                dve.wait_ge(*k.pe_done.now())
                nc.vector.tensor_tensor(logf[:], k.ps[:, 0, 0:16].rearrange("p (t n) -> p t n", t=TT),
                                        fb[:].unsqueeze(1).to_broadcast([P, TT, 8]), ALU.add).then_inc(*k.dve_done.up())
                nc.vector.tensor_copy(glrT[:], k.ps[0:16, 1, 0:S]).then_inc(*k.dve_done.up())

            @block.tensor
            def _(pe):
                pe.wait_ge(*k.dve_done.now())
                for c in range(2):
                    mm = nc.tensor.matmul(k.ps[:, 2, c * S:(c + 1) * S], w2[:, c * P:(c + 1) * P], glrT[:],
                                          start=True, stop=True)
                mm.then_inc(*k.pe_done.up())

            @block.vector
            def _(dve):
                dve.wait_ge(*k.pe_done.now())
                for c in range(2):
                    nc.vector.tensor_scalar(la[:, c, :], k.ps[:, 2, c * S:(c + 1) * S], b2[:, c:c + 1], None,
                                            ALU.add).then_inc(*k.dve_done.up())
                dve.wait_ge(*k.dve_done.now())

            log_sigmoid(block, logf[:], lf1[:])
            log_sigmoid(block, la[:], la1[:])

        fox_attention(k, ctx, fq, fk, fv, logf, mix)
        gla_attention(k, ctx, gq, gk, gv, gg, la, gn, mix)

        with nc.Block() as block:
            transpose_tokens(k, mix, k.hT, k.dve_done.now(), block)
        add = add_to_x(k, k.gate)
        gemm(k, [(src, "tok", k.hT, "v", add(n * 256)) for n, src in enumerate(columns(I["e_w_o"], 0, D))])


def fox_attention(k, ctx, fq, fk, fv, logf, mix):
    nc = k.nc
    H = 8
    cum = k.sb("fox_cum", [1, H, S], ctx=ctx)
    ncum = k.sb("fox_ncum", [1, H, S], ctx=ctx)
    sm = k.sb("fox_sm", [P, 2, 384], ctx=ctx)
    pT = k.sb("fox_pT", [P, 2, 384], ctx=ctx)
    mx = k.sb("fox_mx", [P, 2, 2], ctx=ctx)
    rs = k.sb("fox_rs", [P, 2, 2], ctx=ctx)
    sem = lambda n: Signal(k.sem(n))
    scores_ready, masked, probs_ready, turned, turned_copied, out_ready, out_copied = map(
        sem, ("fox_scores", "fox_masked", "fox_probs", "fox_turned", "fox_turned_copied", "fox_out", "fox_out_copied"))

    with nc.Block() as block:
        @block.tensor
        def _(pe):
            for h in range(H):
                o = k.ps[0:1, h // 2, h % 2 * S:h % 2 * S + S]
                nc.tensor.matmul(o[:, 0:P], logf[:, 0, h:h + 1], k.c("upto"), start=True, stop=True)
                nc.tensor.matmul(o[:, P:S], logf[:, 0, h:h + 1], k.c("ones")[:, 0:P], start=True, stop=False)
                mm = nc.tensor.matmul(o[:, P:S], logf[:, 1, h:h + 1], k.c("upto"), start=False, stop=True)
            mm.then_inc(*k.pe_done.up())

        @block.vector
        def _(dve):
            dve.wait_ge(*k.pe_done.now())
            src = k.ps[0:1, 0:4, :].rearrange("p b (h n) -> p (b h) n", h=2)
            nc.vector.tensor_copy(cum[:], src).then_inc(*k.dve_done.up())
            nc.vector.tensor_scalar(ncum[:], src, -1.0, None, ALU.mult).then_inc(*k.dve_done.up())
            dve.wait_ge(*k.dve_done.now())
            nc.vector.tensor_scalar(fq[:], fq[:], 0.125, None, ALU.mult).then_inc(*k.dve_done.up())

    keys = lambda t: (t + 1) * P
    with nc.Block() as block:
        @block.tensor
        def _(pe):
            def scores(h):
                if h >= 2:
                    pe.wait_ge(masked.sem, h - 1)
                for t in range(TT):
                    o = k.ps[:, h % 2, t * P:t * P + keys(t)]
                    nc.tensor.matmul(o, fq[:, h // 2, h % 2, t * P:(t + 1) * P], fk[:, h // 2, 0:keys(t)],
                                     start=True, stop=False)
                    nc.tensor.matmul(o, cum[:, h, t * P:(t + 1) * P], k.c("ones")[0:1, 0:keys(t)],
                                     start=False, stop=False)
                    mm = nc.tensor.matmul(o, k.c("ones")[0:1, 0:P], ncum[:, h, 0:keys(t)], start=False, stop=True)
                mm.then_inc(*scores_ready.up())

            def turn(h):
                pe.wait_ge(probs_ready.sem, h + 1)
                if h >= 2:
                    pe.wait_ge(turned_copied.sem, h - 1)
                for i in range(3):
                    mm = nc.tensor.transpose(k.ps[:, 2 + h % 2, i * P:(i + 1) * P], sm[:, h % 2, i * P:(i + 1) * P],
                                             k.c("ident"))
                mm.then_inc(*turned.up())

            def values(h):
                pe.wait_ge(turned_copied.sem, h + 1)
                if h >= 2:
                    pe.wait_ge(out_copied.sem, h - 1)
                v = lambda t: fv[:, t, h * 64:(h + 1) * 64]
                b = k.ps[:, 4 + h % 2, :]
                nc.tensor.matmul(b[:, 0:64], pT[:, h % 2, 0:P], v(0), start=True, stop=True)
                nc.tensor.matmul(b[:, 64:128], pT[:, h % 2, P:2 * P], v(0), start=True, stop=False)
                nc.tensor.matmul(b[:, 64:128], pT[:, h % 2, 2 * P:3 * P], v(1), start=False,
                                 stop=True).then_inc(*out_ready.up())

            for i in range(H + 2):
                if i < H:
                    scores(i)
                if 1 <= i <= H:
                    turn(i - 1)
                if i >= 2:
                    values(i - 2)

        @block.vector
        def _(dve):
            def link(ins):
                ins.then_inc(*k.dve_done.up())
                dve.wait_ge(*k.dve_done.now())

            def mask(h):
                dve.wait_ge(scores_ready.sem, h + 1)
                if h >= 2:
                    dve.wait_ge(turned.sem, h - 1)
                b, m = k.ps[:, h % 2, :], k.c("fox_mask")
                nc.vector.tensor_tensor(sm[:, h % 2, 0:P], b[:, 0:P], m, ALU.add).then_inc(*k.dve_done.up())
                nc.vector.tensor_copy(sm[:, h % 2, P:2 * P], b[:, P:2 * P]).then_inc(*k.dve_done.up())
                link(nc.vector.tensor_tensor(sm[:, h % 2, 2 * P:3 * P], b[:, 2 * P:3 * P], m, ALU.add))
                link(nc.vector.tensor_reduce(mx[:, h % 2, 0:1], sm[:, h % 2, 0:P], AX.X, ALU.max))
                link(nc.vector.tensor_reduce(mx[:, h % 2, 1:2], sm[:, h % 2, P:3 * P], AX.X, ALU.max))
                nc.vector.tensor_scalar(mx[:, h % 2, :], mx[:, h % 2, :], -1.0, None, ALU.mult).then_inc(*masked.up())

            def copy_turned(h):
                dve.wait_ge(turned.sem, h + 1)
                if h >= 2:
                    dve.wait_ge(out_ready.sem, h - 1)
                nc.vector.tensor_copy(pT[:, h % 2, :], k.ps[:, 2 + h % 2, 0:384]).then_inc(*turned_copied.up())

            def copy_out(h):
                dve.wait_ge(out_ready.sem, h + 1)
                dve.wait_ge(probs_ready.sem, h + 1)
                link(nc.vector.reciprocal(rs[:, h % 2, :], rs[:, h % 2, :]))
                for t in range(TT):
                    ins = nc.vector.tensor_scalar(mix[:, t, h * 64:(h + 1) * 64],
                                                  k.ps[:, 4 + h % 2, t * 64:(t + 1) * 64],
                                                  rs[:, h % 2, t:t + 1], None, ALU.mult)
                    if t == 0:
                        link(ins)
                ins.then_inc(*out_copied.up())

            for i in range(H + 2):
                if i < H:
                    mask(i)
                if 1 <= i <= H:
                    copy_turned(i - 1)
                if i >= 2:
                    copy_out(i - 2)

        @block.scalar
        def _(act):
            for h in range(H):
                act.wait_ge(masked.sem, h + 1)
                if h >= 2:
                    act.wait_ge(out_copied.sem, h - 1)
                nc.scalar.activation(sm[:, h % 2, 0:P], sm[:, h % 2, 0:P], ACT.Exp, bias=mx[:, h % 2, 0:1],
                                     accum_out=rs[:, h % 2, 0:1]).then_inc(*k.act_done.up())
                nc.scalar.activation(sm[:, h % 2, P:3 * P], sm[:, h % 2, P:3 * P], ACT.Exp, bias=mx[:, h % 2, 1:2],
                                     accum_out=rs[:, h % 2, 1:2]).then_inc(*probs_ready.up())


def gla_attention(k, ctx, gq, gk, gv, gg, la, gn, mix):
    nc = k.nc
    sb = lambda name, shape: k.sb(name, shape, ctx=ctx)
    b = sb("gla_b", [P, 8, C64])
    e1 = sb("gla_e1", [P, 8, C64])
    e2 = sb("gla_e2", [P, 8, C64])
    qin = sb("gla_qin", [P, 2, 2, S])
    qst = sb("gla_qst", [P, 2, 2, S])
    kin = sb("gla_kin", [P, 2, S])
    kst = sb("gla_kst", [P, 2, S])
    kpad = sb("gla_kpad", [P, TT, 2, 2, 2, P])
    att = sb("gla_att", [P, TT, 4, P])
    state = sb("gla_state", [P, 2, P])
    el = sb("gla_el", [P, 8])
    o = sb("gla_o", [P, TT, 4, P])
    sq = sb("gla_sq", [P, TT, 4, P])
    ss = sb("gla_ss", [P, TT * 4])
    g8 = lambda ap: ap.rearrange("p a (c n) -> p (a c) n", n=C64)
    cb = lambda ap: ap.to_broadcast([P, 8, C64])

    with nc.Block() as block:
        def dve_link(dve):
            def link(ins):
                ins.then_inc(*k.dve_done.up())
                dve.wait_ge(*k.dve_done.now())
            return link

        @block.vector
        def _(dve):
            link = dve_link(dve)
            nc.vector.memset(qin[:], 0.0).then_inc(*k.dve_done.up())
            nc.vector.memset(qst[:], 0.0).then_inc(*k.dve_done.up())
            nc.vector.memset(kpad[:], 0.0).then_inc(*k.dve_done.up())
            nc.vector.memset(state[:], 0.0).then_inc(*k.dve_done.up())
            link(nc.vector.tensor_scalar(la[:], la[:], 1.0 / 16.0, None, ALU.mult))
            link(nc.vector.tensor_tensor_scan(b[:].rearrange("p a n -> p (a n)"), k.c("reset"),
                                              la[:].rearrange("p a n -> p (a n)"), 0.0, ALU.mult, ALU.add))
            link(nc.vector.tensor_tensor(e1[:], b[:], cb(b[:, :, 31:32]), ALU.subtract))
            link(nc.vector.tensor_scalar(e2[:], e1[:], -1.0, 43.0, ALU.mult, ALU.min))
            link(nc.vector.tensor_scalar(e1[:], e1[:], 43.0, None, ALU.min))

        @block.scalar
        def _(act):
            act.wait_ge(*k.dve_done.now())
            nc.scalar.activation(e1[:], e1[:], ACT.Exp).then_inc(*k.act_done.up())
            nc.scalar.activation(e2[:], e2[:], ACT.Exp).then_inc(*k.act_done.up())
            nc.scalar.activation(el[:], b[:, :, 63], ACT.Exp).then_inc(*k.act_done.up())

        def scaled_q(dst, e):
            for h in range(2):
                r = slice(64 * h, 64 * h + 64)
                for p in range(2):
                    nc.vector.scalar_tensor_tensor(
                        dst[r, p, h, :], gq[r, p, :], 0.125, e[r, 4 * p:4 * p + 4, :].rearrange("p a n -> p (a n)"),
                        ALU.mult, ALU.mult).then_inc(*k.dve_done.up())

        @block.vector
        def _(dve):
            link = dve_link(dve)
            dve.wait_ge(*k.act_done.now())
            scaled_q(qin, e1)
            link(nc.vector.tensor_tensor(g8(kin[:]), g8(gk[:]), e2[:], ALU.mult))
            link(nc.vector.tensor_tensor(e2[:], cb(b[:, :, 63:64]), b[:], ALU.subtract))

        @block.scalar
        def _(act):
            act.wait_ge(*k.dve_done.now())
            nc.scalar.activation(e1[:], b[:], ACT.Exp).then_inc(*k.act_done.up())
            nc.scalar.activation(e2[:], e2[:], ACT.Exp).then_inc(*k.act_done.up())

        @block.vector
        def _(dve):
            link = dve_link(dve)
            dve.wait_ge(*k.act_done.now())
            scaled_q(qst, e1)
            link(nc.vector.tensor_tensor(g8(kst[:]), g8(gk[:]), e2[:], ALU.mult))

        @block.tensor
        def _(pe):
            pe.wait_ge(*k.dve_done.now())
            for t in range(TT):
                for h in range(4):
                    mm = nc.tensor.matmul(k.ps[:, t, h * P:(h + 1) * P], kin[:, h // 2, t * P:(t + 1) * P],
                                          qin[:, h // 2, h % 2, t * P:(t + 1) * P], start=True, stop=True)
                mm.then_inc(*k.pe_done.up())
            for t in range(TT):
                for p in range(2):
                    i = t * 2 + p
                    mm = nc.tensor.transpose(k.ps[:, 2, i * P:(i + 1) * P], kst[:, p, t * P:(t + 1) * P], k.c("ident"))
            mm.then_inc(*k.pe_done.up())

        @block.vector
        def _(dve):
            link = dve_link(dve)
            dve.wait_ge(*k.pe_done.now())
            for t in range(TT):
                nc.vector.tensor_tensor(att[:, t], k.ps[:, t, :].rearrange("p (h n) -> p h n", h=4),
                                        k.c("incl").unsqueeze(1).to_broadcast([P, 4, P]),
                                        ALU.mult).then_inc(*k.dve_done.up())
            for t in range(TT):
                for cc in range(2):
                    for h in range(2):
                        r = slice(64 * cc, 64 * cc + 64)
                        src = k.ps[r, 2, t * 256:(t + 1) * 256].rearrange("p (a n) -> p a n", a=2)
                        nc.vector.tensor_copy(kpad[r, t, cc, :, h, 64 * h:64 * h + 64],
                                              src[:, :, 64 * h:64 * h + 64]).then_inc(*k.dve_done.up())

        for c in range(4):
            t, cc = c // 2, c % 2

            @block.tensor
            def _(pe):
                pe.wait_ge(*k.dve_done.now())
                for h in range(4):
                    out = k.ps[64 * cc:64 * cc + 64, 4 + t, h * P:(h + 1) * P]
                    nc.tensor.matmul(out, qst[:, h // 2, h % 2, c * 64:(c + 1) * 64], state[:, h // 2, :],
                                     start=True, stop=False)
                    nc.tensor.matmul(out, att[:, t, h, 64 * cc:64 * cc + 64], gv[:, t, h * P:(h + 1) * P],
                                     start=False, stop=True)
                for p in range(2):
                    for h in range(2):
                        mm = nc.tensor.matmul(k.ps[:, 6, p * P:(p + 1) * P], kpad[:, t, cc, p, h, :],
                                              gv[:, t, (2 * p + h) * P:(2 * p + h + 1) * P],
                                              start=(h == 0), stop=(h == 1))
                mm.then_inc(*k.pe_done.up())

            @block.vector
            def _(dve):
                dve.wait_ge(*k.pe_done.now())
                for p in range(2):
                    nc.vector.scalar_tensor_tensor(state[:, p, :], state[:, p, :], el[:, 4 * p + c:4 * p + c + 1],
                                                   k.ps[:, 6, p * P:(p + 1) * P], ALU.mult,
                                                   ALU.add).then_inc(*k.dve_done.up())
                if cc:
                    nc.vector.tensor_copy(o[:, t], k.ps[:, 4 + t, :].rearrange("p (h n) -> p h n", h=4)).then_inc(
                        *k.dve_done.up())

        @block.scalar
        def _(act):
            act.wait_ge(*k.dve_done.now())
            nc.scalar.activation(sq[:], o[:], ACT.Square).then_inc(*k.act_done.up())

        @block.vector
        def _(dve):
            link = dve_link(dve)
            dve.wait_ge(*k.act_done.now())
            link(nc.vector.tensor_reduce(ss[:], sq[:].rearrange("p t h n -> p (t h) n"), AX.X, ALU.add))
            link(nc.vector.tensor_scalar(ss[:], ss[:], 1.0 / P, EPS, ALU.mult, ALU.add))

        @block.scalar
        def _(act):
            act.wait_ge(*k.dve_done.now())
            nc.scalar.activation(ss[:], ss[:], ACT.Sqrt).then_inc(*k.act_done.up())

        @block.vector
        def _(dve):
            link = dve_link(dve)
            dve.wait_ge(*k.act_done.now())
            link(nc.vector.reciprocal(ss[:], ss[:]))
            o8 = o[:].rearrange("p t h n -> p (t h) n")
            link(nc.vector.tensor_tensor(o8, o8, ss[:].unsqueeze(2).to_broadcast([P, 8, P]), ALU.mult))
            link(nc.vector.tensor_tensor(o8, o8, gn[:].unsqueeze(1).to_broadcast([P, 8, P]), ALU.mult))
            for t in range(TT):
                link(nc.vector.tensor_tensor(mix[:, t, 512:D], o[:, t].rearrange("p h n -> p (h n)"), gg[:, t, :],
                                             ALU.mult))


def feed_forward(k, w_gate, w_up, w_down, gates, acc, ctx, tag):
    nc = k.nc
    E = w_gate.shape[0]
    sg = k.sb(f"sg_{tag}", [P, 2, 2, S], ctx=ctx)
    prod = k.sb(f"prod_{tag}", [P, 2, 2, S], ctx=ctx)
    up0, silu0, prod0, down0, free0 = (s.n for s in (k.up_ready, k.silu_ready, k.prod_ready, k.down_used, k.y_free))
    land0 = [s.n for s in k.landed]
    per = min(E, 2)
    steps = per * FF_STEPS
    turns = E // per
    wv = {"g": w_gate.rearrange("e (c p) n -> e p c n", p=P), "u": w_up.rearrange("e (c p) n -> e p c n", p=P),
          "d": w_down.rearrange("e (c p) n -> e p c n", p=P)}

    def over_turns(eng, body):
        if turns == 1:
            body(0)
        else:
            with eng.Fori(0, turns) as i:
                body(i)

    loads_before = lambda n: (n + 1) // 2

    with nc.Block() as block:
        @block.sync
        def _(sp):
            def body(i):
                for n in range(steps):
                    e, s = i * per + n // FF_STEPS, n % FF_STEPS
                    past = turns > 1 or n >= 2
                    if past:
                        sp.wait_ge(k.up_ready.sem, i * steps + (up0 + n - 1))
                    for kind, at in (("g", 0), ("u", 2)):
                        dst = k.ring[:, at + n % 2, :].rearrange("p (c n) -> p c n", c=DC)
                        sp.dma_start(dst, wv[kind][e, :, :, s * 256:(s + 1) * 256]).then_inc(
                            k.landed[at + n % 2].sem, 16)
                    if past:
                        sp.wait_ge(k.down_used.sem, i * steps + (down0 + n - 1))
                    dst = k.ring[:, 4 + n % 2, :].rearrange("p (c n) -> p c n", c=2)
                    sp.dma_start(dst, wv["d"][e, :, 2 * s:2 * s + 2, :]).then_inc(k.landed[4 + n % 2].sem, 16)
            over_turns(sp, body)

        @block.tensor
        def _(pe):
            def body(i):
                def landed(slot, n):
                    pe.wait_ge(k.landed[slot].sem, i * (16 * (steps // 2)) + (land0[slot] + 16 * (n // 2 + 1)))

                def hidden(n):
                    landed(n % 2, n)
                    landed(2 + n % 2, n)
                    if turns > 1 or n >= 2:
                        pe.wait_ge(k.prod_ready.sem, i * steps + (prod0 + n - 1))
                    for at, b in ((0, 0), (2, 1)):
                        w = k.ring[:, at + n % 2, :].rearrange("p (c n) -> p c n", c=DC)
                        for f in range(2):
                            for c in range(DC):
                                mm = nc.tensor.matmul(k.ps[:, 2 * (n % 2) + b, f * S:(f + 1) * S],
                                                      w[:, c, f * P:(f + 1) * P], k.hT[:, c, :],
                                                      start=(c == 0), stop=(c == DC - 1))
                    mm.then_inc(k.up_ready.sem, 1)

                def down(n):
                    s = n % FF_STEPS
                    landed(4 + n % 2, n)
                    pe.wait_ge(k.prod_ready.sem, i * steps + (prod0 + n + 1))
                    if s == 0 and (turns > 1 or n):
                        pe.wait_ge(k.y_free.sem, i * per + (free0 + n // FF_STEPS))
                    w = k.ring[:, 4 + n % 2, :].rearrange("p (c n) -> p c n", c=2)
                    for t in range(TT):
                        for half in range(2):
                            for f in range(2):
                                mm = nc.tensor.matmul(k.ps[:, 4 + 2 * t + half, :], prod[:, n % 2, f, t * P:(t + 1) * P],
                                                      w[:, f, half * 512:(half + 1) * 512],
                                                      start=(s == 0 and f == 0), stop=(s == FF_STEPS - 1 and f == 1))
                    mm.then_inc(k.down_used.sem, 1)

                for n in range(steps):
                    hidden(n)
                    if n:
                        down(n - 1)
                down(steps - 1)
            over_turns(pe, body)

        @block.scalar
        def _(act):
            def body(i):
                for n in range(steps):
                    act.wait_ge(k.up_ready.sem, i * steps + (up0 + n + 1))
                    if turns > 1 or n >= 2:
                        act.wait_ge(k.prod_ready.sem, i * steps + (prod0 + n - 1))
                    nc.scalar.activation(sg[:, n % 2], k.ps[:, 2 * (n % 2), :].rearrange("p (f n) -> p f n", f=2),
                                         ACT.Silu).then_inc(k.silu_ready.sem, 1)
            over_turns(act, body)

        @block.vector
        def _(dve):
            def body(i):
                for n in range(steps):
                    dve.wait_ge(k.silu_ready.sem, i * steps + (silu0 + n + 1))
                    if turns > 1 or n >= 2:
                        dve.wait_ge(k.down_used.sem, i * steps + (down0 + n - 1))
                    nc.vector.tensor_tensor(prod[:, n % 2], sg[:, n % 2],
                                            k.ps[:, 2 * (n % 2) + 1, :].rearrange("p (f n) -> p f n", f=2),
                                            ALU.mult).then_inc(k.prod_ready.sem, 1)
                    if n % FF_STEPS == FF_STEPS - 1:
                        dve.wait_ge(k.down_used.sem, i * steps + (down0 + n + 1))
                        e = i * per + n // FF_STEPS
                        for t in range(TT):
                            for half in range(2):
                                a = acc[:, t, half * 512:(half + 1) * 512]
                                ins = nc.vector.scalar_tensor_tensor(
                                    a, k.ps[:, 4 + 2 * t + half, :], gates[:, t, bass.ds(e, 1)], a, ALU.mult, ALU.add)
                        ins.then_inc(k.y_free.sem, 1)
            over_turns(dve, body)

    for s in (k.up_ready, k.silu_ready, k.prod_ready, k.down_used):
        s.n += E * FF_STEPS
    k.y_free.n += E
    for i, s in enumerate(k.landed):
        s.n += 16 * turns * ((steps + 1 - i % 2) // 2)
    k.job += (-k.job) % NSLOT


def add_gated(k, acc, gate):
    nc = k.nc
    with nc.Block() as block:
        @block.vector
        def _(dve):
            nc.vector.tensor_tensor(acc[:], acc[:], gate.unsqueeze(1).to_broadcast([P, TT, D]),
                                    ALU.mult).then_inc(*k.dve_done.up())
            dve.wait_ge(*k.dve_done.now())
            nc.vector.tensor_tensor(k.x[:], k.x[:], acc[:], ALU.add).then_inc(*k.dve_done.up())


def even_ffn(k):
    nc, I = k.nc, k.ins
    with ExitStack() as ctx:
        acc = k.sb("ffn_acc", [P, TT, D], ctx=ctx)
        one = k.sb("ffn_one", [P, TT, 1], ctx=ctx)
        with nc.Block() as block:
            @block.vector
            def _(dve):
                nc.vector.memset(acc[:], 0.0).then_inc(*k.dve_done.up())
                nc.vector.memset(one[:], 1.0).then_inc(*k.dve_done.up())
        feed_forward(k, I["e_ffn_gate"], I["e_ffn_up"], I["e_ffn_down"], one, acc, ctx, "ffn")
        add_gated(k, acc, k.gate[:])


def s5_mixer(k):
    nc, I = k.nc, k.ins
    NT = 32
    with ExitStack() as ctx:
        sb = lambda name, shape, dt=F32: k.sb("s5_" + name, shape, dt, ctx)
        uT = sb("uT", [P, DC, S])
        par = sb("par", [P, 3, NT])
        m = {n: sb(n, [P, NT]) for n in ("dt", "mag", "th", "sin", "cos", "den", "nr", "f_re", "f_im", "t0", "t1")}
        ti = sb("ti", [P, NT], I32)
        braw = sb("braw", [P, 2, NT, 16])
        craw = sb("craw", [P, 2, NT, 16])
        cpad = sb("cpad", [P, 2, NT, 32])
        w = sb("w", [P, 2, 2, NT])
        dsk = sb("dsk", [P, DC])
        e_im = sb("e_im", [P, NT, S])
        e_re = k.ring[:].rearrange("p a n -> p (a n)")[:, 0:NT * S].rearrange("p (j n) -> p j n", j=NT)
        spare = k.ring[:].rearrange("p a n -> p (a n)")[:, NT * S:].rearrange("p (a n) -> p a n", a=2)
        tmp_v = spare[:, 0, 0:1024]
        tmp_p = spare[:, 0, 1024:2048]
        bpad = spare[:, 1, 0:1024].rearrange("p (r j n) -> p r j n", r=2, j=4)
        bT = spare[:, 1, 1024:2048].rearrange("p (r j n) -> p r j n", r=2, j=4)
        z = sb("z", [P, 2, 4, S])
        t4 = sb("t4", [P, 2, 4, S])
        load(k, [(par[:], I["s5_par"]), (braw[:], I["s5_b"]), (craw[:], I["s5_c"]), (dsk[:], I["s5_dskip"])])
        V = nc.vector
        tt = lambda o, a, b, op: V.tensor_tensor(o, a, b, op)
        TWO_PI_HI = 6.28125
        TWO_PI_LO = 2 * math.pi - TWO_PI_HI

        def parameters(block):
            @block.scalar
            def _(act):
                nc.scalar.activation(m["dt"][:], par[:, 2, :], ACT.Exp).then_inc(*k.act_done.up())

            @block.vector
            def _(dve):
                link = linker(dve, k.dve_done)
                dve.wait_ge(*k.act_done.now())
                link(tt(m["th"][:], par[:, 1, :], m["dt"][:], ALU.mult))
                link(tt(m["mag"][:], par[:, 0, :], m["dt"][:], ALU.mult))
                for name, turn, quarter in (("sin", 0.0, 0.0), ("cos", 0.25, math.pi / 2)):
                    a, t0 = m[name][:], m["t0"][:]
                    link(V.tensor_scalar(ti[:], m["th"][:], 1 / (2 * math.pi), turn, ALU.mult, ALU.add))
                    link(V.tensor_copy(t0, ti[:]))
                    link(V.scalar_tensor_tensor(a, t0, -TWO_PI_HI, m["th"][:], ALU.mult, ALU.add))
                    link(V.scalar_tensor_tensor(a, t0, -TWO_PI_LO, a, ALU.mult, ALU.add))
                    link(V.tensor_scalar(a, a, quarter, 3.1415925, ALU.add, ALU.min))
                    link(V.tensor_scalar(a, a, -3.1415925, None, ALU.max))

            @block.scalar
            def _(act):
                act.wait_ge(*k.dve_done.now())
                nc.scalar.activation(m["mag"][:], m["mag"][:], ACT.Exp).then_inc(*k.act_done.up())
                nc.scalar.activation(m["sin"][:], m["sin"][:], ACT.Sin).then_inc(*k.act_done.up())
                nc.scalar.activation(m["cos"][:], m["cos"][:], ACT.Sin).then_inc(*k.act_done.up())

            @block.vector
            def _(dve):
                link = linker(dve, k.dve_done)
                dve.wait_ge(*k.act_done.now())
                lre, lim = par[:, 0, :], par[:, 1, :]
                nr, ni, t0, t1, den = (m[x][:] for x in ("nr", "th", "t0", "t1", "den"))
                link(tt(nr, m["mag"][:], m["cos"][:], ALU.mult))
                link(V.tensor_scalar(nr, nr, -1.0, None, ALU.add))
                link(tt(ni, m["mag"][:], m["sin"][:], ALU.mult))
                link(tt(t0, lre, lre, ALU.mult))
                link(tt(t1, lim, lim, ALU.mult))
                link(tt(den, t0, t1, ALU.add))
                link(V.reciprocal(den, den))
                for f, a, b, op in ((m["f_re"][:], nr, ni, ALU.add), (m["f_im"][:], ni, nr, ALU.subtract)):
                    link(tt(t0, a, lre, ALU.mult))
                    link(tt(t1, b, lim, ALU.mult))
                    link(tt(t0, t0, t1, op))
                    link(tt(f, t0, den, ALU.mult))
                fb = lambda f: m[f][:].unsqueeze(2).to_broadcast([P, NT, 16])
                s = [t4[:, 0, a, :].rearrange("p (j n) -> p j n", n=16) for a in range(4)]
                s = [t4[:].rearrange("p r a n -> p (r a n)")[:, i * 512:(i + 1) * 512].rearrange(
                    "p (j n) -> p j n", n=16) for i in range(4)]
                for i, (f, b) in enumerate((("f_re", 0), ("f_im", 1), ("f_re", 1), ("f_im", 0))):
                    link(tt(s[i], fb(f), braw[:, b], ALU.mult))
                link(tt(braw[:, 0], s[0], s[1], ALU.subtract))
                link(tt(braw[:, 1], s[2], s[3], ALU.add))
                link(V.memset(cpad[:], 0.0))
                for r, sign in ((0, 1.0), (1, -1.0)):
                    for g in range(2):
                        q = slice(64 * g, 64 * g + 64)
                        link(V.tensor_scalar(cpad[q, r, :, 16 * g:16 * g + 16], craw[q, r], sign, None, ALU.mult))

        gemm(k, [(src, "feat", k.hT, "s", copy_feat(k, uT, 2 * n, "s"))
                 for n, src in enumerate(columns(I["o_w_in"], 0, D))], parameters)

        with nc.Block() as block:
            @block.vector
            def _(dve):
                link = linker(dve, k.dve_done)
                link(V.memset(bpad, 0.0))
                link(V.memset(e_re[:, :, 0:1], 1.0))
                link(V.memset(e_im[:, :, 0:1], 0.0))
                link(V.tensor_copy(w[:, 0, 0, :], m["cos"][:]))
                link(V.tensor_copy(w[:, 0, 1, :], m["sin"][:]))

            for level in range(8):
                n = 1 << level
                a, b = level % 2, 1 - level % 2

                tiles = min(NT, 1024 // n)
                groups = list(range(0, NT, tiles))
                by_pool = {1: 1, 2: 1, 4: 3}[len(groups)]

                def imaginary(link, eng, tmp, g):
                    wr, wi = (w[:, a, r, g:g + tiles].unsqueeze(2).to_broadcast([P, tiles, n]) for r in range(2))
                    o, t = e_im[:, g:g + tiles, n:2 * n], tmp[:, 0:tiles * n].rearrange("p (j n) -> p j n", j=tiles)
                    link(eng.tensor_tensor(o, e_im[:, g:g + tiles, 0:n], wr, ALU.mult))
                    link(eng.tensor_tensor(t, e_re[:, g:g + tiles, 0:n], wi, ALU.mult))
                    link(eng.tensor_tensor(o, o, t, ALU.add))

                @block.gpsimd
                def _(pool):
                    pool.wait_ge(*k.dve_done.now())
                    for g in groups[:by_pool]:
                        imaginary(linker(pool, k.pool_done), nc.gpsimd, tmp_p, g)

                @block.vector
                def _(dve):
                    link = linker(dve, k.dve_done)
                    for g in groups:
                        wr, wi = (w[:, a, r, g:g + tiles].unsqueeze(2).to_broadcast([P, tiles, n]) for r in range(2))
                        o, t = e_re[:, g:g + tiles, n:2 * n], tmp_v[:, 0:tiles * n].rearrange("p (j n) -> p j n", j=tiles)
                        link(tt(o, e_re[:, g:g + tiles, 0:n], wr, ALU.mult))
                        link(tt(t, e_im[:, g:g + tiles, 0:n], wi, ALU.mult))
                        link(tt(o, o, t, ALU.subtract))
                    for g in groups[by_pool:]:
                        imaginary(link, V, tmp_v, g)
                    wr, wi, t0, t1 = w[:, a, 0, :], w[:, a, 1, :], m["t0"][:], m["t1"][:]
                    link(tt(t0, wr, wr, ALU.mult))
                    link(tt(t1, wi, wi, ALU.mult))
                    link(tt(w[:, b, 0, :], t0, t1, ALU.subtract))
                    link(V.scalar_tensor_tensor(w[:, b, 1, :], wr, 2.0, wi, ALU.mult, ALU.mult))
                    dve.wait_ge(*k.pool_done.now())

        sem = lambda n: Signal(k.sem("s5_" + n))
        b_laid, b_turned, bT_ready, bu_ready, bu_read, z_ready, xr_ready, xi_ready, y_ready, y_read, x_used = map(
            sem, ("b_laid", "b_turned", "bT_ready", "bu_ready", "bu_read", "z_ready", "xr_ready", "xi_ready",
                  "y_ready", "y_read", "x_used"))
        yT = k.hT
        with nc.Block() as block:
            @block.scalar
            def _(act):
                for c in range(DC):
                    if c:
                        act.wait_ge(b_turned.sem, c)
                    for r in range(2):
                        for j in range(4):
                            for g in range(2):
                                q = slice(64 * g, 64 * g + 64)
                                ins = nc.scalar.copy(bpad[q, r, j, 32 * j + 16 * g:32 * j + 16 * g + 16],
                                                     braw[q, r, 4 * c + j, :])
                    ins.then_inc(*b_laid.up())
                    act.wait_ge(b_turned.sem, c + 1)
                    if c:
                        act.wait_ge(bu_ready.sem, c)
                    nc.scalar.copy(bT[:], k.ps[:, 4:6, :].rearrange("p r (j n) -> p r j n", j=4)).then_inc(*bT_ready.up())

            @block.tensor
            def _(pe):
                def prepare(c):
                    pe.wait_ge(b_laid.sem, c + 1)
                    if c:
                        pe.wait_ge(bT_ready.sem, c)
                    for r in range(2):
                        for j in range(4):
                            mm = nc.tensor.transpose(k.ps[:, 4 + r, j * P:(j + 1) * P], bpad[:, r, j, :], k.c("ident"))
                    mm.then_inc(*b_turned.up())
                    pe.wait_ge(bT_ready.sem, c + 1)
                    if c:
                        pe.wait_ge(bu_read.sem, c)
                    for r in range(2):
                        for j in range(4):
                            mm = nc.tensor.matmul(k.ps[:, 2 * r + j // 2, j % 2 * S:j % 2 * S + S], bT[:, r, j, :],
                                                  uT[:, c, :], start=True, stop=True)
                    mm.then_inc(*bu_ready.up())

                def outputs(c):
                    pe.wait_ge(xr_ready.sem, c + 1)
                    pe.wait_ge(xi_ready.sem, c + 1)
                    if c >= 2:
                        pe.wait_ge(y_read.sem, c - 1)
                    for j in range(4):
                        o = k.ps[32 * j:32 * j + 32, 6 + c % 2, 0:S]
                        for r in range(2):
                            mm = nc.tensor.matmul(o, cpad[:, r, 4 * c + j, :], t4[:, r, j, :], start=(r == 0), stop=(r == 1))
                    mm.then_inc(*y_ready.up())

                prepare(0)
                for c in range(DC):
                    if c + 1 < DC:
                        prepare(c + 1)
                    outputs(c)

            flat = lambda ap: ap.rearrange("p a n -> p (a n)")

            @block.vector
            def _(dve):
                link = linker(dve, k.dve_done)
                for c in range(DC):
                    dve.wait_ge(bu_ready.sem, c + 1)
                    br, bi = (flat(k.ps[:, 2 * r:2 * r + 2, :]) for r in range(2))
                    er, ei = flat(e_re[:, 4 * c:4 * c + 4, :]), flat(e_im[:, 4 * c:4 * c + 4, :])
                    zr, zi = flat(z[:, 0]), flat(z[:, 1])
                    if c:
                        dve.wait_ge(xi_ready.sem, c)
                    link(tt(zr, br, er, ALU.mult))
                    link(tt(tmp_v, bi, ei, ALU.mult))
                    link(tt(zr, zr, tmp_v, ALU.add))
                    link(tt(zi, bi, er, ALU.mult))
                    tt(tmp_v, br, ei, ALU.mult).then_inc(*bu_read.up())
                    dve.wait_ge(bu_read.sem, c + 1)
                    link(tt(zi, zi, tmp_v, ALU.subtract))
                    for r in range(2):
                        for j in range(4):
                            V.tensor_tensor_scan(z[:, r, j, :], m["mag"][:, 4 * c + j:4 * c + j + 1].to_broadcast([P, S]),
                                                 z[:, r, j, :], 0.0, ALU.mult, ALU.add).then_inc(*z_ready.up())
                    dve.wait_ge(*z_ready.now())
                    if c:
                        dve.wait_ge(y_ready.sem, c)
                        V.scalar_tensor_tensor(yT[:, c - 1, :], uT[:, c - 1, :], dsk[:, c - 1:c],
                                               k.ps[:, 6 + (c - 1) % 2, 0:S], ALU.mult, ALU.add).then_inc(*y_read.up())
                    xr = flat(t4[:, 0])
                    link(tt(xr, zr, er, ALU.mult))
                    link(tt(tmp_v, zi, ei, ALU.mult))
                    tt(xr, xr, tmp_v, ALU.subtract).then_inc(*xr_ready.up())
                c = DC - 1
                dve.wait_ge(y_ready.sem, DC)
                V.scalar_tensor_tensor(yT[:, c, :], uT[:, c, :], dsk[:, c:c + 1], k.ps[:, 6 + c % 2, 0:S],
                                       ALU.mult, ALU.add).then_inc(*y_read.up())

            @block.gpsimd
            def _(pool):
                link = linker(pool, k.pool_done)
                for c in range(DC):
                    er, ei = flat(e_re[:, 4 * c:4 * c + 4, :]), flat(e_im[:, 4 * c:4 * c + 4, :])
                    zr, zi, xi = flat(z[:, 0]), flat(z[:, 1]), flat(t4[:, 1])
                    pool.wait_ge(z_ready.sem, 8 * (c + 1))
                    if c:
                        pool.wait_ge(y_ready.sem, c)
                    link(nc.gpsimd.tensor_tensor(xi, zi, er, ALU.mult))
                    link(nc.gpsimd.tensor_tensor(tmp_p, zr, ei, ALU.mult))
                    nc.gpsimd.tensor_tensor(xi, xi, tmp_p, ALU.add).then_inc(*xi_ready.up())

        with nc.Block() as block:
            @block.scalar
            def _(act):
                nc.scalar.activation(yT[:], yT[:], ACT.Gelu_apprx_tanh).then_inc(*k.act_done.up())

        def glu(n):
            def run(bank, link):
                b = bank.rearrange("p (c n) -> p c n", c=2)
                return nc.scalar.activation(uT[:, 2 * n:2 * n + 2, :], b, ACT.Sigmoid)
            return run

        gemm(k, [(src, "feat", yT, "s", glu(n)) for n, src in enumerate(columns(I["o_w_glu"], 0, D))],
             then=columns(I["o_w_o"], 0, D))
        with nc.Block() as block:
            @block.vector
            def _(dve):
                tt(uT[:], uT[:], yT[:], ALU.mult).then_inc(*k.dve_done.up())
        add = add_to_x(k, k.gate)
        gemm(k, [(src, "tok", uT, "v", add(n * 256)) for n, src in enumerate(columns(I["o_w_o"], 0, D))])


NE = 8
LIST = 96


def moe(k):
    nc, I = k.nc, k.ins
    V = nc.vector
    with ExitStack() as ctx:
        sb = lambda name, shape, dt=F32: k.sb("moe_" + name, shape, dt, ctx)
        acc = sb("acc", [P, TT, D])
        wr = sb("wr", [P, DC, 8])
        logits = sb("logits", [P, TT, 8])
        top = sb("top", [P, TT, 8])
        idx = sb("idx", [P, TT, 8], U32)
        idf = sb("idf", [P, TT, 8])
        e = sb("e", [P, TT, 1])
        w0 = sb("w0", [P, TT, 1])
        w1 = sb("w1", [P, TT, 1])
        picked = sb("picked", [P, TT, 8])
        gates = sb("gates", [P, TT, NE + 2])
        place = sb("place", [P, TT, NE + 2])
        busy = sb("busy", [P, NE], I32)
        load(k, [(wr[:], I["o_router"].rearrange("(c p) n -> p c n", p=P))])
        with nc.Block() as block:
            @block.tensor
            def _(pe):
                for t in range(TT):
                    for c in range(DC):
                        mm = nc.tensor.matmul(k.ps[:, 0, 8 * t:8 * t + 8], k.hT[:, c, t * P:(t + 1) * P], wr[:, c, :],
                                              start=(c == 0), stop=(c == DC - 1))
                mm.then_inc(*k.pe_done.up())

            @block.vector
            def _(dve):
                def link(ins):
                    ins.then_inc(*k.dve_done.up())
                    dve.wait_ge(*k.dve_done.now())
                dve.wait_ge(*k.pe_done.now())
                link(V.memset(acc[:], 0.0))
                link(V.tensor_copy(logits[:], k.ps[:, 0, 0:16].rearrange("p (t n) -> p t n", t=TT)))
                for t in range(TT):
                    link(V.max(top[:, t, :], logits[:, t, :]))
                    link(V.max_index(idx[:, t, :], top[:, t, :], logits[:, t, :]))
                link(V.tensor_copy(idf[:], idx[:]))
                link(V.tensor_tensor(e[:], top[:, :, 1:2], top[:, :, 0:1], ALU.subtract))

            @block.scalar
            def _(act):
                act.wait_ge(*k.dve_done.now())
                nc.scalar.activation(e[:], e[:], ACT.Exp).then_inc(*k.act_done.up())

            @block.vector
            def _(dve):
                def link(ins):
                    ins.then_inc(*k.dve_done.up())
                    dve.wait_ge(*k.dve_done.now())
                dve.wait_ge(*k.act_done.now())
                link(V.tensor_scalar(w0[:], e[:], 1.0, None, ALU.add))
                link(V.reciprocal(w0[:], w0[:]))
                link(V.tensor_tensor(w1[:], w0[:], e[:], ALU.mult))
                iota = k.c("iota")[:, 0:NE]
                link(V.memset(gates[:], 0.0))
                link(V.memset(place[:], -1.0))
                for t in range(TT):
                    first, second = idf[:, t, 0:1], idf[:, t, 1:2]
                    link(V.tensor_scalar(picked[:, t, :], iota, second, w1[:, t, :], ALU.is_equal, ALU.mult))
                    link(V.tensor_scalar(gates[:, t, 0:NE], iota, first, w0[:, t, :], ALU.is_equal, ALU.mult))
                    link(V.tensor_tensor(gates[:, t, 0:NE], gates[:, t, 0:NE], picked[:, t, :], ALU.add))
                    link(V.tensor_scalar(picked[:, t, :], iota, second, None, ALU.is_equal))
                    link(V.scalar_tensor_tensor(picked[:, t, :], iota, first, picked[:, t, :], ALU.is_equal, ALU.add))

            @block.tensor
            def _(pe):
                pe.wait_ge(*k.dve_done.now())
                ones = k.c("ones")[:, 0:P]
                nc.tensor.matmul(k.ps[:, 1, 0:NE], k.c("upto"), picked[:, 0, :], start=True, stop=True)
                nc.tensor.matmul(k.ps[:, 1, NE:2 * NE], ones, picked[:, 0, :], start=True, stop=False)
                nc.tensor.matmul(k.ps[:, 1, NE:2 * NE], k.c("upto"), picked[:, 1, :], start=False, stop=True)
                nc.tensor.matmul(k.ps[:, 1, 2 * NE:3 * NE], ones, picked[:, 0, :], start=True, stop=False)
                nc.tensor.matmul(k.ps[:, 1, 2 * NE:3 * NE], ones, picked[:, 1, :], start=False, stop=True).then_inc(
                    *k.pe_done.up())

            @block.vector
            def _(dve):
                link = linker(dve, k.dve_done)
                dve.wait_ge(*k.pe_done.now())
                for t in range(TT):
                    link(V.tensor_tensor(place[:, t, 0:NE], picked[:, t, :], k.ps[:, 1, t * NE:(t + 1) * NE], ALU.mult))
                    link(V.tensor_scalar(place[:, t, 0:NE], place[:, t, 0:NE], -1.0, None, ALU.add))
                link(V.tensor_scalar(busy[:], k.ps[:, 1, 2 * NE:3 * NE], float(LIST), None, ALU.is_gt))

        routed_experts(k, I["o_exp_gate"], I["o_exp_up"], I["o_exp_down"], gates, place, busy, acc, ctx)
        add_gated(k, acc, k.gate[:])


def routed_experts(k, w_gate, w_up, w_down, gates, place, busy, acc, ctx):
    nc = k.nc
    V = nc.vector
    sb = lambda name, shape: k.sb("moe_" + name, shape, F32, ctx)
    sg = sb("sg", [P, 2, 2, S])
    prod = sb("prod", [P, 2, 2, S])
    prod_list = sb("prod_list", [P, 2, 2, P])
    h_list = sb("h_list", [P, DC, LIST])
    y_list = sb("y_list", [P, D])
    take = sb("take", [P, TT, LIST])
    give = sb("give", [P, TT, P])
    giveT = sb("giveT", [P, TT, P])
    sem = lambda n: Signal(k.sem("moe_" + n))
    hots_ready, give_turned, list_taken, list_ready, y_kept, spread = map(
        sem, ("hots_ready", "give_turned", "list_taken", "list_ready", "y_kept", "spread"))
    steps = 2 * FF_STEPS
    turns = NE // 2
    wv = {"g": w_gate.rearrange("e (c p) n -> e p c n", p=P), "u": w_up.rearrange("e (c p) n -> e p c n", p=P),
          "d": w_down.rearrange("e (c p) n -> e p c n", p=P)}
    iota = k.c("iota")

    def take_list(bank):
        for c in range(DC):
            o = k.ps[:, bank + c // 4, c % 4 * LIST:(c % 4 + 1) * LIST]
            for t in range(TT):
                mm = nc.tensor.matmul(o, k.h[:, t, c * P:(c + 1) * P], take[:, t, :], start=(t == 0), stop=(t == TT - 1))
        mm.then_inc(list_taken.sem, 1)

    def keep_list(bank):
        nc.scalar.copy(h_list[:].rearrange("p (b c) n -> p b (c n)", b=2),
                       k.ps[:, bank:bank + 2, 0:4 * LIST]).then_inc(list_ready.sem, 1)

    with nc.Block() as block:
        @block.vector
        def _(dve):
            V.memset(prod_list[:], 0.0).then_inc(*spread.up())
            for t in range(TT):
                V.tensor_scalar(take[:, t, :], iota[:, 0:LIST], place[:, t, 0:1], None, ALU.is_equal).then_inc(
                    *k.dve_done.up())

        @block.tensor
        def _(pe):
            pe.wait_ge(*k.dve_done.now())
            take_list(2)
            list_taken.n += 1

        @block.scalar
        def _(act):
            act.wait_ge(*list_taken.now())
            keep_list(2)
            list_ready.n += 1

    up0, silu0, prod0, down0, free0 = (s.n for s in (k.up_ready, k.silu_ready, k.prod_ready, k.down_used, k.y_free))
    land0 = [s.n for s in k.landed]

    with nc.Block() as block:
        @block.sync
        def _(sp):
            with sp.Fori(0, turns) as i:
                def down_weights(n):
                    sp.wait_ge(k.down_used.sem, i * steps + (down0 + n - 1))
                    dst = k.ring[:, 4 + n % 2, :].rearrange("p (c n) -> p c n", c=2)
                    e, s = i * 2 + n // FF_STEPS, n % FF_STEPS
                    sp.dma_start(dst, wv["d"][e, :, 2 * s:2 * s + 2, :]).then_inc(k.landed[4 + n % 2].sem, 16)

                for n in range(steps):
                    e, s = i * 2 + n // FF_STEPS, n % FF_STEPS
                    sp.wait_ge(k.up_ready.sem, i * steps + (up0 + n - 1))
                    for kind, at in (("g", 0), ("u", 2)):
                        dst = k.ring[:, at + n % 2, :].rearrange("p (c n) -> p c n", c=DC)
                        sp.dma_start(dst, wv[kind][e, :, :, s * 256:(s + 1) * 256]).then_inc(
                            k.landed[at + n % 2].sem, 16)
                    if n:
                        down_weights(n - 1)
                down_weights(steps - 1)

        def over_experts(eng, body):
            with eng.Fori(0, turns) as i:
                for q in range(2):
                    long = eng.value_load(busy[0:1, bass.ds(i * 2 + q, 1)], min_val=0, max_val=1)
                    with eng.If(long > 0):
                        body(i, q, False)
                    with eng.Else():
                        body(i, q, True)

        @block.tensor
        def _(pe):
            def body(i, q, short):
                width = LIST if short else S

                def landed(slot, n):
                    pe.wait_ge(k.landed[slot].sem, i * (16 * (steps // 2)) + (land0[slot] + 16 * (n // 2 + 1)))

                def hidden(n):
                    landed(n % 2, n)
                    landed(2 + n % 2, n)
                    pe.wait_ge(k.prod_ready.sem, i * steps + (prod0 + n - 1))
                    for at, b in ((0, 0), (2, 1)):
                        w = k.ring[:, at + n % 2, :].rearrange("p (c n) -> p c n", c=DC)
                        for f in range(2):
                            for c in range(DC):
                                mm = nc.tensor.matmul(k.ps[:, 2 * (n % 2) + b, f * width:(f + 1) * width],
                                                      w[:, c, f * P:(f + 1) * P],
                                                      h_list[:, c, :] if short else k.hT[:, c, :],
                                                      start=(c == 0), stop=(c == DC - 1))
                    mm.then_inc(k.up_ready.sem, 1)

                def down(n):
                    s = n % FF_STEPS
                    landed(4 + n % 2, n)
                    pe.wait_ge(k.prod_ready.sem, i * steps + (prod0 + n + 1))
                    w = k.ring[:, 4 + n % 2, :].rearrange("p (c n) -> p c n", c=2)
                    for t in range(1 if short else TT):
                        for half in range(2):
                            for f in range(2):
                                a = prod_list[:, n % 2, f, :] if short else prod[:, n % 2, f, t * P:(t + 1) * P]
                                mm = nc.tensor.matmul(k.ps[:, 4 + 2 * t + half, :], a,
                                                      w[:, f, half * 512:(half + 1) * 512],
                                                      start=(s == 0 and f == 0), stop=(s == FF_STEPS - 1 and f == 1))
                    mm.then_inc(k.down_used.sem, 1)

                first, last = q * FF_STEPS, (q + 1) * FF_STEPS - 1
                pe.wait_ge(list_ready.sem, i * 2 + (list_ready.n + q))
                hidden(first)
                pe.wait_ge(k.y_free.sem, i * 2 + (free0 + q))
                for n in range(first + 1, last + 1):
                    hidden(n)
                    down(n - 1)
                pe.wait_ge(hots_ready.sem, i * 2 + (q + 1))
                if short:
                    for t in range(TT):
                        mm = nc.tensor.transpose(k.ps[:, 6, t * P:(t + 1) * P], give[:, t, :], k.c("ident"))
                    mm.then_inc(give_turned.sem, 1)
                take_list(2 * (1 - last % 2))
                down(last)
                if short:
                    pe.wait_ge(y_kept.sem, i * 4 + (2 * q + 2))
                    for t in range(TT):
                        for half in range(2):
                            mm = nc.tensor.matmul(k.ps[:, 6 - 2 * t + half, :], giveT[:, t, :],
                                                  y_list[:, half * 512:(half + 1) * 512], start=True, stop=True)
                    mm.then_inc(spread.sem, 1)
                else:
                    pe.sem_inc(give_turned.sem, 1)
                    pe.sem_inc(spread.sem, 1)
            over_experts(pe, body)

        @block.scalar
        def _(act):
            def body(i, q, short):
                width = LIST if short else S
                last = (q + 1) * FF_STEPS - 1
                for n in range(q * FF_STEPS, last + 1):
                    act.wait_ge(k.up_ready.sem, i * steps + (up0 + n + 1))
                    act.wait_ge(k.prod_ready.sem, i * steps + (prod0 + n - 1))
                    nc.scalar.activation(sg[:, n % 2, :, 0:width], k.ps[:, 2 * (n % 2), 0:2 * width].rearrange(
                        "p (f n) -> p f n", f=2), ACT.Silu).then_inc(k.silu_ready.sem, 1)
                if short:
                    act.wait_ge(give_turned.sem, i * 2 + (q + 1))
                    act.wait_ge(spread.sem, i * 2 + (spread.n + q))
                    nc.scalar.copy(giveT[:], k.ps[:, 6, 0:TT * P].rearrange("p (t n) -> p t n", t=TT)).then_inc(
                        y_kept.sem, 1)
                else:
                    act.sem_inc(y_kept.sem, 2)
                act.wait_ge(list_taken.sem, i * 2 + (list_taken.n + q + 1))
                keep_list(2 * (1 - last % 2))
                if short:
                    act.wait_ge(k.down_used.sem, i * steps + (down0 + last + 1))
                    nc.scalar.copy(y_list[:].rearrange("p (b n) -> p b n", b=2), k.ps[:, 4:6, :]).then_inc(y_kept.sem, 1)
            over_experts(act, body)

        @block.vector
        def _(dve):
            def body(i, q, short):
                width = LIST if short else S
                first, last = q * FF_STEPS, (q + 1) * FF_STEPS - 1
                for n in range(first, last + 1):
                    dve.wait_ge(k.silu_ready.sem, i * steps + (silu0 + n + 1))
                    dve.wait_ge(k.down_used.sem, i * steps + (down0 + n - 1))
                    V.tensor_tensor(prod_list[:, n % 2, :, 0:LIST] if short else prod[:, n % 2],
                                    sg[:, n % 2, :, 0:width],
                                    k.ps[:, 2 * (n % 2) + 1, 0:2 * width].rearrange("p (f n) -> p f n", f=2),
                                    ALU.mult).then_inc(k.prod_ready.sem, 1)
                    if n == first:
                        dve.wait_ge(list_taken.sem, i * 2 + (list_taken.n + q))
                        for t in range(TT):
                            V.tensor_scalar(give[:, t, :], iota, place[:, t, bass.ds(i * 2 + q, 1)],
                                            gates[:, t, bass.ds(i * 2 + q, 1)], ALU.is_equal, ALU.mult)
                            ins = V.tensor_scalar(take[:, t, :], iota[:, 0:LIST],
                                                  place[:, t, bass.ds(i * 2 + (q + 1), 1)], None, ALU.is_equal)
                        ins.then_inc(hots_ready.sem, 1)
                dve.wait_ge(k.down_used.sem, i * steps + (down0 + last + 1))
                if short:
                    dve.wait_ge(spread.sem, i * 2 + (spread.n + q + 1))
                for t in range(TT):
                    for half in range(2):
                        a = acc[:, t, half * 512:(half + 1) * 512]
                        if short:
                            ins = V.tensor_tensor(a, k.ps[:, 6 - 2 * t + half, :], a, ALU.add)
                        else:
                            ins = V.scalar_tensor_tensor(a, k.ps[:, 4 + 2 * t + half, :],
                                                         gates[:, t, bass.ds(i * 2 + q, 1)], a, ALU.mult, ALU.add)
                ins.then_inc(k.y_free.sem, 1)
            over_experts(dve, body)

    for s in (k.up_ready, k.silu_ready, k.prod_ready, k.down_used):
        s.n += NE * FF_STEPS
    k.y_free.n += NE
    for s in k.landed:
        s.n += 16 * turns * FF_STEPS
    k.job += (-k.job) % NSLOT


def final_norm(k):
    with ExitStack() as ctx:
        sq = k.sb("fin_sq", [P, TT, D], ctx=ctx)
        load(k, [(k.gain[:], k.ins["final_norm"].partition_broadcast(P))])
        norm_modulate(k, k.x, k.gain[:], None, k.x, None, sq)


LAM_INIT = 0.8 - 0.6 * math.exp(-0.3 * 0)
W_Q, W_K, W_V, W_Z, W_G = 0, D, 2 * D, 3 * D, 3 * D + 3328


def linker(eng, done):
    def link(ins):
        ins.then_inc(*done.up())
        eng.wait_ge(*done.now())
    return link


def hybrid_mixer(k):
    nc, I = k.nc, k.ins
    with ExitStack() as ctx:
        sb = lambda name, shape, dt=F32: k.sb("hy_" + name, shape, dt, ctx)
        oaT = sb("oaT", [P, DC, S])
        obT = sb("obT", [P, DC, S])
        hcT = obT
        with ExitStack() as c2:
            gain_c = k.sb("gain_c", [P, D], ctx=c2)
            shift_c = k.sb("shift_c", [P, D], ctx=c2)
            ctxt = k.sb("ctxt", [P, TT, D], ctx=c2)
            sq = k.sb("hy_sq", [P, TT, D], ctx=c2)
            adaln_rows(k, [I["c_2"], I["c_ctx_2"]], I["w_mod_2"], I["b_mod_2"], I["norm1_g_2"],
                       [(0, [("shift", k.shift), ("shift", shift_c)]), (1, [("gain", k.gain), ("gain", gain_c)]),
                        (2, [("gate", k.gate)])], c2, "mod2a", then=columns(I["w_in_2"], W_Q, W_V))
            load(k, [(ctxt[:], I["ctx_2"].rearrange("(t p) d -> p t d", p=P))])
            norm_modulate(k, ctxt, gain_c[:], shift_c[:], ctxt, hcT, sq)
            norm_modulate(k, k.x, k.gain[:], k.shift[:], k.h, k.hT, sq)
        diff_branch(k, hcT, oaT)
        rwkv_branch(k, hcT, obT)

        ga = sb("ga", [P, DC, S])
        gb = sb("gb", [P, DC, S])
        tmp = sb("tmp", [P, 2, S])

        def sig(dst, n):
            return lambda bank, link: nc.scalar.activation(dst[:, 2 * n:2 * n + 2, :],
                                                           bank.rearrange("p (c n) -> p c n", c=2), ACT.Sigmoid)

        W = I["w_in_2"]
        gemm(k, [(src, "feat", k.hT, "s", sig(dst, n)) for at, dst in ((W_G, ga), (W_G + D, gb))
                 for n, src in enumerate(columns(W, at, at + D))],
             then=columns(I["w_branch_a_2"], 0, D) + columns(I["w_branch_b_2"], 0, D))

        def gated(n, g, add):
            def run(bank, link):
                b, o = bank.rearrange("p (c n) -> p c n", c=2), ga[:, 2 * n:2 * n + 2, :]
                if not add:
                    return nc.vector.tensor_tensor(o, b, o, ALU.mult)
                link(nc.vector.tensor_tensor(tmp[:], b, g[:, 2 * n:2 * n + 2, :], ALU.mult))
                return nc.vector.tensor_tensor(o, o, tmp[:], ALU.add)
            return run

        gemm(k, [(src, "feat", o, "v", gated(n, g, add))
                 for w, o, g, add in (("w_branch_a_2", oaT, ga, False), ("w_branch_b_2", obT, gb, True))
                 for n, src in enumerate(columns(I[w], 0, D))],
             then=columns(I["w_out_2"], 0, D))
        add = add_to_x(k, k.gate)
        gemm(k, [(src, "tok", ga, "v", add(n * 256)) for n, src in enumerate(columns(I["w_out_2"], 0, D))])


def diff_branch(k, hcT, oaT):
    nc, I = k.nc, k.ins
    V = nc.vector
    H = 8
    with ExitStack() as ctx:
        sb = lambda name, shape, dt=F32: k.sb("da_" + name, shape, dt, ctx)
        q = sb("q", [P, TT, D])
        kx = sb("kx", [P, 4, D])
        v = sb("v", [P, 4, D])
        gq = sb("gq", [P, 64])
        gk = sb("gk", [P, 64])
        lam4 = sb("lam4", [P, 4, 64])
        lam = sb("lam", [P, 4])
        og = sb("og", [P, P])
        ss = sb("ss", [P, 32])
        ctx2 = ExitStack()
        sq = k.sb("da_sq", [P, 2, D], ctx=ctx2)
        load(k, [(gq[:], I["q_norm_g_2"].partition_broadcast(P)), (gk[:], I["k_norm_g_2"].partition_broadcast(P)),
                 (lam4[:], I["diff_lambda_2"].partition_broadcast(P)), (og[:], I["diff_out_g_2"].partition_broadcast(P))])
        W = I["w_in_2"]
        jobs = []
        for n, src in enumerate(columns(W, W_Q, W_Q + D)):
            jobs.append((src, "tok", k.hT, "v" if n % 2 else "s", copy_tok(k, q, n * 256, "v" if n % 2 else "s")))
        for at, dst in ((W_K, kx), (W_V, v)):
            for n, src in enumerate(columns(W, at, at + D)):
                jobs.append((src, "tok", k.hT, "v", copy_tok(k, dst[:, 2:4], n * 256, "v")))
                jobs.append((None, "tok", hcT, "s", copy_tok(k, dst[:, 0:2], n * 256, "s")))
        gemm(k, jobs)

        def head_norm(buf, g, n, width):
            groups = TT * D // width
            view = buf.rearrange("p t (g n) -> p (t g) n", n=width)
            with nc.Block() as block:
                @block.scalar
                def _(act):
                    nc.scalar.activation(sq[:], buf, ACT.Square).then_inc(*k.act_done.up())

                @block.vector
                def _(dve):
                    link = linker(dve, k.dve_done)
                    dve.wait_ge(*k.act_done.now())
                    link(V.tensor_reduce(ss[:, 0:groups], sq[:].rearrange("p t (g n) -> p (t g) n", n=width), AX.X, ALU.add))
                    link(V.tensor_scalar(ss[:, 0:groups], ss[:, 0:groups], 1.0 / width, EPS, ALU.mult, ALU.add))

                @block.scalar
                def _(act):
                    act.wait_ge(*k.dve_done.now())
                    nc.scalar.activation(ss[:, 0:groups], ss[:, 0:groups], ACT.Sqrt).then_inc(*k.act_done.up())

                @block.vector
                def _(dve):
                    link = linker(dve, k.dve_done)
                    dve.wait_ge(*k.act_done.now())
                    link(V.reciprocal(ss[:, 0:groups], ss[:, 0:groups]))
                    link(V.tensor_tensor(view, view, ss[:, 0:groups].unsqueeze(2).to_broadcast([P, groups, width]), ALU.mult))
                    link(V.tensor_tensor(view, view, g.unsqueeze(1).to_broadcast([P, groups, width]), ALU.mult))

        head_norm(q[:], gq[:], 64, 64)
        head_norm(kx[:, 0:2], gk[:], 64, 64)
        head_norm(kx[:, 2:4], gk[:], 64, 64)

        with nc.Block() as block:
            @block.vector
            def _(dve):
                link = linker(dve, k.dve_done)
                s4 = sq[:].rearrange("p t n -> p (t n)")
                s = [s4[:, i * 512:(i + 1) * 512].rearrange("p (g a f) -> p g a f", g=16, a=2) for i in range(4)]
                for buf, tiles in ((q, 0), (kx, 2)):
                    for t in range(TT):
                        xs = buf[:, tiles + t, :].rearrange("p (g a h f) -> p g a h f", g=16, a=2, h=2)
                        x1, x2 = xs[:, :, :, 0, :], xs[:, :, :, 1, :]
                        cos, sin = (k.c(n)[:, t * 32:(t + 1) * 32].rearrange("p (a f) -> p a f", a=2).unsqueeze(1)
                                    .to_broadcast([P, 16, 2, 16]) for n in ("rope_cos", "rope_sin"))
                        for o, x, cs in ((s[0], x1, cos), (s[1], x2, sin), (s[2], x2, cos), (s[3], x1, sin)):
                            link(V.tensor_tensor(o, x, cs, ALU.mult))
                        link(V.tensor_tensor(x1, s[0], s[1], ALU.subtract))
                        link(V.tensor_tensor(x2, s[2], s[3], ALU.add))
                link(V.tensor_tensor(lam4[:, 0, :], lam4[:, 0, :], lam4[:, 1, :], ALU.mult))
                link(V.tensor_tensor(lam4[:, 2, :], lam4[:, 2, :], lam4[:, 3, :], ALU.mult))
                link(V.tensor_reduce(lam[:, 0:1], lam4[:, 0, :], AX.X, ALU.add))
                link(V.tensor_reduce(lam[:, 1:2], lam4[:, 2, :], AX.X, ALU.add))

            @block.scalar
            def _(act):
                act.wait_ge(*k.dve_done.now())
                nc.scalar.activation(lam[:, 0:2], lam[:, 0:2], ACT.Exp).then_inc(*k.act_done.up())

            @block.vector
            def _(dve):
                link = linker(dve, k.dve_done)
                dve.wait_ge(*k.act_done.now())
                link(V.tensor_tensor(lam[:, 2:3], lam[:, 1:2], lam[:, 0:1], ALU.subtract))
                link(V.tensor_scalar(lam[:, 2:3], lam[:, 2:3], -LAM_INIT, None, ALU.add))
        ctx2.close()

        qT = sb("qT", [P, H, 2, S])
        kT = k.h[:].rearrange("p t n -> p (t n)")
        kT2 = sb("kT2", [P, 4, 512])
        kT_of = lambda h: (kT.rearrange("p (h n) -> p h n", h=4) if h < 4 else kT2[:])[:, h % 4, :]
        e = sb("e", [P, 2, 2, 512])
        pd = sb("pd", [P, 2, 512])
        pdT = sb("pdT", [P, 2, 512])
        st = sb("st", [P, 2, 2, 2])
        o = q
        sem = lambda n: Signal(k.sem("da_" + n))
        scores_ready, maxed, exps_ready, diffed, turned, turned_copied, out_ready, out_copied = map(
            sem, ("scores", "maxed", "exps", "diffed", "turned", "turned_copied", "out", "out_copied"))
        with nc.Block() as block:
            @block.vector
            def _(dve):
                V.memset(qT[:], 0.0).then_inc(*k.dve_done.up())

            @block.tensor
            def _(pe):
                for b in range(4):
                    for i in range(4):
                        h, t = 2 * b + i // 2, i % 2
                        mm = nc.tensor.transpose(k.ps[:, b, i * P:(i + 1) * P], q[:, t, h * P:(h + 1) * P], k.c("ident"))
                mm.then_inc(*k.pe_done.up())
                for b in range(4):
                    for t in range(4):
                        mm = nc.tensor.transpose(k.ps[:, 4 + b, t * P:(t + 1) * P], kx[:, t, b * P:(b + 1) * P], k.c("ident"))
                mm.then_inc(*k.pe_done.up())

            @block.vector
            def _(dve):
                dve.wait_ge(k.dve_done.sem, k.dve_done.n)
                dve.wait_ge(k.pe_done.sem, k.pe_done.n - 1)
                for b in range(4):
                    for m in range(2):
                        r = slice(64 * m, 64 * m + 64)
                        V.tensor_copy(qT[r, 2 * b:2 * b + 2, m, :],
                                      k.ps[r, b, :].rearrange("p (h n) -> p h n", h=2)).then_inc(*k.dve_done.up())
                dve.wait_ge(*k.pe_done.now())
                for b in range(4):
                    V.tensor_copy(kT_of(b), k.ps[:, 4 + b, :]).then_inc(*k.dve_done.up())

            @block.tensor
            def _(pe):
                pe.wait_ge(*k.dve_done.now())
                for b in range(4):
                    for t in range(4):
                        mm = nc.tensor.transpose(k.ps[:, b, t * P:(t + 1) * P], kx[:, t, (4 + b) * P:(5 + b) * P],
                                                 k.c("ident"))
                mm.then_inc(*k.pe_done.up())

            @block.vector
            def _(dve):
                dve.wait_ge(*k.pe_done.now())
                for b in range(4):
                    V.tensor_copy(kT_of(4 + b), k.ps[:, b, :]).then_inc(*k.dve_done.up())

        N = H * TT
        with nc.Block() as block:
            @block.tensor
            def _(pe):
                def scores(i):
                    h, t = i // 2, i % 2
                    if i >= 2:
                        pe.wait_ge(exps_ready.sem, i - 1)
                    for m in range(2):
                        mm = nc.tensor.matmul(k.ps[:, 2 * (i % 2) + m, :], qT[:, h, m, t * P:(t + 1) * P], kT_of(h),
                                              start=True, stop=True)
                    mm.then_inc(*scores_ready.up())

                def turn(i):
                    pe.wait_ge(diffed.sem, i + 1)
                    if i >= 2:
                        pe.wait_ge(turned_copied.sem, i - 1)
                    for c in range(4):
                        mm = nc.tensor.transpose(k.ps[:, 4 + i % 2, c * P:(c + 1) * P], pd[:, i % 2, c * P:(c + 1) * P],
                                                 k.c("ident"))
                    mm.then_inc(*turned.up())

                def values(i):
                    h = i // 2
                    pe.wait_ge(turned_copied.sem, i + 1)
                    if i >= 2:
                        pe.wait_ge(out_copied.sem, i - 1)
                    for c in range(4):
                        mm = nc.tensor.matmul(k.ps[:, 6 + i % 2, 0:P], pdT[:, i % 2, c * P:(c + 1) * P],
                                              v[:, c, h * P:(h + 1) * P], start=(c == 0), stop=(c == 3))
                    mm.then_inc(*out_ready.up())

                for i in range(N + 2):
                    if i < N:
                        scores(i)
                    if 1 <= i <= N:
                        turn(i - 1)
                    if i >= 2:
                        values(i - 2)

            @block.vector
            def _(dve):
                link = linker(dve, k.dve_done)

                def maxima(i):
                    dve.wait_ge(scores_ready.sem, i + 1)
                    for m in range(2):
                        link(V.tensor_reduce(st[:, i % 2, 0, m:m + 1], k.ps[:, 2 * (i % 2) + m, :], AX.X, ALU.max))
                    V.tensor_scalar(st[:, i % 2, 0, :], st[:, i % 2, 0, :], -0.125, None, ALU.mult).then_inc(*maxed.up())

                def difference(i):
                    dve.wait_ge(exps_ready.sem, i + 1)
                    if i >= 2:
                        dve.wait_ge(turned.sem, i - 1)
                    link(V.reciprocal(st[:, i % 2, 1, :], st[:, i % 2, 1, :]))
                    link(V.tensor_tensor(st[:, i % 2, 1, 1:2], st[:, i % 2, 1, 1:2], lam[:, 2:3], ALU.mult))
                    link(V.tensor_scalar(pd[:, i % 2, :], e[:, i % 2, 0, :], st[:, i % 2, 1, 0:1], None, ALU.mult))
                    V.scalar_tensor_tensor(pd[:, i % 2, :], e[:, i % 2, 1, :], st[:, i % 2, 1, 1:2], pd[:, i % 2, :],
                                           ALU.mult, ALU.add).then_inc(*diffed.up())

                def copy_out(i):
                    h, t = i // 2, i % 2
                    dve.wait_ge(out_ready.sem, i + 1)
                    V.tensor_copy(o[:, t, h * P:(h + 1) * P], k.ps[:, 6 + i % 2, 0:P]).then_inc(*out_copied.up())

                for i in range(N + 2):
                    if i < N:
                        maxima(i)
                    if 1 <= i <= N:
                        difference(i - 1)
                    if i >= 2:
                        copy_out(i - 2)

            @block.scalar
            def _(act):
                def exps(i):
                    act.wait_ge(maxed.sem, i + 1)
                    if i >= 2:
                        act.wait_ge(diffed.sem, i - 1)
                    for m in range(2):
                        nc.scalar.activation(e[:, i % 2, m, :], k.ps[:, 2 * (i % 2) + m, :], ACT.Exp,
                                             bias=st[:, i % 2, 0, m:m + 1], scale=0.125,
                                             accum_out=st[:, i % 2, 1, m:m + 1]).then_inc(
                                                 *(exps_ready.up() if m else k.act_done.up()))

                def copy_turned(i):
                    act.wait_ge(turned.sem, i + 1)
                    if i >= 2:
                        act.wait_ge(out_ready.sem, i - 1)
                    nc.scalar.copy(pdT[:, i % 2, :], k.ps[:, 4 + i % 2, :]).then_inc(*turned_copied.up())

                for i in range(N + 1):
                    if i < N:
                        exps(i)
                    if i >= 1:
                        copy_turned(i - 1)

        sq = kx[:, 0:2]
        head_norm(o[:], og[:], 128, 128)
        with nc.Block() as block:
            @block.vector
            def _(dve):
                link = linker(dve, k.dve_done)
                link(V.tensor_scalar(o[:], o[:], 1.0 - LAM_INIT, None, ALU.mult))
            transpose_tokens(k, o, oaT, k.dve_done.now(), block)


ROW_KK, ROW_KA, ROW_RK, ROW_G, ROW_B, ROW_W0, ROW_A0 = 0, 1, 2, 3, 4, 5, 7
L2_EPS = 1e-12
RW_LN_EPS = 64e-5
LANES = 4
LAG = 1
LOG_DECAY = -math.exp(-0.5)


def rwkv_branch(k, hcT, obT):
    nc, I = k.nc, k.ins
    V, G = nc.vector, nc.gpsimd
    with ExitStack() as ctx:
        sb = lambda name, shape, dt=F32: k.sb("rw_" + name, shape, dt, ctx)
        zx = sb("zx", [P, 26, S])
        zc = sb("zc", [P, 17, S])
        kk = {"c": sb("kkc", [P, DC, S]), "x": sb("kkx", [P, DC, S])}
        zl = {s: sb("zl" + s, [P, 2, S]) for s in "cx"}
        y = sb("y", [P, DC, 4, C64])
        shw = sb("shw", [P, 3, 26])
        rows = sb("rows", [P, 9, DC])
        ka1 = sb("ka1", [P, DC])
        lora = [k.gain, k.shift]
        load(k, [(shw[:], I["rw_shift_2"]), (rows[:], I["rw_rows"]), (lora[0][:], I["rw_lora"][:, 0, :]),
                 (lora[1][:], I["rw_lora"][:, 1, :])], ahead=columns(I["w_in_2"], W_Z, W_G))

        def shifted(dst, at, chunk, n):
            def run(bank, link):
                for i in range(n):
                    b, o, c = bank[:, i * S:(i + 1) * S], dst[:, at + i, :], chunk + i
                    link(V.tensor_scalar(o, b, shw[:, 1, c:c + 1], None, ALU.mult))
                    link(V.scalar_tensor_tensor(o[:, 1:S], b[:, 0:S - 1], shw[:, 0, c:c + 1], o[:, 1:S], ALU.mult, ALU.add))
                    ins = V.scalar_tensor_tensor(o[:, 0:S - 1], b[:, 1:S], shw[:, 2, c:c + 1], o[:, 0:S - 1],
                                                 ALU.mult, ALU.add)
                    if i < n - 1:
                        link(ins)
                return ins
            return run

        jobs = []
        for n, src in enumerate(columns(I["w_in_2"], W_Z, W_Z + 3328)):
            jobs.append((src, "feat", k.hT, "v", shifted(zx, 2 * n, 2 * n, 2)))
            if 4 <= n < 12:
                jobs.append((None, "feat", hcT, "v", shifted(zc, 2 * n - 8, 2 * n, 2)))
            elif n == 12:
                jobs.append((None, "feat", hcT, "v", shifted(zc, 16, 24, 1)))
        gemm(k, jobs)

        ring = k.ring[:].rearrange("p a n -> p (a n)")
        keys = {"c": zc[:, 0:8], "x": zx[:, 8:16]}
        vals = {"c": zc[:, 8:16], "x": zx[:, 16:24]}
        two = lambda n: ring[:, n * 2048:(n + 1) * 2048].rearrange("p (c n) -> p c n", c=DC)
        wide = lambda ap: ap.to_broadcast([P, DC, S])

        with nc.Block() as block:
            @block.vector
            def _(dve):
                for s in "cx":
                    V.memset(zl[s][:], 0.0).then_inc(*k.dve_done.up())
                V.tensor_scalar(ka1[:], rows[:, ROW_KA, :], -1.0, 1.0, ALU.mult, ALU.add).then_inc(*k.dve_done.up())
                dve.wait_ge(*k.dve_done.now())
                for s in "cx":
                    V.tensor_tensor(kk[s][:], keys[s], wide(rows[:, ROW_KK, :].unsqueeze(2)), ALU.mult).then_inc(
                        *k.dve_done.up())

            @block.scalar
            def _(act):
                act.wait_ge(*k.dve_done.now())
                for s, z in (("c", zc[:, 16]), ("x", zx[:, 24])):
                    nc.scalar.activation(zl[s][0:64, 0, :], z[0:64], ACT.Tanh).then_inc(*k.act_done.up())
                    nc.scalar.copy(zl[s][64:128, 1, :], z[64:128]).then_inc(*k.act_done.up())
                for i, s in enumerate("cx"):
                    nc.scalar.activation(two(i), kk[s][:], ACT.Square).then_inc(*k.act_done.up())

            @block.tensor
            def _(pe):
                pe.wait_ge(*k.act_done.now())
                for i in range(2):
                    for b in range(4):
                        mm = nc.tensor.matmul(k.ps[:, 4 * i + b, :], k.c("head_ones"),
                                              two(i)[:, 2 * b:2 * b + 2, :].rearrange("p c n -> p (c n)"),
                                              start=True, stop=True)
                mm.then_inc(*k.pe_done.up())

            @block.vector
            def _(dve):
                dve.wait_ge(*k.pe_done.now())
                for i in range(2):
                    V.tensor_scalar(two(i), k.ps[:, 4 * i:4 * i + 4, :].rearrange("p b (c n) -> p (b c) n", c=2),
                                    L2_EPS, None, ALU.add).then_inc(*k.dve_done.up())

            @block.scalar
            def _(act):
                act.wait_ge(*k.dve_done.now())
                nc.scalar.activation(ring[:, 0:4096], ring[:, 0:4096], ACT.Sqrt).then_inc(*k.act_done.up())

            @block.vector
            def _(dve):
                link = linker(dve, k.dve_done)
                dve.wait_ge(*k.act_done.now())
                link(V.reciprocal(ring[:, 0:4096], ring[:, 0:4096]))
                for i, s in enumerate("cx"):
                    link(V.tensor_tensor(kk[s][:], kk[s][:], two(i), ALU.mult))

        class Lane:
            pass
        lanes = []
        for number in range(LANES):
            n = Lane()
            n.d, n.i = number % 2, number // 2
            n.pe, n.dve, n.act, n.pool = (Signal(k.sem(f"rw{number}_{e}")) for e in ("pe", "dve", "act", "pool"))
            at = [number * NSLOT * SLOT // LANES, number * TT * D // LANES]

            def cut(*shape, where=0):
                size = int(np.prod(shape))
                src = (ring, k.h[:].rearrange("p t n -> p (t n)"))[where]
                ap = src[:, at[where]:at[where] + size]
                at[where] += size
                return ap if len(shape) == 1 else ap.rearrange("p (a n) -> p a n", a=shape[0])

            n.ep = cut(2, 4 * (C64 + 1)).rearrange("p h (c n) -> p h c n", c=4)
            n.en = cut(2, S)
            n.ak, n.ke = cut(S), cut(S)
            n.last = cut(4)
            n.ar = cut(2, P)
            n.logs = cut(2, S)
            n.lt, n.mt, n.rbt, n.rkt = (n.logs.rearrange("p a n -> p (a n)")[:, i * P:(i + 1) * P] for i in range(4))
            n.b, n.kb = cut(P, where=1), cut(P, where=1)
            n.xx = cut(2, P)
            n.p = cut(P)
            n.turned = cut(2, P)
            n.state, n.vst, n.g, n.u = (cut(C64, where=1) for _ in range(4))
            n.scaled = cut(C64)
            bank = lambda b, at, size, number=number: k.ps[:, 2 * number + b, at:at + size]
            n.with_b, n.with_k = bank(0, 0, 2 * P), bank(0, 2 * P, 2 * P)
            n.low, n.high = bank(1, 0, P), bank(1, P, 2 * P)
            n.scan = (lambda ap: ap) if n.d == 0 else (lambda ap: ap[:, ::-1])
            lanes.append(n)

        halves = [slice(0, 64), slice(64, 128)]

        split = lambda ap: ap.rearrange("p (h n) -> p h n", h=2)
        both = lambda ap: ap.unsqueeze(1).to_broadcast([P, 2, C64])

        def tokens(n, ap, c):
            r = c if n.d == 0 else 3 - c
            return n.scan(ap[:, r * C64:(r + 1) * C64])

        with nc.Block() as block:
            def start(n, first):
                @block.gpsimd
                def _(pool):
                    if first:
                        linker(pool, n.pool)(G.memset(n.ep, 0.0))
                        linker(pool, n.pool)(G.memset(n.en, 0.0))
                        for hh, r in enumerate(halves):
                            linker(pool, n.pool)(G.memset(n.ep[r, hh, :, 0:1], 1.0))
                    pool.wait_ge(*n.pe.now())
                    pool.wait_ge(*n.dve.now())
                    linker(pool, n.pool)(G.memset(n.state, 0.0))

            def prep_pe(n, s):
                @block.tensor
                def _(pe):
                    pe.wait_ge(*n.dve.now())
                    pe.wait_ge(*n.act.now())
                    for b, o in enumerate((n.with_b, n.with_k)):
                        mm = nc.tensor.matmul(o, lora[n.d][:, n.pair * P:(n.pair + 1) * P], zl[s][:, b, :],
                                              start=True, stop=True)
                    mm.then_inc(*n.pe.up())

            def prep_act(n, s):
                @block.scalar
                def _(act):
                    act.wait_ge(*n.pe.now())
                    act.wait_ge(*n.dve.now())
                    act.wait_ge(*n.pool.now())
                    for src, dst, row in ((n.with_b, n.logs[:, 0], ROW_W0 + n.d), (n.with_k, n.ak, ROW_A0 + n.d)):
                        nc.scalar.activation(n.scan(dst), src, ACT.Sigmoid,
                                             bias=rows[:, row, n.pair:n.pair + 1]).then_inc(*n.act.up())

            def prep_logs(n, s):
                @block.vector
                def _(dve):
                    link = linker(dve, n.dve)
                    dve.wait_ge(*n.act.now())
                    link(V.tensor_scalar(n.logs[:, 0], n.logs[:, 0], LOG_DECAY, None, ALU.mult))
                    V.tensor_tensor_scan(n.logs[:, 1], k.c("reset")[:, 0:S], n.logs[:, 0], 0.0, ALU.mult,
                                         ALU.add).then_inc(*n.dve.up())

            def prep_keys(n, s):
                @block.vector
                def _(dve):
                    link = linker(dve, n.dve)
                    link(V.tensor_scalar(n.ke, n.ak, rows[:, ROW_KA, n.pair:n.pair + 1],
                                         ka1[:, n.pair:n.pair + 1], ALU.mult, ALU.add))
                    V.tensor_tensor(n.ke, n.ke, n.scan(keys[s][:, n.pair, :]), ALU.mult).then_inc(*n.dve.up())

            def prep_a(n, s):
                @block.vector
                def _(dve):
                    dve.wait_ge(*n.dve.now())
                    V.tensor_tensor(n.ak, n.ak, n.scan(kk[s][:, n.pair, :]), ALU.mult).then_inc(*n.dve.up())

            def prep_exp(n, s):
                @block.scalar
                def _(act):
                    act.wait_ge(*n.dve.now())
                    logs = n.logs[:, 1].rearrange("p (c n) -> p c n", c=4)
                    for hh, r in enumerate(halves):
                        nc.scalar.activation(n.en[r, hh, :], n.logs[r, 1], ACT.Exp, scale=-1.0).then_inc(*n.act.up())
                        nc.scalar.activation(n.ep[r, hh, :, 1:C64 + 1], logs[r], ACT.Exp).then_inc(*n.act.up())
                    nc.scalar.activation(n.last, logs[:, :, C64 - 1], ACT.Exp).then_inc(*n.act.up())

            def build(n, s, c):
                here = slice(c * C64, (c + 1) * C64)
                wanted = s == "x"
                @block.vector
                def _(dve):
                    dve.wait_ge(*n.act.now())
                    dve.wait_ge(*n.pe.now())
                    dve.wait_ge(*n.pool.now())
                    V.tensor_tensor(split(n.ar[:, 0]), both(tokens(n, kk[s][:, n.pair, :], c)), n.ep[:, :, c, 0:C64],
                                    ALU.mult).then_inc(*n.dve.up())
                    V.tensor_tensor(split(n.b), both(n.ak[:, here]), n.en[:, :, here], ALU.mult).then_inc(*n.dve.up())
                    if wanted:
                        rc = c if n.d == 0 else 3 - c
                        ep = n.ep[:, :, c, 1:C64 + 1]
                        V.tensor_tensor(split(n.ar[:, 1]), both(zx[:, n.pair, rc * C64:(rc + 1) * C64]),
                                        ep if n.d == 0 else ep[:, :, ::-1], ALU.mult).then_inc(*n.dve.up())

                @block.gpsimd
                def _(pool):
                    pool.wait_ge(*n.act.now())
                    pool.wait_ge(*n.pe.now())
                    linker(pool, n.pool)(G.tensor_tensor(split(n.kb), both(n.ke[:, here]), n.en[:, :, here], ALU.mult))

                @block.scalar
                def _(act):
                    act.wait_ge(*n.pe.now())
                    nc.scalar.copy(split(n.p), both(tokens(n, vals[s][:, n.pair, :], c))).then_inc(*n.act.up())

            def products(n, s, c):
                wanted = s == "x"
                @block.tensor
                def _(pe):
                    pe.wait_ge(*n.dve.now())
                    pe.wait_ge(*n.pool.now())
                    pe.wait_ge(*n.act.now())
                    w = 2 * P if wanted else P
                    for o, t in ((n.with_b, n.b), (n.with_k, n.kb)):
                        nc.tensor.matmul(o[:, 0:w], t, n.ar.rearrange("p a n -> p (a n)")[:, 0:w],
                                         start=True, stop=True)
                    nc.tensor.transpose(n.low, n.p, k.c("ident"))
                    for j, t in enumerate((n.b, n.kb)):
                        mm = nc.tensor.transpose(n.high[:, j * P:(j + 1) * P], t, k.c("ident"))
                    mm.then_inc(*n.pe.up())

            def masks(n, s, c):
                @block.vector
                def _(dve):
                    dve.wait_ge(*n.pe.now())
                    V.tensor_tensor(n.p, n.with_b[:, 0:P], k.c("level0"), ALU.mult).then_inc(*n.dve.up())
                    p_ready = n.dve.now()
                    V.tensor_tensor(n.lt, n.with_b[:, 0:P], k.c("strict"), ALU.mult).then_inc(*n.dve.up())
                    dve.wait_ge(*p_ready)
                    V.tensor_tensor(n.xx[:, 1], k.c("ident"), n.p, ALU.subtract).then_inc(*n.dve.up())

                @block.scalar
                def _(act):
                    act.wait_ge(*n.pe.now())
                    for hh, r in enumerate(halves):
                        nc.scalar.copy(n.vst[r], n.low[r, 64 * hh:64 * hh + 64]).then_inc(*n.act.up())
                    nc.scalar.copy(n.turned.rearrange("p a n -> p (a n)"), n.high).then_inc(*n.act.up())

            def turn_x(n, s, level):
                @block.tensor
                def _(pe):
                    pe.wait_ge(*n.dve.now())
                    pe.wait_ge(*n.act.now())
                    nc.tensor.transpose(n.low, n.xx[:, 1], k.c("ident")).then_inc(*n.pe.up())

            def copy_x(n, s, level):
                @block.scalar
                def _(act):
                    act.wait_ge(*n.pe.now())
                    nc.scalar.copy(n.xx[:, 0], n.low).then_inc(*n.act.up())

            def off_x(n, s, level):
                @block.tensor
                def _(pe):
                    pe.wait_ge(*n.act.now())
                    pe.wait_ge(*n.dve.now())
                    nc.tensor.matmul(n.low, n.lt, n.xx[:, 0], start=True, stop=True).then_inc(*n.pe.up())

                incl = k.c("incl" if n.d == 0 else "incl_rev")
                more = [(n.mt, n.with_k[:, 0:P], k.c("strict"))]
                if s == "x":
                    more += [(n.rbt, n.with_b[:, P:2 * P], incl), (n.rkt, n.with_k[:, P:2 * P], incl)]
                if level <= len(more):
                    @block.vector
                    def _(dve):
                        V.tensor_tensor(*more[level - 1], ALU.mult).then_inc(*n.dve.up())

            def keep_off_x(n, s, level):
                @block.vector
                def _(dve):
                    dve.wait_ge(*n.pe.now())
                    V.tensor_tensor(n.p, n.low, k.c(f"level{level}"), ALU.mult).then_inc(*n.dve.up())

            def x_off_x(n, s, level):
                @block.tensor
                def _(pe):
                    pe.wait_ge(*n.dve.now())
                    nc.tensor.matmul(n.high[:, 0:P], n.p, n.xx[:, 1], start=True, stop=True).then_inc(*n.pe.up())

            def next_x(n, s, level):
                @block.vector
                def _(dve):
                    dve.wait_ge(*n.pe.now())
                    V.tensor_tensor(n.xx[:, 1], n.xx[:, 1], n.high[:, 0:P], ALU.subtract).then_inc(*n.dve.up())

            def right_side(n, s, c):
                @block.tensor
                def _(pe):
                    pe.wait_ge(*n.dve.now())
                    pe.wait_ge(*n.pool.now())
                    pe.wait_ge(*n.act.now())
                    o = n.low[:, 0:C64]
                    nc.tensor.matmul(o, n.ar[:, 0, :], n.state, start=True, stop=False)
                    nc.tensor.matmul(o, n.mt, n.vst, start=False, stop=True).then_inc(*n.pe.up())

                @block.gpsimd
                def _(pool):
                    pool.wait_ge(*n.dve.now())
                    pool.wait_ge(*n.act.now())
                    linker(pool, n.pool)(G.tensor_scalar(n.scaled, n.state, n.last[:, c:c + 1], None, ALU.mult))

            def keep_right(n, s, c):
                @block.scalar
                def _(act):
                    act.wait_ge(*n.pe.now())
                    nc.scalar.mul(n.g, n.low[:, 0:C64], -1.0).then_inc(*n.act.up())

            def solve(n, s, c):
                @block.tensor
                def _(pe):
                    pe.wait_ge(*n.act.now())
                    nc.tensor.matmul(n.high[:, 0:C64], n.xx[:, 1], n.g, start=True, stop=True).then_inc(
                        *n.pe.up())

            def keep_u(n, s, c):
                @block.scalar
                def _(act):
                    act.wait_ge(*n.pe.now())
                    nc.scalar.copy(n.u, n.high[:, 0:C64]).then_inc(*n.act.up())

            def results(n, s, c):
                wanted = s == "x"
                @block.tensor
                def _(pe):
                    pe.wait_ge(*n.act.now())
                    o = n.with_b[:, 0:C64]
                    nc.tensor.matmul(o, n.turned[:, 0], n.u, start=True, stop=False)
                    nc.tensor.matmul(o, n.turned[:, 1], n.vst, start=False, stop=True).then_inc(*n.pe.up())
                    if wanted:
                        o = n.low[:, 0:C64]
                        nc.tensor.matmul(o, n.ar[:, 1, :], n.state, start=True, stop=False)
                        nc.tensor.matmul(o, n.rbt, n.u, start=False, stop=False)
                        nc.tensor.matmul(o, n.rkt, n.vst, start=False, stop=True).then_inc(*n.pe.up())

            def keep_results(n, s, c):
                wanted = s == "x"
                @block.vector
                def _(dve):
                    dve.wait_ge(*n.pe.now())
                    dve.wait_ge(*n.pool.now())
                    if wanted and c == 2:
                        dve.wait_ge(*lanes[2 * n.i + 1 - n.d].dve.now())
                    V.scalar_tensor_tensor(n.state, n.with_b[:, 0:C64], n.last[:, c:c + 1], n.scaled, ALU.mult,
                                           ALU.add).then_inc(*n.dve.up())
                    if wanted:
                        o = y[:, n.pair, c if n.d == 0 else 3 - c, :]
                        b = n.low[:, 0:C64]
                        if c < 2:
                            V.tensor_copy(o, b).then_inc(*n.dve.up())
                        else:
                            V.tensor_tensor(o, o, b, ALU.add).then_inc(*n.dve.up())

            prepare = [prep_pe, prep_act, prep_logs, prep_keys, prep_a, prep_exp]
            open_chunk = [build, products, masks]
            double_x = [turn_x, copy_x, off_x, keep_off_x, x_off_x, next_x]
            close_chunk = [right_side, keep_right, solve, keep_u, results, keep_results]
            steps = []
            for q in range(DC // 2):
                steps.append((start, (q == 0,), q))
                for s in "cx":
                    steps += [(step, (s,), q) for step in prepare]
                    for c in range(4):
                        steps += [(step, (s, c), q) for step in open_chunk]
                        for level in range(1, 6):
                            steps += [(step, (s, level), q) for step in double_x]
                        steps += [(step, (s, c), q) for step in close_chunk]

            for tick in range(len(steps) + LAG * (LANES - 1)):
                for number, n in enumerate(lanes):
                    i = tick - number * LAG
                    if 0 <= i < len(steps):
                        step, args, q = steps[i]
                        n.pair = 2 * q + n.i
                        step(n, *args)

        rwkv_post(k, ctx, zx, y, rows, ring, obT)


def rwkv_post(k, ctx, zx, y, rows, ring, obT):
    nc, I = k.nc, k.ins
    V = nc.vector
    st = k.sb("rw_st", [P, 2, 32], ctx=ctx)
    y32 = y[:].rearrange("p a c n -> p (a c) n")
    wide = lambda ap: ap.to_broadcast([P, 32, C64])
    sq = ring[:, 0:2048].rearrange("p (g n) -> p g n", g=32)
    ybd = ring[:, 2048:2048 + 4096].rearrange("p (g n) -> p g n", g=32)
    bon = ring[:, 6144:8192].rearrange("p (c n) -> p c n", c=DC)
    g_up = ring[:, 8192:9216]
    sg = ring[:, 9216:9472]
    gate = ring[:, 10240:12288].rearrange("p (c n) -> p c n", c=DC)
    load(k, [(g_up, I["rw_g_up_2"])])
    with nc.Block() as block:
        @block.vector
        def _(dve):
            link = linker(dve, k.dve_done)
            link(V.tensor_reduce(st[:, 0, :], y32, AX.X, ALU.add))
            link(V.tensor_scalar(st[:, 0, :], st[:, 0, :], 1.0 / C64, None, ALU.mult))
            link(V.tensor_tensor(y32, y32, wide(st[:, 0, :].unsqueeze(2)), ALU.subtract))

        @block.scalar
        def _(act):
            nc.scalar.activation(sg, zx[:, 25, :], ACT.Sigmoid).then_inc(*k.act_done.up())
            act.wait_ge(*k.dve_done.now())
            nc.scalar.activation(sq, y32, ACT.Square).then_inc(*k.act_done.up())

        @block.tensor
        def _(pe):
            pe.wait_ge(*k.act_done.now())
            for c in range(DC):
                mm = nc.tensor.matmul(k.ps[:, c // 2, c % 2 * S:c % 2 * S + S], g_up[:, c * P:(c + 1) * P], sg,
                                      start=True, stop=True)
            mm.then_inc(*k.pe_done.up())

        @block.vector
        def _(dve):
            link = linker(dve, k.dve_done)
            dve.wait_ge(*k.act_done.now())
            link(V.tensor_reduce(st[:, 1, :], sq, AX.X, ALU.add))
            link(V.tensor_scalar(st[:, 1, :], st[:, 1, :], 1.0 / C64, RW_LN_EPS, ALU.mult, ALU.add))
            link(V.memset(ybd, 0.0))
            for c in range(DC):
                link(V.scalar_tensor_tensor(bon[:, c, :], zx[:, c, :], rows[:, ROW_RK, c:c + 1], zx[:, 8 + c, :],
                                            ALU.mult, ALU.mult))
            dve.wait_ge(*k.pe_done.now())
            link(V.tensor_copy(gate, k.ps[:, 0:4, :].rearrange("p b (c n) -> p (b c) n", c=2)))

        @block.scalar
        def _(act):
            act.wait_ge(*k.dve_done.now())
            nc.scalar.activation(st[:, 1, :], st[:, 1, :], ACT.Sqrt).then_inc(*k.act_done.up())

        @block.tensor
        def _(pe):
            pe.wait_ge(*k.dve_done.now())
            for b in range(4):
                mm = nc.tensor.matmul(k.ps[:, 4 + b, :], k.c("head_ones"),
                                      bon[:, 2 * b:2 * b + 2, :].rearrange("p c n -> p (c n)"), start=True, stop=True)
            mm.then_inc(*k.pe_done.up())

        @block.vector
        def _(dve):
            link = linker(dve, k.dve_done)
            dve.wait_ge(*k.act_done.now())
            link(V.reciprocal(st[:, 1, :], st[:, 1, :]))
            for hh in range(2):
                r = slice(64 * hh, 64 * hh + 64)
                link(V.tensor_tensor(ybd[r, :, 64 * hh:64 * hh + 64], y32[r],
                                     st[r, 1, :].unsqueeze(2).to_broadcast([64, 32, C64]), ALU.mult))

        @block.tensor
        def _(pe):
            pe.wait_ge(*k.dve_done.now())
            for c in range(DC):
                for n in range(4):
                    mm = nc.tensor.matmul(k.ps[:, c // 2, c % 2 * S + n * C64:c % 2 * S + (n + 1) * C64],
                                          ybd[:, 4 * c + n, :], k.c("fold"), start=True, stop=True)
            mm.then_inc(*k.pe_done.up())

        @block.vector
        def _(dve):
            link = linker(dve, k.dve_done)
            dve.wait_ge(*k.pe_done.now())
            link(V.tensor_tensor(bon, k.ps[:, 4:8, :].rearrange("p b (c n) -> p (b c) n", c=2), zx[:, 16:24, :], ALU.mult))
            for c in range(DC):
                link(V.tensor_scalar(obT[:, c, :], k.ps[:, c // 2, c % 2 * S:c % 2 * S + S], rows[:, ROW_G, c:c + 1],
                                     rows[:, ROW_B, c:c + 1], ALU.mult, ALU.add))
            link(V.tensor_tensor(obT[:], obT[:], bon, ALU.add))
            link(V.tensor_tensor(obT[:], obT[:], gate, ALU.mult))


PH = 8
TOPK = 16
SLOTS = PH * TOPK
NBUF = 8


def peer(k):
    nc, I = k.nc, k.ins
    V = nc.vector
    with ExitStack() as ctx:
        sb = lambda name, shape, dt=F32: k.sb("pr_" + name, shape, dt, ctx)
        qT = sb("qT", [P, 2 * PH, S])
        keysT = sb("keysT", [P, 2 * PH, P])
        idxT = sb("idxT", [P, S], U32)
        gateT = sb("gateT", [P, S])
        load(k, [(keysT[:], I["peer_keysT"])])
        gemm(k, [(src, "feat", k.hT, "v" if n % 2 else "s", copy_feat(k, qT, 2 * n, "v" if n % 2 else "s"))
                 for n, src in enumerate(columns(I["peer_wq_2"], 0, 2 * D))])
        gathers(k, ctx, Picks(k, ctx, qT, keysT, idxT, gateT), idxT, gateT)


class Picks:

    def __init__(self, k, ctx, qT, keysT, idxT, gateT):
        sb = lambda name, shape, dt=F32: k.sb("pk_" + name, shape, dt, ctx)
        self.k, self.qT, self.keysT, self.idxT, self.gateT = k, qT, keysT, idxT, gateT
        self.sc = sb("sc", [P, 2 * PH, P])
        self.sv = sb("sv", [P, PH, 2, TOPK])
        self.si = sb("si", [P, PH, 2, TOPK], U32)
        self.sif = sb("sif", [P, PH, 2, TOPK])
        self.cand = sb("cand", [P, PH, TOPK * TOPK])
        self.ts = sb("ts", [P, PH, TOPK])
        self.tp = sb("tp", [P, PH, TOPK], U32)
        self.ij = sb("ij", [P, PH * TOPK], U32)
        self.ijf = sb("ijf", [P, PH * TOPK])
        self.big = self.sc[:].rearrange("p h (a n) -> p (h a) n", n=TOPK)
        self.part = sb("part", [P, 2, PH * TOPK])
        self.den = sb("den", [P, PH])

    def choose(self, block, t):
        k = self.k
        nc, V = k.nc, k.nc.vector
        sc, sv, si, sif, cand, ts, tp, ij, ijf, part = (
            self.sc, self.sv, self.si, self.sif, self.cand, self.ts, self.tp, self.ij, self.ijf, self.part)

        def top16(link, values, indices, data):
            link(V.max(values[:, 0:8], data))
            link(V.max_index(indices[:, 0:8], values[:, 0:8], data))
            link(V.match_replace(data, values[:, 0:8], data, NEG))
            link(V.max(values[:, 8:16], data))
            link(V.max_index(indices[:, 8:16], values[:, 8:16], data))

        big = self.big

        @block.tensor
        def _(pe):
            for hp in range(2 * PH):
                mm = nc.tensor.matmul(k.ps[:, 4 + hp // 4, hp % 4 * P:(hp % 4 + 1) * P], self.qT[:, hp, t * P:(t + 1) * P],
                                      self.keysT[:, hp, :], start=True, stop=True)
            mm.then_inc(*k.pe_done.up())

        @block.vector
        def _(dve):
            link = linker(dve, k.dve_done)
            dve.wait_ge(*k.pe_done.now())
            link(V.tensor_copy(sc[:], k.ps[:, 4:8, :].rearrange("p b (h n) -> p (b h) n", h=4)))
            for hp in range(2 * PH):
                top16(link, sv[:, hp // 2, hp % 2, :], si[:, hp // 2, hp % 2, :], sc[:, hp, :])
            link(V.tensor_copy(sif[:], si[:]))
            link(V.tensor_tensor(cand[:].rearrange("p h (i j) -> p h i j", i=TOPK),
                                 sv[:, :, 0, :].unsqueeze(3).to_broadcast([P, PH, TOPK, TOPK]),
                                 sv[:, :, 1, :].unsqueeze(2).to_broadcast([P, PH, TOPK, TOPK]), ALU.add))
            for h in range(PH):
                top16(link, ts[:, h, :], tp[:, h, :], cand[:, h, :])
            tpf = tp[:].rearrange("p h n -> p (h n)")
            iota = k.c("iota")[:, 0:TOPK].unsqueeze(1).to_broadcast([P, PH * TOPK, TOPK])
            for side in range(2):
                link(V.tensor_scalar(ij[:], tpf, 4, None, ALU.logical_shift_right) if side == 0 else
                     V.tensor_scalar(ij[:], tpf, TOPK - 1, None, ALU.bitwise_and))
                link(V.tensor_copy(ijf[:], ij[:]))
                link(V.tensor_tensor(big, iota, ijf[:].unsqueeze(2).to_broadcast([P, PH * TOPK, TOPK]),
                                     ALU.is_equal))
                b4 = big.rearrange("p (h s) n -> p h s n", h=PH)
                link(V.tensor_tensor(b4, b4, sif[:, :, side, :].unsqueeze(2).to_broadcast([P, PH, TOPK, TOPK]),
                                     ALU.mult))
                link(V.tensor_reduce(part[:, side, :], big, AX.X, ALU.add))
            link(V.scalar_tensor_tensor(part[:, 0, :], part[:, 0, :], float(P), part[:, 1, :], ALU.mult, ALU.add))
            link(V.tensor_tensor(cand[:, :, 0:TOPK], ts[:], ts[:, :, 0:1].to_broadcast([P, PH, TOPK]),
                                 ALU.subtract))

    def weigh(self, block, t):
        k = self.k
        nc, V = k.nc, k.nc.vector
        cand, ts, part, den = self.cand, self.ts, self.part, self.den

        @block.scalar
        def _(act):
            act.wait_ge(*k.dve_done.now())
            nc.scalar.activation(ts[:], cand[:, :, 0:TOPK], ACT.Exp).then_inc(*k.act_done.up())

        @block.vector
        def _(dve):
            link = linker(dve, k.dve_done)
            dve.wait_ge(*k.act_done.now())
            link(V.tensor_reduce(den[:], ts[:], AX.X, ALU.add))
            link(V.reciprocal(den[:], den[:]))
            link(V.tensor_tensor(ts[:], ts[:], den[:].unsqueeze(2).to_broadcast([P, PH, TOPK]), ALU.mult))

        @block.tensor
        def _(pe):
            pe.wait_ge(*k.dve_done.now())
            nc.tensor.transpose(k.ps[:, 4, 0:P], part[:, 0, :], k.c("ident"))
            nc.tensor.transpose(k.ps[:, 4, P:2 * P], ts[:].rearrange("p h n -> p (h n)"), k.c("ident")).then_inc(
                *k.pe_done.up())

        @block.vector
        def _(dve):
            dve.wait_ge(*k.pe_done.now())
            V.tensor_copy(self.idxT[:, t * P:(t + 1) * P], k.ps[:, 4, 0:P]).then_inc(*k.dve_done.up())
            V.tensor_copy(self.gateT[:, t * P:(t + 1) * P], k.ps[:, 4, P:2 * P]).then_inc(*k.dve_done.up())


def gathers(k, ctx, picks, idxT, gateT):
    nc, I = k.nc, k.ins
    V = nc.vector
    sb = lambda name, shape, dt=F32: k.sb("ga_" + name, shape, dt, ctx)
    rows = k.ring[:].rearrange("p a n -> p (a n)")[:, 0:NBUF * D].rearrange("p (j n) -> p j n", j=NBUF)
    junk = k.ring[:].rearrange("p a n -> p (a n)")[:, NBUF * D:NBUF * D + D]
    rest = k.ring[:].rearrange("p a n -> p (a n)")[:, NBUF * D + D:NBUF * D + 3 * D].rearrange("p (t n) -> p t n", t=TT)
    num = sb("num", [P, NBUF], U32)
    h_parts = sb("h_parts", [P, 3, TT, D], BF16)
    sel = sb("sel", [P, 4, P], BF16)
    dots = sb("dots", [P, S])
    dot8 = sb("dot8", [P, NBUF])
    window = sb("window", [P, 2 * P - 1])
    zero = sb("zero", [P, P])
    wcol = sb("wcol", [P, 4, P])
    acc = sb("acc", [P, TT, D])
    sem = lambda n: Signal(k.sem("ga_" + n))
    landed = [sem(f"landed{j}") for j in range(NBUF)]
    num_ready, sel_ready, bcast_ready, dot_done, dots_kept, wcol_ready, v_used = map(
        sem, ("num_ready", "sel_ready", "bcast_ready", "dot_done", "dots_kept", "wcol_ready", "v_used"))
    TURNS = P // NBUF
    CREDIT = NBUF

    def gather(pool, j, table, turn, base, freed, freed_base):
        pool.sem_clear(num_ready.sem)
        pool.wait_ge(freed.sem, turn * NBUF + (freed_base + j + 1))
        nc.gpsimd.tensor_copy(num[:, j:j + 1], idxT[:, bass.ds(turn * NBUF + (base + j), 1)]).then_inc(num_ready.sem, 1)
        pool.wait_ge(num_ready.sem, 1)
        nc.gpsimd.indirect_dma_start(rows[:, j, :], None, table, bass.IndirectOffsetOnAxis(ap=num[:, j:j + 1], axis=0)
                                     ).then_inc(landed[j].sem, 16)

    def dot_products(t):
        with nc.Block() as block:
            @block.gpsimd
            def _(pool):
                with pool.Fori(0, TURNS) as i:
                    for j in range(NBUF):
                        gather(pool, j, I["peer_u_2"], i, t * P, dot_done, dot_done.n - NBUF)

            @block.scalar
            def _(act):
                with act.Fori(0, TURNS) as i:
                    for j in range(NBUF):
                        act.wait_ge(bcast_ready.sem, i * NBUF + (bcast_ready.n + j - 3))
                        nc.scalar.copy(sel[:, j % 4, :], k.c("ident")[:, bass.ds(i * NBUF + j, 1)].to_broadcast([P, P])
                                       ).then_inc(sel_ready.sem, 1)

            @block.tensor
            def _(pe):
                with pe.Fori(0, TURNS) as i:
                    for j in range(NBUF):
                        pe.wait_ge(sel_ready.sem, i * NBUF + (sel_ready.n + j + 1))
                        pe.wait_ge(dot_done.sem, i * NBUF + (dot_done.n + j - 3))
                        for half in range(2):
                            for part in range(3):
                                mm = nc.tensor.matmul(k.ps[:, 2 * (j % 4) + half, :], sel[:, j % 4, :],
                                                      h_parts[:, part, t, half * 512:(half + 1) * 512],
                                                      start=(part == 0), stop=(part == 2))
                        mm.then_inc(bcast_ready.sem, 1)

            @block.vector
            def _(dve):
                with dve.Fori(0, TURNS) as i:
                    for j in range(NBUF):
                        dve.wait_ge(bcast_ready.sem, i * NBUF + (bcast_ready.n + j + 1))
                        dve.wait_ge(landed[j].sem, i * 16 + (landed[j].n + 16))
                        V.scalar_tensor_tensor(junk, rows[:, j, :], 1.0,
                                               k.ps[:, 2 * (j % 4):2 * (j % 4) + 2, :].rearrange("p b n -> p (b n)"),
                                               ALU.mult, ALU.mult, accum_out=dot8[:, j:j + 1]).then_inc(dot_done.sem, 1)
                        dve.wait_ge(dot_done.sem, i * NBUF + (dot_done.n + j + 1))
                    V.tensor_copy(dots[:, bass.ds(i * NBUF + t * P, NBUF)], dot8[:]).then_inc(dots_kept.sem, 1)
                    dve.wait_ge(dots_kept.sem, i + (dots_kept.n + 1))
        for s in [sel_ready, bcast_ready, dot_done]:
            s.n += P
        dots_kept.n += TURNS
        for s in landed:
            s.n += 16 * TURNS

    def sums(t):
        mine = slice(t * P, (t + 1) * P)
        with nc.Block() as block:
            @block.scalar
            def _(act):
                nc.scalar.activation(dots[:, mine], dots[:, mine], ACT.Gelu_apprx_tanh).then_inc(*k.act_done.up())

            @block.vector
            def _(dve):
                dve.wait_ge(*k.act_done.now())
                V.tensor_tensor(dots[:, mine], dots[:, mine], gateT[:, mine], ALU.mult).then_inc(*k.dve_done.up())

            weights_ready = k.dve_done.now()

            @block.tensor
            def _(pe):
                for b in range(2):
                    mm = nc.tensor.matmul(k.ps[:, b, :], zero[:], rows[:, 0, 0:512], start=True, stop=False)
                mm.then_inc(v_used.sem, CREDIT)
                v_used.n += CREDIT

            @block.gpsimd
            def _(pool):
                with pool.Fori(0, TURNS) as i:
                    for j in range(NBUF):
                        gather(pool, j, I["peer_v_2"], i, t * P, v_used, v_used.n - NBUF)

            if t + 1 < TT:
                picks.choose(block, t + 1)

            @block.scalar
            def _(act):
                act.wait_ge(*weights_ready)
                with act.Fori(0, TURNS) as i:
                    for j in range(NBUF):
                        act.wait_ge(v_used.sem, i * NBUF + (v_used.n + j - 3))
                        nc.scalar.activation(wcol[:, j % 4, :], window[:, bass.ds(i * -NBUF + (P - 1 - j), P)], ACT.Copy,
                                             scale=dots[:, bass.ds(i * NBUF + (t * P + j), 1)]).then_inc(
                                                 wcol_ready.sem, 1)

            @block.tensor
            def _(pe):
                with pe.Fori(0, TURNS) as i:
                    for j in range(NBUF):
                        pe.wait_ge(wcol_ready.sem, i * NBUF + (wcol_ready.n + j + 1))
                        pe.wait_ge(landed[j].sem, i * 16 + (landed[j].n + 16))
                        for half in range(2):
                            mm = nc.tensor.matmul(k.ps[:, half, :], wcol[:, j % 4, :],
                                                  rows[:, j, half * 512:(half + 1) * 512], start=False, stop=False)
                        mm.then_inc(v_used.sem, 1)
                for b in range(2):
                    mm = nc.tensor.matmul(k.ps[:, b, :], zero[:], rows[:, 0, 0:512], start=False, stop=True)
                mm.then_inc(*k.pe_done.up())

            @block.vector
            def _(dve):
                dve.wait_ge(*k.pe_done.now())
                V.tensor_copy(acc[:, t, :], k.ps[:, 0:2, :].rearrange("p b n -> p (b n)")).then_inc(*k.dve_done.up())
            if t + 1 < TT:
                picks.weigh(block, t + 1)
        for s in [v_used, wcol_ready]:
            s.n += P
        for s in landed:
            s.n += 16 * TURNS

    with nc.Block() as block:
        @block.vector
        def _(dve):
            V.memset(window[:], 0.0).then_inc(*k.dve_done.up())
            V.memset(zero[:], 0.0).then_inc(*k.dve_done.up())
            dve.wait_ge(*k.dve_done.now())
            V.memset(window[:, P - 1:P], 1.0).then_inc(dot_done.sem, CREDIT)
            dot_done.n += CREDIT

        @block.gpsimd
        def _(pool):
            link = linker(pool, k.pool_done)
            link(nc.gpsimd.tensor_copy(h_parts[:, 0], k.h[:]))
            link(nc.gpsimd.tensor_tensor(rest, k.h[:], h_parts[:, 0], ALU.subtract))
            link(nc.gpsimd.tensor_copy(h_parts[:, 1], rest))
            link(nc.gpsimd.tensor_tensor(rest, rest, h_parts[:, 1], ALU.subtract))
            link(nc.gpsimd.tensor_copy(h_parts[:, 2], rest))

        @block.tensor
        def _(pe):
            pe.wait_ge(*dot_done.now())
            nc.tensor.matmul(k.ps[:, 0, 0:P], zero[:], zero[:], start=True, stop=True).then_inc(bcast_ready.sem, CREDIT)
            bcast_ready.n += CREDIT

        picks.choose(block, 0)
        picks.weigh(block, 0)

    for t in range(TT):
        dot_products(t)
        sums(t)
    add_gated(k, acc, k.gate[:])


def modulation(k, c, w, b, norm, then=()):
    with ExitStack() as ctx:
        adaln_rows(k, [k.ins[c]], k.ins[w], k.ins[b], k.ins[norm],
                   [(0, [("shift", k.shift)]), (1, [("gain", k.gain)]), (2, [("gate", k.gate)])], ctx, w, then)


def program(nc, ins, out):
    with ExitStack() as ctx:
        k = Core(nc, ins, ctx)
        load(k, [(k.const[:], ins["const_table"]), (k.x[:], ins["x"].rearrange("(t p) d -> p t d", p=P))])

        def normed(src=None):
            with ExitStack() as c2:
                sq = k.sb(f"sq{k.dve_done.n}", [P, TT, D], ctx=c2)
                norm_modulate(k, k.x, k.gain[:], k.shift[:], k.h, k.hT, sq)

        def even_a():
            modulation(k, "c", "e_mod_mix_w", "e_mod_mix_b", "e_norm_mix", columns(k.ins["e_w_in"], 0, 1536))
            normed()
            even_mixer(k)

        def even_b():
            modulation(k, "c", "e_mod_ffn_w", "e_mod_ffn_b", "e_norm_ffn")
            normed()
            even_ffn(k)

        def odd_a():
            modulation(k, "c", "o_mod_mix_w", "o_mod_mix_b", "o_norm_mix", columns(k.ins["o_w_in"], 0, D))
            normed()
            s5_mixer(k)

        def odd_b():
            modulation(k, "c", "o_mod_ffn_w", "o_mod_ffn_b", "o_norm_ffn")
            normed()
            moe(k)
            final_norm(k)

        def second_a():
            hybrid_mixer(k)

        def second_b():
            with ExitStack() as ctx:
                adaln_rows(k, [k.ins["c_2"]], k.ins["w_mod_2"], k.ins["b_mod_2"], k.ins["norm2_g_2"],
                           [(3, [("shift", k.shift)]), (4, [("gain", k.gain)]), (5, [("gate", k.gate)])], ctx, "mod2b",
                           then=columns(k.ins["peer_wq_2"], 0, 2 * D))
            normed()
            peer(k)

        stages = [even_a, even_b, odd_a, odd_b, second_a, second_b]
        for stage in stages:
            stage()
        with nc.Block() as block:
            @block.sync
            def _(sp):
                sp.dma_start(out.rearrange("(t p) d -> p t d", p=P), k.x[:]).then_inc(*k.loaded.up(16))
                sp.wait_ge(*k.loaded.now())


def _laid_out(i):
    d = {}
    for name in ("e_norm_mix e_mod_mix_w e_mod_mix_b e_w_in e_fox_fb e_gla_w2 e_gla_norm e_w_o e_norm_ffn e_mod_ffn_w "
                 "e_mod_ffn_b o_norm_mix o_mod_mix_w o_mod_mix_b o_w_in o_w_glu o_w_o o_norm_ffn o_mod_ffn_w "
                 "o_mod_ffn_b o_router o_exp_gate o_exp_up o_exp_down x w_mod_2 b_mod_2 norm1_g_2 w_in_2 q_norm_g_2 "
                 "k_norm_g_2 diff_lambda_2 diff_out_g_2 rw_g_up_2 w_branch_a_2 w_branch_b_2 w_out_2 norm2_g_2 "
                 "peer_wq_2 peer_u_2 peer_v_2 ctx_2").split():
        d[name] = i[name][0]
    for name in "e_ffn_gate e_ffn_up e_ffn_down final_norm".split():
        d[name] = i[name]

    def features(a):
        return a.reshape(-1, P).T

    def states(a):
        return a.reshape(32, P, -1).transpose(1, 0, 2)

    for name in ("c", "c_2", "c_ctx_2", "e_gla_b2"):
        d[name] = features(i[name])
    d["w_small"] = np.concatenate([i["e_w_in"][0][:, 1536:1544], i["e_w_in"][0][:, 3080:3096]], 1)
    log_dt = np.repeat(i["o_log_dt"][0][:, None], 64, 1)
    d["s5_par"] = np.stack([states(a)[:, :, 0] for a in (i["o_lam_re"][0], i["o_lam_im"][0], log_dt)], 1)
    d["s5_b"] = np.stack([states(i["o_b_re"][0]), states(i["o_b_im"][0])], 1)
    d["s5_c"] = np.stack([states(i[n][0].transpose(0, 2, 1)) for n in ("o_c_re", "o_c_im")], 1)
    d["s5_dskip"] = features(i["o_d_skip"])
    d["rw_shift_2"] = i["rw_shift_2"][0].reshape(3, 26, P).transpose(2, 0, 1)
    d["rw_rows"] = np.stack([features(a) for a in (
        i["rw_k_k_2"], i["rw_k_a_2"], i["rw_r_k_2"], i["rw_ln_g_2"], i["rw_ln_b_2"], i["rw_w0_2"][0, 0],
        i["rw_w0_2"][0, 1], i["rw_a0_2"][0, 0], i["rw_a0_2"][0, 1])], 1)
    d["rw_lora"] = np.concatenate([i["rw_w_up_2"][0].transpose(1, 0, 2), i["rw_a_up_2"][0].transpose(1, 0, 2)], 0)
    d["peer_keysT"] = i["peer_keys_2"][0].transpose(3, 0, 1, 2).reshape(P, 2 * PH, P)
    d["const_table"] = np.concatenate(list(constant_table().values()), 1)
    return {n: np.ascontiguousarray(a) for n, a in d.items()}


def kernel(**inputs):
    import concourse.bacc as _bacc
    from concourse.bass_utils import run_bass_kernel_spmd as _run

    nc = _bacc.Bacc("TRN2", target_bir_lowering=False, num_devices=1)
    laid = _laid_out({n: np.asarray(a) for n, a in inputs.items()})
    ins = {n: nc.dram_tensor(f"in_{n}", list(a.shape), mybir.dt.from_np(a.dtype), kind="ExternalInput").ap()
           for n, a in laid.items()}
    out = nc.dram_tensor("out_x", [S, D], F32, kind="ExternalOutput").ap()
    program(nc, ins, out)
    r = _run(nc, [{f"in_{n}": a for n, a in laid.items()}], core_ids=[0])
    return r.results[0]["out_x"].reshape(1, S, D)
```
